# Optimizing a Trainium2 kernel written in Bass

```python
import math
import jax, jax.numpy as jnp
from jax import lax
import numpy as np

D_MODEL = 1024
BATCH = 1
SEQ = 256
DEPTH = 2
DEC_BATCH = 1
DEC_SEQ = 1024
PAST_LEN = 256

GRID_W = 64
N_ATTN_LAYERS = (DEPTH + 1) // 2
N_REC_LAYERS = DEPTH // 2
HY_WIDTH = D_MODEL // 2
HEAD_DIM = 64
ATTN_HEADS = (D_MODEL // 2) // HEAD_DIM
KV_HEADS = ATTN_HEADS // 4
KV_GROUP = ATTN_HEADS // KV_HEADS
Q_BLOCK = 128
ROPE_THETA = 10000.0
FILTER_BANDS = 16
FILTER_EMB = 2 * FILTER_BANDS + 1
FILTER_HIDDEN = 64
E_IN = 3 * HY_WIDTH + (ATTN_HEADS + 2 * KV_HEADS) * HEAD_DIM
REC_HEAD_DIM = 128
REC_HEADS = D_MODEL // REC_HEAD_DIM
REC_CHUNK = 32
N_EXPERTS = 16
EXPERT_HIDDEN = D_MODEL
CAPACITY_FACTOR = 2
EPS = 1e-6
HYENA_SLOW_DECAY = -math.log(1e-2) / 1.5
HYENA_FAST_DECAY = -math.log(1e-2) / 0.3

kernel_name = 'hybrid_diffusion_hyena_gqa_hgrn2_ec_step'

def rms_norm(x, g):
    xf = x.astype(jnp.float32)
    y = xf * lax.rsqrt(jnp.mean(xf * xf, axis=-1, keepdims=True) + EPS)
    return (y * g.astype(jnp.float32)).astype(x.dtype)

def short_conv(z, w, b):
    L = z.shape[1]
    zp = jnp.pad(z, ((0, 0), (1, 1), (0, 0)))
    return zp[:, :L] * w[0] + zp[:, 1:L + 1] * w[1] + zp[:, 2:L + 2] * w[2] + b

def hyena_filter(L, w1, b1, freq, w2, b2, w3, decay):
    f32 = lambda a: a.astype(jnp.float32)
    t = jnp.arange(L, dtype=jnp.float32)
    tn = t / L
    bands = jnp.arange(1, FILTER_BANDS + 1, dtype=jnp.float32)
    ang = 2.0 * math.pi * tn[:, None] * bands[None, :]
    feats = jnp.concatenate([tn[:, None], jnp.sin(ang), jnp.cos(ang)], axis=-1)
    h = jnp.sin(f32(freq) * (feats @ f32(w1) + f32(b1)))
    h = jnp.sin(f32(freq) * (h @ f32(w2) + f32(b2)))
    h = h @ f32(w3)
    half = L // 2
    offset = jnp.abs(t - half) / half
    h = h * jnp.exp(-offset[:, None] * jnp.abs(f32(decay))[None, :])
    return h / (jnp.sum(jnp.abs(h), axis=0, keepdims=True) + EPS)

def centred_fftconv(u, h):
    L = u.shape[1]
    n = 2 * L
    U = jnp.fft.rfft(u.astype(jnp.float32), n=n, axis=1)
    H = jnp.fft.rfft(h, n=n, axis=0)
    y = jnp.fft.irfft(U * H[None], n=n, axis=1)
    return y[:, L // 2:L // 2 + L]

def axial_rope(x):
    L = x.shape[1]
    rows = L // GRID_W
    row = jnp.repeat(jnp.arange(rows, dtype=jnp.float32), GRID_W)
    col = jnp.tile(jnp.arange(GRID_W, dtype=jnp.float32), rows)
    axis_dim = HEAD_DIM // 2
    inv = ROPE_THETA ** (-jnp.arange(0, axis_dim, 2, dtype=jnp.float32) / axis_dim)
    xf = x.astype(jnp.float32)

    def rot(xa, pos):
        ang = pos[:, None] * inv[None, :]
        cos = jnp.cos(ang)[None, :, None, :]
        sin = jnp.sin(ang)[None, :, None, :]
        x1, x2 = xa[..., :axis_dim // 2], xa[..., axis_dim // 2:]
        return jnp.concatenate([x1 * cos - x2 * sin, x2 * cos + x1 * sin], axis=-1)

    out = jnp.concatenate([rot(xf[..., :axis_dim], row), rot(xf[..., axis_dim:], col)], axis=-1)
    return out.astype(x.dtype)

def block_attention(q, k, v):
    B, Lq, H, Dh = q.shape
    nb = Lq // Q_BLOCK
    qb = q.reshape(B, nb, Q_BLOCK, KV_HEADS, KV_GROUP, Dh).transpose(1, 0, 2, 3, 4, 5)
    scale = Dh ** -0.5

    def one_block(qblk):
        s = jnp.einsum('bqkgd,bskd->bkgqs', qblk, k, preferred_element_type=jnp.float32) * scale
        p = jax.nn.softmax(s, axis=-1).astype(v.dtype)
        return jnp.einsum('bkgqs,bskd->bqkgd', p, v)

    o = lax.map(one_block, qb)
    return o.transpose(1, 0, 2, 3, 4, 5).reshape(B, Lq, H * Dh)

def gla_chunk_scan(q, k, v, log_f, s0):
    B, L, H, DK = q.shape
    DV = v.shape[-1]
    nc = L // REC_CHUNK

    def to_chunks(a):
        return a.reshape(B, nc, REC_CHUNK, H, a.shape[-1]).transpose(1, 0, 3, 2, 4)

    lower = jnp.tril(jnp.ones((REC_CHUNK, REC_CHUNK), dtype=bool))

    def step(S, inp):
        qc, kc, vc, gc = inp
        b = jnp.cumsum(gc, axis=2)
        inter = jnp.einsum('bhtd,bhde->bhte', qc * jnp.exp(b), S)
        rel = jnp.where(lower[None, None, :, :, None],
                        b[:, :, :, None, :] - b[:, :, None, :, :], -jnp.inf)
        scores = jnp.einsum('bhtd,bhsd,bhtsd->bhts', qc, kc, jnp.exp(rel))
        intra = jnp.einsum('bhts,bhse->bhte', scores, vc)
        b_last = b[:, :, -1]
        S_new = jnp.exp(b_last)[..., None] * S + jnp.einsum(
            'bhsd,bhse->bhde', kc * jnp.exp(b_last[:, :, None, :] - b), vc)
        return S_new, inter + intra

    s_final, o = lax.scan(step, s0, (to_chunks(q), to_chunks(k), to_chunks(v), to_chunks(log_f)))
    o = o.transpose(1, 0, 3, 2, 4).reshape(B, L, H, DV)
    return o, s_final

def expert_choice_ffn(h, router_w, w_gu, w_down):
    B, L, D = h.shape
    n = B * L
    cap = CAPACITY_FACTOR * n // N_EXPERTS
    xf = h.reshape(n, D)
    aff = jax.nn.softmax((xf @ router_w).astype(jnp.float32), axis=-1)
    gate, idx = lax.top_k(aff.T, cap)
    xin = xf[idx]
    gu = jnp.einsum('ecd,edf->ecf', xin, w_gu)
    a, u = jnp.split(gu, 2, axis=-1)
    out = jnp.einsum('ecf,efd->ecd', jax.nn.silu(a) * u, w_down)
    out = out * gate[..., None].astype(out.dtype)
    y = jnp.zeros_like(xf).at[idx.reshape(-1)].add(out.reshape(-1, D))
    return y.reshape(B, L, D)

def setup_inputs(seed: int = 0) -> dict:
    key = jax.random.key(seed)
    ks = jax.random.split(key, 40)
    D = D_MODEL

    def nrm(i, shape, scale):
        return jax.random.normal(ks[i], shape, jnp.float32) * scale

    decay_init = jnp.linspace(HYENA_SLOW_DECAY, HYENA_FAST_DECAY, HY_WIDTH, dtype=jnp.float32)
    return {
        'x_prompt': nrm(0, (BATCH, SEQ, D), 1.0),
        'x_sample': nrm(1, (DEC_BATCH, DEC_SEQ, D), 1.0),
        'cache_k': nrm(2, (DEC_BATCH, N_ATTN_LAYERS, PAST_LEN, KV_HEADS, HEAD_DIM), 1.0),
        'cache_v': nrm(3, (DEC_BATCH, N_ATTN_LAYERS, PAST_LEN, KV_HEADS, HEAD_DIM), 1.0),
        'state_rec': nrm(4, (DEC_BATCH, N_REC_LAYERS, 2, REC_HEADS, REC_HEAD_DIM, REC_HEAD_DIM), 0.3),
        'c': nrm(5, (DEC_BATCH, D), 1.0),
        'c_ctx': nrm(6, (D,), 1.0),
        'mod_w': nrm(7, (DEPTH, D, 6 * D), D ** -0.5),
        'mod_b': nrm(8, (DEPTH, 6 * D), 0.01),
        'norm_mix_g': 1.0 + nrm(9, (DEPTH, D), 0.05),
        'norm_ffn_g': 1.0 + nrm(10, (DEPTH, D), 0.05),
        'e_w_in': nrm(11, (N_ATTN_LAYERS, D, E_IN), D ** -0.5),
        'e_conv_w': nrm(12, (N_ATTN_LAYERS, 3, 3 * HY_WIDTH), 3 ** -0.5),
        'e_conv_b': nrm(13, (N_ATTN_LAYERS, 3 * HY_WIDTH), 0.01),
        'f_w1': nrm(14, (N_ATTN_LAYERS, FILTER_EMB, FILTER_HIDDEN), FILTER_EMB ** -0.5),
        'f_b1': nrm(15, (N_ATTN_LAYERS, FILTER_HIDDEN), 0.1),
        'f_freq': 1.0 + nrm(16, (N_ATTN_LAYERS, FILTER_HIDDEN), 0.1),
        'f_w2': nrm(17, (N_ATTN_LAYERS, FILTER_HIDDEN, FILTER_HIDDEN), FILTER_HIDDEN ** -0.5),
        'f_b2': nrm(18, (N_ATTN_LAYERS, FILTER_HIDDEN), 0.1),
        'f_w3': nrm(19, (N_ATTN_LAYERS, FILTER_HIDDEN, HY_WIDTH), FILTER_HIDDEN ** -0.5),
        'f_decay': decay_init[None, :] + nrm(20, (N_ATTN_LAYERS, HY_WIDTH), 0.1),
        'hy_bias': nrm(21, (N_ATTN_LAYERS, HY_WIDTH), 1.0),
        'q_norm_g': 1.0 + nrm(22, (N_ATTN_LAYERS, HEAD_DIM), 0.05),
        'k_norm_g': 1.0 + nrm(23, (N_ATTN_LAYERS, HEAD_DIM), 0.05),
        'e_w_out': nrm(24, (N_ATTN_LAYERS, HY_WIDTH + ATTN_HEADS * HEAD_DIM, D), D ** -0.5),
        'r_w_in': nrm(25, (N_REC_LAYERS, D, 5 * D), D ** -0.5),
        'r_lb_logits': nrm(26, (N_REC_LAYERS, 2, REC_HEADS * REC_HEAD_DIM), 1.0),
        'r_onorm_g': 1.0 + nrm(27, (N_REC_LAYERS, REC_HEADS * REC_HEAD_DIM), 0.05),
        'r_w_out': nrm(28, (N_REC_LAYERS, D, D), D ** -0.5),
        'router_w': nrm(29, (DEPTH, D, N_EXPERTS), D ** -0.5),
        'moe_w_gu': nrm(30, (DEPTH, N_EXPERTS, D, 2 * EXPERT_HIDDEN), D ** -0.5),
        'moe_w_down': nrm(31, (DEPTH, N_EXPERTS, EXPERT_HIDDEN, D), EXPERT_HIDDEN ** -0.5),
        'final_norm_g': 1.0 + nrm(32, (D,), 0.05),
    }

def reference(x_prompt, x_sample, cache_k, cache_v, state_rec, c, c_ctx,
              mod_w, mod_b, norm_mix_g, norm_ffn_g,
              e_w_in, e_conv_w, e_conv_b, f_w1, f_b1, f_freq, f_w2, f_b2, f_w3, f_decay,
              hy_bias, q_norm_g, k_norm_g, e_w_out,
              r_w_in, r_lb_logits, r_onorm_g, r_w_out,
              router_w, moe_w_gu, moe_w_down, final_norm_g):
    p_lb = jax.nn.softmax(r_lb_logits.astype(jnp.float32), axis=0)
    lower_bounds = jnp.maximum(jnp.cumsum(p_lb, axis=0) - p_lb[0:1], 0.0)

    def hybrid_mixer(h, a, ctx_k, ctx_v):
        B, L, _ = h.shape
        z = h @ e_w_in[a]
        s1 = 3 * HY_WIDTH
        s2 = s1 + ATTN_HEADS * HEAD_DIM
        s3 = s2 + KV_HEADS * HEAD_DIM
        zh, zq, zk, zv = jnp.split(z, [s1, s2, s3], axis=-1)
        zh = short_conv(zh, e_conv_w[a], e_conv_b[a])
        x0, x1, hv = jnp.split(zh, 3, axis=-1)
        filt = hyena_filter(L, f_w1[a], f_b1[a], f_freq[a], f_w2[a], f_b2[a], f_w3[a], f_decay[a])
        u = x1 * hv
        y_h = x0 * (centred_fftconv(u, filt).astype(h.dtype) + u * hy_bias[a])
        q = rms_norm(zq.reshape(B, L, ATTN_HEADS, HEAD_DIM), q_norm_g[a])
        k = rms_norm(zk.reshape(B, L, KV_HEADS, HEAD_DIM), k_norm_g[a])
        v = zv.reshape(B, L, KV_HEADS, HEAD_DIM)
        if ctx_k is None:
            y_a = block_attention(q, k, v)
        else:
            keys = jnp.concatenate([ctx_k.astype(k.dtype), axial_rope(k)], axis=1)
            vals = jnp.concatenate([ctx_v.astype(v.dtype), v], axis=1)
            y_a = block_attention(axial_rope(q), keys, vals)
        out = jnp.concatenate([y_h, y_a], axis=-1) @ e_w_out[a]
        return out, k, v

    def rec_mixer(h, r, s0_fw, s0_bw):
        B, L, _ = h.shape
        z = h @ r_w_in[r]
        zq, zi, zf_fw, zf_bw, zg = jnp.split(z, 5, axis=-1)

        def heads(t):
            return t.astype(jnp.float32).reshape(B, L, REC_HEADS, REC_HEAD_DIM)

        q = jax.nn.silu(heads(zq))
        v = heads(zi)

        def gates(zf, lb):
            zf = heads(zf)
            lb = lb.reshape(REC_HEADS, REC_HEAD_DIM)
            log_f = jnp.logaddexp(jnp.log(lb), jnp.log1p(-lb) + jax.nn.log_sigmoid(zf))
            kk = (1.0 - lb) * jax.nn.sigmoid(-zf)
            return kk, log_f

        k_fw, lf_fw = gates(zf_fw, lower_bounds[r, 0])
        k_bw, lf_bw = gates(zf_bw, lower_bounds[r, 1])
        flip = lambda t: jnp.flip(t, axis=1)
        o_fw, s_fw = gla_chunk_scan(q, k_fw, v, lf_fw, s0_fw)
        o_bw, s_bw = gla_chunk_scan(flip(q), flip(k_bw), flip(v), flip(lf_bw), s0_bw)
        o = o_fw + flip(o_bw)
        o = o * lax.rsqrt(jnp.mean(o * o, axis=-1, keepdims=True) + EPS)
        o = (o.reshape(B, L, D_MODEL) * r_onorm_g[r].astype(jnp.float32)).astype(h.dtype)
        o = o * jax.nn.silu(zg)
        return o @ r_w_out[r], jnp.stack([s_fw, s_bw], axis=1)

    def trunk(x, cond, ctx_k, ctx_v, ctx_s):
        is_context = ctx_k is None
        B = x.shape[0]
        keys, vals, states = [], [], []
        for l in range(DEPTH):
            mod = jax.nn.silu(cond) @ mod_w[l] + mod_b[l]
            mod = mod[None, None, :] if is_context else mod[:, None, :]
            sh_a, sc_a, g_a, sh_f, sc_f, g_f = jnp.split(mod, 6, axis=-1)
            hn = rms_norm(x, norm_mix_g[l]) * (1.0 + sc_a) + sh_a
            if l % 2 == 0:
                a = l // 2
                if is_context:
                    out, k, v = hybrid_mixer(hn, a, None, None)
                    keys.append(k)
                    vals.append(v)
                else:
                    out, _, _ = hybrid_mixer(hn, a, ctx_k[:, a], ctx_v[:, a])
            else:
                r = l // 2
                if is_context:
                    zero = jnp.zeros((B, REC_HEADS, REC_HEAD_DIM, REC_HEAD_DIM), jnp.float32)
                    out, s = rec_mixer(hn, r, zero, zero)
                    states.append(s)
                else:
                    out, _ = rec_mixer(hn, r, ctx_s[:, r, 0].astype(jnp.float32),
                                       ctx_s[:, r, 1].astype(jnp.float32))
            x = x + g_a * out
            hn = rms_norm(x, norm_ffn_g[l]) * (1.0 + sc_f) + sh_f
            x = x + g_f * expert_choice_ffn(hn, router_w[l], moe_w_gu[l], moe_w_down[l])
        return rms_norm(x, final_norm_g), keys, vals, states

    y_prompt, keys, vals, states = trunk(x_prompt, c_ctx, None, None, None)
    y_sample, _, _, _ = trunk(x_sample, c, cache_k, cache_v, state_rec)
    new_cache_k = jnp.stack(keys, axis=1)
    new_cache_v = jnp.stack(vals, axis=1)
    new_state_rec = jnp.stack(states, axis=1).astype(x_prompt.dtype)
    return (y_prompt, y_sample, new_cache_k, new_cache_v, new_state_rec)


_drawn_inputs = setup_inputs


def setup_inputs(seed=0):
    import zlib

    import numpy as np

    out = dict(_drawn_inputs(seed))
    spreads = {}
    factors = {'cache_k': 4.201,
     'cache_v': 3.436,
     'state_rec': 64.0,
     'e_conv_b': 3.125,
     'q_norm_g': 8.0,
     'r_onorm_g': 2.714}
    for name, (base, spread) in spreads.items():
        noise = np.random.default_rng([zlib.crc32(name.encode()), seed]).standard_normal(out[name].shape)
        drawn = base * np.exp(spread * noise) if base else spread * noise
        out[name] = __import__('jax').numpy.asarray(drawn.astype(out[name].dtype))
    for name, factor in factors.items():
        out[name] = (out[name] * factor).astype(out[name].dtype)
    return out
```

```python
import math
from contextlib import ExitStack

import numpy as np
import concourse.bass as bass
from concourse import mybir

F32 = mybir.dt.float32
U32 = mybir.dt.uint32
ALU = mybir.AluOpType
ACT = mybir.ActivationFunctionType
AX_X = mybir.AxisListType.X

P = 128
D = 1024
KD = D // P
LC, LL = 256, 1024
T = LC + LL
NT = T // P
CT = LC // P
DEPTH = 2
EPS = 1e-6
HW = D // 2
HD, NH, NKV = 64, 8, 2
PAST = 256
RH, RD = 8, 128
NE = 16
FH = D
CAP = [2 * LC // NE, 2 * LL // NE]
PIECES = [(0, 2, 0), (2, 4, 1), (6, 4, 1)]
SEQS = [(0, LC), (LC, LL)]

ROWS = {}
_at = 0
for _name, _n in [("norm_mix_g", 2 * KD), ("norm_ffn_g", 2 * KD), ("e_conv_w", 36), ("e_conv_b", 12),
                  ("hy_bias", 4), ("r_onorm_g", KD), ("r_lb_logits", 2 * KD), ("c_ctx", KD), ("c", KD)]:
    ROWS[_name] = (_at, _n)
    _at += _n
NROWS = _at


class Count:

    def __init__(self, sem, start=0):
        self.sem, self.start, self.n = sem, start, 0

    def give(self, ins, by=1):
        ins.then_inc(self.sem, by)
        self.n += by
        return self.n

    def wait(self, eng, n=None):
        eng.wait_ge(self.sem, self.start + (self.n if n is None else n))

    def link(self, eng, ins):
        self.give(ins)
        self.wait(eng)


def scope(nc, ctx, tag):
    sems = []

    def clear():
        if sems:
            nc.clear_and_free_semaphores(sems)
            nc.all_engine_barrier()

    ctx.callback(clear)

    def sb(name, shape, dt=F32):
        return ctx.enter_context(nc.sbuf_tensor(f"{tag}_{name}", shape, dt))

    def ps(name, shape, dt=F32):
        return ctx.enter_context(nc.psum_tensor(f"{tag}_{name}", shape, dt))

    def sem(name):
        sems.append(nc.alloc_semaphore(f"{tag}_{name}"))
        return sems[-1]
    return sb, ps, sem


def modulation(nc, A, S):
    NB = 12
    G = 3
    RING = 4
    with ExitStack() as ctx:
        sb, ps, sem = scope(nc, ctx, "mod")
        pack = sb("pack", [P, P])
        w = sb("w_ring", [P, RING, KD, 512])
        row = sb("row", [P, DEPTH, G, 512])
        brow = sb("brow", [P, DEPTH, G, 512])
        scond = sb("scond", [P, 2, KD])
        pst = ps("pst", [P, 512])
        psm = [ps(f"psm{i}", [P, 512]) for i in range(2)]
        pack_in, bias_in, bias_zero = sem("pack_in"), sem("bias_in"), sem("bias_zero")
        w_in = [sem(f"w_in{i}") for i in range(RING)]
        w_used, packed, col_ready, cond_ready = sem("w_used"), sem("packed"), sem("col_ready"), sem("cond_ready")
        row_ready, tr_done, tr_used, stored = sem("row_ready"), sem("tr"), sem("tr_used"), sem("stored")
        v_steps = sem("v")
        block = ctx.enter_context(nc.Block())

        @block.sync
        def _(sp):
            n = 0
            for name, (at, rows) in ROWS.items():
                src = A[name]
                flat = {1: "(r p) -> r p", 2: "a (r p) -> (a r) p", 3: "a b (r p) -> (a b r) p"}[len(src.shape)]
                sp.dma_start(pack[at:at + rows, :], src.rearrange(flat, p=P)).then_inc(pack_in, 16)
                n += 16
            assert n == 16 * len(ROWS)
            sp.dma_start(S["ident"][:, :], A["k_ident"]).then_inc(pack_in, 16)
            for i in range(DEPTH * NB):
                l, b = divmod(i, NB)
                if i >= RING:
                    sp.wait_ge(w_used, i - RING + 1)
                sp.dma_start(w[:, i % RING, :, :],
                             A["mod_w"][l, :, b * 512:(b + 1) * 512].rearrange("(k p) n -> p k n", p=P)
                             ).then_inc(w_in[i % RING], 16)

        @block.scalar
        def _(act):
            act.wait_ge(bias_zero, 1)
            for j in range(4):
                for l in range(DEPTH):
                    src = A["mod_b"][l, :].rearrange("(g j n) -> j g n", j=4, n=512)[j:j + 1]
                    for c in range(2):
                        act.dma_start(brow[32 * j + c:32 * j + c + 1, l, :, :], src).then_inc(bias_in, 16)
            act.wait_ge(col_ready, 1)
            at = ROWS["c_ctx"][0]
            nc.scalar.activation(scond[:, :, :].rearrange("p c k -> p (c k)"), S["vec"][:, at:at + 2 * KD],
                                 ACT.Silu).then_inc(cond_ready, 1)
            act.wait_ge(row_ready, DEPTH * G)
            for j in range(4):
                for l in range(DEPTH):
                    dst = S["mod_dram"][l].rearrange("c (g j n) -> j c g n", j=4, n=512)[j]
                    act.dma_start(dst, row[32 * j:32 * j + 2, l, :, :]).then_inc(stored, 16)
            act.wait_ge(stored, 16 * 4 * DEPTH)

        @block.tensor
        def _(pe):
            pe.wait_ge(pack_in, 16 * (len(ROWS) + 1))
            nc.tensor.transpose(pst[:, 0:NROWS], pack[0:NROWS, :], S["ident"][0:NROWS, 0:NROWS]).then_inc(packed, 1)
            pe.wait_ge(cond_ready, 1)
            for g in range(DEPTH * G):
                if g >= 2:
                    pe.wait_ge(row_ready, g - 1)
                for j in range(4):
                    i = 4 * g + j
                    pe.wait_ge(w_in[i % RING], 16 * (i // RING + 1))
                for k in range(KD):
                    for j in range(4):
                        m = nc.tensor.matmul(psm[g % 2][32 * j:32 * j + 2, :], scond[:, :, k], w[:, (4 * g + j) % RING, k, :],
                                             start=(k == 0), stop=(k == KD - 1), tile_position=(0, 32 * j))
                        if k == KD - 1:
                            m.then_inc(w_used, 1)
            pe.wait_ge(row_ready, DEPTH * G)
            for l in range(DEPTH):
                for g in range(G):
                    i = l * G + g
                    if i >= 1:
                        pe.wait_ge(tr_used, i)
                    for q in range(4):
                        m = nc.tensor.transpose(pst[:, q * P:(q + 1) * P], row[:, l, g, q * P:(q + 1) * P],
                                                S["ident"][:, :])
                    m.then_inc(tr_done, 1)

        @block.vector
        def _(dve):
            steps = Count(v_steps)
            nc.vector.memset(brow[:, :, :, :], 0.0).then_inc(bias_zero, 1)
            steps.link(dve, nc.vector.memset(row[:, :, :, :], 0.0))
            dve.wait_ge(packed, 1)
            nc.vector.tensor_copy(S["vec"][:, :], pst[:, 0:NROWS]).then_inc(col_ready, 1)
            dve.wait_ge(bias_in, 16 * 4 * DEPTH * 2)
            for g in range(DEPTH * G):
                dve.wait_ge(w_used, 4 * (g + 1))
                for j in range(4):
                    r = nc.vector.tensor_tensor(row[32 * j:32 * j + 2, g // G, g % G, :], psm[g % 2][32 * j:32 * j + 2, :],
                                                brow[32 * j:32 * j + 2, g // G, g % G, :], ALU.add)
                r.then_inc(row_ready, 1)
            mc = S["modcol"]
            for l in range(DEPTH):
                for g in range(G):
                    dve.wait_ge(tr_done, l * G + g + 1)
                    for j in range(4):
                        b = 4 * g + j
                        src = pst[:, :].rearrange("p (q r) -> p q r", r=P)[:, :, 32 * j:32 * j + 2]
                        r = nc.vector.tensor_copy(
                            mc[:, l, b // 2, :, 4 * (b % 2):4 * (b % 2) + 4].rearrange("p c q -> p q c"), src)
                    r.then_inc(tr_used, 1)
            dve.wait_ge(tr_used, DEPTH * G)
            dve.wait_ge(col_ready, 1)
            for l in range(DEPTH):
                for s, gain in ((1, "norm_mix_g"), (4, "norm_ffn_g")):
                    at = ROWS[gain][0] + l * KD
                    for c in range(2):
                        r = nc.vector.scalar_tensor_tensor(mc[:, l, s, c, :], mc[:, l, s, c, :], 1.0,
                                                           S["vec"][:, at:at + KD], ALU.add, ALU.mult)


def norm_transpose(nc, A, S, tag, x_dram, layer, shift, scale, hnT, xn_dram=None, residual=None):
    with ExitStack() as ctx:
        sb, ps, sem = scope(nc, ctx, tag)
        x = sb("x", [P, NT, D])
        src = x
        if residual is not None:
            src = sb("y", [P, NT, D])
            gate = sb("gate", [P, 2, D])
            y_in, g_in, x_stored, gated, summed = [sem(f"y{t}") for t in range(NT)], sem("g_in"), sem("x_stored"), sem("gated"), sem("summed")
        junk = sb("junk", [P, 2, D])
        ssq, rstd = sb("ssq", [P, NT]), sb("rstd", [P, NT])
        NPS = 6
        pst = [ps(f"ps{i}", [P, 512]) for i in range(NPS)]
        x_in = [sem(f"x{t}") for t in range(NT)]
        squared, inverted, v_steps, rooted, scaled, tr, ev_a, ev_v, stored = (
            sem("squared"), sem("inverted"), sem("v"), sem("rooted"), sem("scaled"), sem("tr"),
            sem("ev_a"), sem("ev_v"), sem("stored"))
        block = ctx.enter_context(nc.Block())
        units = [(t0, n, c, k) for t0, n, c in PIECES for k in range(KD)]
        groups = [(t0, n) for t0, n, _ in PIECES]

        @block.sync
        def _(sp):
            for t in range(NT):
                sp.dma_start(x[:, t, :], x_dram(t)).then_inc(x_in[t], 16)
                if residual is not None:
                    if t == 0:
                        for c in range(2):
                            sp.dma_start(gate[:, c, :], S["mod_dram"][residual[1], c:c + 1, 5 * D:6 * D].broadcast_to([P, D])).then_inc(g_in, 16)
                    sp.dma_start(src[:, t, :], residual[0][t * P:(t + 1) * P, :]).then_inc(y_in[t], 16)
            if residual is not None:
                for t in range(NT):
                    sp.wait_ge(summed, t + 1)
                    sp.dma_start(residual[2][t * P:(t + 1) * P, :], src[:, t, :]).then_inc(x_stored, 16)
                sp.wait_ge(x_stored, 16 * NT)
            if xn_dram is not None:
                for t in range(NT):
                    sp.wait_ge(scaled, t + 1)
                    sp.dma_start(xn_dram[t * P:(t + 1) * P, :], x[:, t, :]).then_inc(stored, 16)
                sp.wait_ge(stored, 16 * NT)

        @block.scalar
        def _(act):
            for g, (t0, n) in enumerate(groups):
                for t in range(t0, t0 + n):
                    if residual is None:
                        act.wait_ge(x_in[t], 16)
                    else:
                        act.wait_ge(summed, t + 1)
                    if t >= 2:
                        act.wait_ge(squared, t - 1)
                    nc.scalar.activation(junk[:, t % 2, :], src[:, t, :], ACT.Square,
                                         accum_out=ssq[:, t:t + 1]).then_inc(squared, 1)
                act.wait_ge(inverted, g + 1)
                nc.scalar.activation(rstd[:, t0:t0 + n], rstd[:, t0:t0 + n], ACT.Sqrt).then_inc(rooted, 1)
            for u, (t0, n, c, k) in enumerate(units):
                if u % 2 == 0:
                    act.wait_ge(tr, u + 1)
                    nc.scalar.activation(hnT[:, k, t0 * P:(t0 + n) * P], pst[u % NPS][:, 0:n * P], ACT.Identity,
                                         bias=S["modcol"][:, layer, shift, c, k:k + 1],
                                         scale=S["modcol"][:, layer, scale, c, k:k + 1]).then_inc(ev_a, 1)

        @block.vector
        def _(dve):
            steps = Count(v_steps)
            if residual is not None:
                dve.wait_ge(g_in, 32)
            for g, (t0, n) in enumerate(groups):
                if residual is not None:
                    for t in range(t0, t0 + n):
                        dve.wait_ge(y_in[t], 16)
                        nc.vector.tensor_tensor(src[:, t, :], src[:, t, :], gate[:, 0 if t < CT else 1, :], ALU.mult).then_inc(gated, 1)
                        dve.wait_ge(gated, t + 1)
                        dve.wait_ge(x_in[t], 16)
                        nc.vector.tensor_tensor(src[:, t, :], src[:, t, :], x[:, t, :], ALU.add).then_inc(summed, 1)
                    dve.wait_ge(summed, t0 + n)
                dve.wait_ge(squared, t0 + n)
                steps.link(dve, nc.vector.tensor_scalar(rstd[:, t0:t0 + n], ssq[:, t0:t0 + n], 1.0 / D, EPS, ALU.mult, ALU.add))
                nc.vector.reciprocal(rstd[:, t0:t0 + n], rstd[:, t0:t0 + n]).then_inc(inverted, 1)
                dve.wait_ge(rooted, g + 1)
                for t in range(t0, t0 + n):
                    nc.vector.tensor_scalar(x[:, t, :], src[:, t, :], rstd[:, t:t + 1], None, ALU.mult).then_inc(scaled, 1)
            for u, (t0, n, c, k) in enumerate(units):
                if u % 2 == 1:
                    dve.wait_ge(tr, u + 1)
                    nc.vector.tensor_scalar(hnT[:, k, t0 * P:(t0 + n) * P], pst[u % NPS][:, 0:n * P],
                                            S["modcol"][:, layer, scale, c, k:k + 1],
                                            S["modcol"][:, layer, shift, c, k:k + 1], ALU.mult, ALU.add).then_inc(ev_v, 1)

        @block.tensor
        def _(pe):
            for u, (t0, n, c, k) in enumerate(units):
                pe.wait_ge(scaled, t0 + n)
                if u >= NPS:
                    prev = u - NPS
                    pe.wait_ge(ev_v if prev % 2 else ev_a, prev // 2 + 1)
                for i in range(n):
                    m = nc.tensor.transpose(pst[u % NPS][:, i * P:(i + 1) * P], x[:, t0 + i, k * P:(k + 1) * P],
                                            S["ident"][:, :])
                m.then_inc(tr, 1)


def hyena_in(nc, A, S, hnT, x0, u, uT):
    NPS, NTR, NZ = 5, 3, 3
    with ExitStack() as ctx:
        sb, ps, sem = scope(nc, ctx, "hin")
        w = sb("w", [P, 2, KD, 3, P])
        z = sb("z", [P, NZ, LC + 2 + LL + 2])
        x1 = sb("x1", [P, 2, T])
        hv = sb("hv", [P, 2, T])
        psm = [ps(f"psm{i}", [P, 512]) for i in range(NPS)]
        pst = [ps(f"pst{i}", [P, 512]) for i in range(NTR)]
        w_in = [sem("w_in0"), sem("w_in1")]
        mm, z_ready, z_used, v_steps, u_ready, tr, tr_used, zeroed = (
            sem("mm"), sem("z_ready"), sem("z_used"), sem("v"), sem("u_ready"),
            sem("tr"), sem("tr_used"), sem("zeroed"))
        ZAT = {0: 1, LC: LC + 3}
        block = ctx.enter_context(nc.Block())

        @block.sync
        def _(sp):
            for i in range(4):
                if i >= 2:
                    sp.wait_ge(mm, 9 * (i - 1))
                for part in range(3):
                    c0 = part * HW + i * P
                    sp.dma_start(w[:, i % 2, :, part, :],
                                 A["e_w_in"][0, :, c0:c0 + P].rearrange("(k p) n -> p k n", p=P)).then_inc(w_in[i % 2], 16)

        @block.tensor
        def _(pe):
            def transposes(i):
                pe.wait_ge(u_ready, i + 1)
                for g, (t0, n, _) in enumerate(PIECES):
                    if i >= 1:
                        pe.wait_ge(tr_used, 3 * (i - 1) + g + 1)
                    for t in range(n):
                        m = nc.tensor.transpose(pst[g][:, t * P:(t + 1) * P],
                                                u[:, i, (t0 + t) * P:(t0 + t + 1) * P], S["ident"][:, :])
                    m.then_inc(tr, 1)

            for i in range(4):
                pe.wait_ge(w_in[i % 2], 48 * (i // 2 + 1))
                for part in range(3):
                    for g, (t0, n, _) in enumerate(PIECES):
                        j = 9 * i + 3 * part + g
                        if j >= NPS:
                            pe.wait_ge(z_ready, j - NPS + 1)
                        for k in range(KD):
                            m = nc.tensor.matmul(psm[j % NPS][:, 0:n * P], w[:, i % 2, k, part, :],
                                                 hnT[:, k, t0 * P:(t0 + n) * P], start=(k == 0), stop=(k == KD - 1))
                        m.then_inc(mm, 1)
                    if part == 0 and i >= 1:
                        transposes(i - 1)
            transposes(3)

        @block.scalar
        def _(act):
            act.wait_ge(zeroed, 1)

            def to_uT(i):
                for g, (t0, n, _) in enumerate(PIECES):
                    act.wait_ge(tr, 3 * i + g + 1)
                    nc.scalar.activation(uT[:, t0:t0 + n, i * P:(i + 1) * P],
                                         pst[g][:, 0:n * P].rearrange("p (t c) -> p t c", c=P), ACT.Copy).then_inc(tr_used, 1)

            for tile in range(12):
                i, part = divmod(tile, 3)
                if tile >= NZ:
                    act.wait_ge(z_used, tile - NZ + 1)
                for g, (t0, n, c) in enumerate(PIECES):
                    at = ZAT[SEQS[c][0]] + t0 * P - SEQS[c][0]
                    act.wait_ge(mm, 3 * tile + g + 1)
                    nc.scalar.activation(z[:, tile % NZ, at:at + n * P], psm[(3 * tile + g) % NPS][:, 0:n * P],
                                         ACT.Copy).then_inc(z_ready, 1)
                if part == 1 and i >= 1:
                    to_uT(i - 1)
            to_uT(3)

        @block.vector
        def _(dve):
            steps = Count(v_steps)
            nc.vector.memset(z[:, :, :], 0.0).then_inc(zeroed, 1)
            for tile in range(12):
                i, part = divmod(tile, 3)
                dve.wait_ge(z_ready, 3 * (tile + 1))
                out = (x0[:, i, :], x1[:, i % 2, :], hv[:, i % 2, :])[part]
                wc, bc = ROWS["e_conv_w"][0] + part * 4 + i, ROWS["e_conv_b"][0] + part * 4 + i
                at = [(o, ln, ZAT[o] - 1) for o, ln in SEQS]
                for o, ln, a in at:
                    r = nc.vector.tensor_scalar(out[:, o:o + ln], z[:, tile % NZ, a:a + ln], S["vec"][:, wc:wc + 1],
                                                S["vec"][:, bc:bc + 1], ALU.mult, ALU.add)
                steps.link(dve, r)
                for tap in (1, 2):
                    for o, ln, a in at:
                        r = nc.vector.scalar_tensor_tensor(out[:, o:o + ln], z[:, tile % NZ, a + tap:a + tap + ln],
                                                           S["vec"][:, wc + 12 * tap:wc + 12 * tap + 1],
                                                           out[:, o:o + ln], ALU.mult, ALU.add)
                    if tap == 1:
                        steps.link(dve, r)
                r.then_inc(z_used, 1)
                if part == 2:
                    dve.wait_ge(z_used, tile + 1)
                    nc.vector.tensor_tensor(u[:, i, :], x1[:, i % 2, :], hv[:, i % 2, :], ALU.mult).then_inc(u_ready, 1)


def hyena_filter(nc, A, S, filt):
    MAGIC = 12582912.0
    TWO_PI = 2 * math.pi
    HI = 6.28125
    LO = TWO_PI - HI
    EMB, FHID = 33, 64
    with ExitStack() as ctx:
        sb, ps, sem = scope(nc, ctx, "fil")
        feats = sb("feats", [EMB, T])
        w1, w2, w3 = sb("w1", [EMB, FHID]), sb("w2", [FHID, FHID]), sb("w3", [FHID, HW])
        cols = sb("cols", [FHID, 3])
        arg, turn, hid = sb("arg", [FHID, T]), sb("turn", [FHID, T]), sb("hid", [FHID, T])
        decay, offs = sb("decay", [P, HW]), sb("offs", [P, NT])
        win = sb("win", [P, NT, HW])
        ones = sb("ones", [P, P])
        rsum = sb("rsum", [P, 2, HW])
        psl = [ps(f"psl{i}", [P, 512]) for i in range(3)]
        psw = [ps(f"psw{i}", [P, 512]) for i in range(3)]
        pss = [ps("pss0", [P, 512]), ps("pss1", [P, 512])]
        loaded, v_steps, mm, sined, w_ready, h_mm, h_ready, a_ready, summed, ab, abs_ready = (
            sem("loaded"), sem("v"), sem("mm"), sem("sined"), sem("w_ready"), sem("h_mm"), sem("h_ready"),
            sem("a_ready"), sem("summed"), sem("ab"), sem("abs_ready"))
        block = ctx.enter_context(nc.Block())

        @block.sync
        def _(sp):
            for dst, src in ((feats, A["k_feats"]), (w1, A["f_w1"][0]), (w2, A["f_w2"][0]), (w3, A["f_w3"][0]),
                             (offs, A["k_offsets"])):
                sp.dma_start(dst[:, :], src).then_inc(loaded, 16)
            for j, name in enumerate(("f_b1", "f_freq", "f_b2")):
                sp.dma_start(cols[:, j:j + 1], A[name][0].rearrange("(p a) -> p a", a=1)).then_inc(loaded, 16)
            sp.dma_start(decay[:, :], A["f_decay"].broadcast_to([P, HW])).then_inc(loaded, 16)

        LOADS = 9 * 16

        @block.tensor
        def _(pe):
            pe.wait_ge(loaded, LOADS)
            for layer, (wt, x) in enumerate(((w1, feats), (w2, hid))):
                if layer:
                    pe.wait_ge(sined, 1)
                for g, (t0, n, _) in enumerate(PIECES):
                    m = nc.tensor.matmul(psl[g][0:FHID, 0:n * P], wt[:, :], x[:, t0 * P:(t0 + n) * P], start=True, stop=True)
                m.then_inc(mm, 1)
            pe.wait_ge(sined, 2)
            for t in range(NT):
                if t >= 3:
                    pe.wait_ge(h_ready, t - 2)
                nc.tensor.matmul(psw[t % 3][:, :], hid[:, t * P:(t + 1) * P], w3[:, :], start=True, stop=True).then_inc(h_mm, 1)
            pe.wait_ge(abs_ready, NT)
            for c, (o, ln) in enumerate(SEQS):
                for t in range(o // P, (o + ln) // P):
                    m = nc.tensor.matmul(pss[c][:, :], ones[:, :], win[:, t, :], start=(t == o // P), stop=((t + 1) * P == o + ln))
                m.then_inc(summed, 1)

        @block.scalar
        def _(act):
            act.wait_ge(loaded, LOADS)
            nc.scalar.activation(decay[:, :], decay[:, :], ACT.Abs).then_inc(ab, 1)
            for layer in range(2):
                act.wait_ge(a_ready, layer + 1)
                nc.scalar.activation(hid[:, :], arg[:, :], ACT.Sin).then_inc(sined, 1)
            act.wait_ge(ab, 1)
            for t in range(NT):
                nc.scalar.activation(win[:, t, :], decay[:, :], ACT.Exp, scale=offs[:, t:t + 1]).then_inc(w_ready, 1)
            for t in range(NT):
                act.wait_ge(h_ready, t + 1)
                nc.scalar.activation(win[:, t, :], filt[:, t, :], ACT.Abs).then_inc(abs_ready, 1)

        @block.vector
        def _(dve):
            steps = Count(v_steps)
            nc.vector.memset(ones[:, :], 1.0)
            dve.wait_ge(loaded, LOADS)
            for layer in range(2):
                dve.wait_ge(mm, layer + 1)
                for g, (t0, n, _) in enumerate(PIECES):
                    r = nc.vector.tensor_scalar(arg[:, t0 * P:(t0 + n) * P], psl[g][0:FHID, 0:n * P],
                                                cols[:, 2 * layer:2 * layer + 1], cols[:, 1:2], ALU.add, ALU.mult)
                steps.link(dve, r)
                steps.link(dve, nc.vector.tensor_scalar(turn[:, :], arg[:, :], 1.0 / TWO_PI, MAGIC, ALU.mult, ALU.add))
                steps.link(dve, nc.vector.tensor_scalar(turn[:, :], turn[:, :], MAGIC, None, ALU.subtract))
                steps.link(dve, nc.vector.scalar_tensor_tensor(arg[:, :], turn[:, :], -HI, arg[:, :], ALU.mult, ALU.add))
                steps.link(dve, nc.vector.scalar_tensor_tensor(arg[:, :], turn[:, :], -LO, arg[:, :], ALU.mult, ALU.add))
                nc.vector.tensor_scalar(arg[:, :], arg[:, :], 3.1415925, -3.1415925, ALU.min, ALU.max).then_inc(a_ready, 1)
            for t in range(NT):
                dve.wait_ge(h_mm, t + 1)
                dve.wait_ge(w_ready, t + 1)
                nc.vector.tensor_tensor(filt[:, t, :], psw[t % 3][:, :], win[:, t, :], ALU.mult).then_inc(h_ready, 1)
            dve.wait_ge(summed, 2)
            for c in range(2):
                steps.link(dve, nc.vector.tensor_scalar(rsum[:, c, :], pss[c][:, :], EPS, None, ALU.add))
                steps.link(dve, nc.vector.reciprocal(rsum[:, c, :], rsum[:, c, :]))
            for t in range(NT):
                nc.vector.tensor_tensor(filt[:, t, :], filt[:, t, :], rsum[:, 0 if t < CT else 1, :], ALU.mult)


CONV = [
    (3 * LC // 2, 96, 2), (3 * LL // 2, 128, 6)]


def hyena_conv(nc, A, S, x0, u, uT, filt):
    NF, NG = 2, 2
    NFT = [c[2] for c in CONV]
    with ExitStack() as ctx:
        sb, ps, sem = scope(nc, ctx, "cv")
        fwd = sb("fwd", [P, NF, 8, 2, P])
        inv = sb("inv", [P, 12, 512])
        Y = sb("Y", [P, 6, 2, HW])
        H = sb("H", [P, 2, HW])
        tmp = sb("tmp", [P, 4, HW])
        psf = [ps(f"psf{i}", [P, 512]) for i in range(8)]
        f_in = [sem(f"f_in{i}") for i in range(NF)]
        i_in = sem("i_in")
        u_mm, h_mm, h_out, prod, v_steps, y_ready, inv_mm, out_ready = (
            sem("u_mm"), sem("h_mm"), sem("h_out"), sem("prod"), sem("v"), sem("y_ready"), sem("inv_mm"), sem("out_ready"))
        block = ctx.enter_context(nc.Block())
        ftiles = [(c, f) for c in range(2) for f in range(NFT[c])]
        halves = [(0, 0, LC)] + [(1, h * 512, 512) for h in range(2)]

        def inverse_in(sp, h):
            if h:
                sp.wait_ge(inv_mm, 4 * h)
            if h == 0:
                sp.dma_start(inv[0:96, 0:4, 0:LC], A["k_inv_c"]).then_inc(i_in, 16)
            else:
                sp.dma_start(inv[:, :, :], A["k_inv_l"][h - 1]).then_inc(i_in, 16)

        @block.sync
        def _(sp):
            for n, (c, f) in enumerate(ftiles):
                if n >= NF:
                    sp.wait_ge(h_mm, n - NF + 1)
                tt, fw = (2, 96) if c == 0 else (8, 128)
                src = A["k_fwd_c"][f] if c == 0 else A["k_fwd_l"][f]
                sp.dma_start(fwd[:, n % NF, 0:tt, :, 0:fw], src.rearrange("p (t r f) -> p t r f", t=tt, r=2)).then_inc(f_in[n % NF], 16)
                if n in (1, 6):
                    inverse_in(sp, 0 if n == 1 else 1)
            inverse_in(sp, 2)

        @block.tensor
        def _(pe):
            def forward(n):
                c, f = ftiles[n]
                t0, tt, fw = (0, 2, 96) if c == 0 else (2, 8, 128)
                pe.wait_ge(f_in[n % NF], 16 * (n // NF + 1))
                if n == 2:
                    pe.wait_ge(out_ready, 4)
                if n >= 2:
                    pe.wait_ge(prod, n - 1)
                for q, (src, done) in enumerate(((uT, u_mm), (filt, h_mm))):
                    for r in range(2):
                        for t in range(tt):
                            m = nc.tensor.matmul(psf[4 * (n % 2) + 2 * q + r][0:fw, :], fwd[:, n % NF, t, r, 0:fw], src[:, t0 + t, :],
                                                 start=(t == 0), stop=(t == tt - 1))
                    m.then_inc(done, 1)

            def inverse(h):
                c, o, ln = halves[h]
                fw, nf = CONV[c][1], NFT[c]
                pe.wait_ge(i_in, 16 * (h + 1))
                pe.wait_ge(y_ready, 2 if c == 0 else 8)
                for ch in range(4):
                    n = 4 * h + ch
                    bank = psf[4 + ch if h < 2 else ch]
                    for j in range(2 * nf):
                        m = nc.tensor.matmul(bank[:, 0:ln], Y[0:fw, j // 2, j % 2, ch * P:(ch + 1) * P], inv[0:fw, j, 0:ln],
                                             start=(j == 0), stop=(j == 2 * nf - 1))
                    m.then_inc(inv_mm, 1)

            forward(0)
            forward(1)
            pe.wait_ge(prod, 2)
            inverse(0)
            for n in range(2, 8):
                forward(n)
            pe.wait_ge(prod, 8)
            inverse(1)
            inverse(2)

        @block.scalar
        def _(act):
            for n, (c, f) in enumerate(ftiles):
                fw = CONV[c][1]
                act.wait_ge(h_mm, n + 1)
                if n >= 1:
                    act.wait_ge(prod, n)
                for r in range(2):
                    h = nc.scalar.activation(H[0:fw, r, :], psf[4 * (n % 2) + 2 + r][0:fw, :], ACT.Copy)
                h.then_inc(h_out, 1)

        @block.vector
        def _(dve):
            steps = Count(v_steps)

            def outputs(h):
                c, o, ln = halves[h]
                o += SEQS[c][0]
                at = ROWS["hy_bias"][0]
                for ch in range(4):
                    n = 4 * h + ch
                    dve.wait_ge(inv_mm, n + 1)
                    bank = psf[4 + ch if h < 2 else ch]
                    steps.link(dve, nc.vector.scalar_tensor_tensor(u[:, ch, o:o + ln], u[:, ch, o:o + ln],
                                                                   S["vec"][:, at + ch:at + ch + 1], bank[:, 0:ln], ALU.mult, ALU.add))
                    nc.vector.tensor_tensor(x0[:, ch, o:o + ln], x0[:, ch, o:o + ln], u[:, ch, o:o + ln], ALU.mult).then_inc(out_ready, 1)

            for n, (c, f) in enumerate(ftiles):
                if n == 2:
                    outputs(0)
                fw = CONV[c][1]
                dve.wait_ge(u_mm, n + 1)
                dve.wait_ge(h_out, n + 1)
                if n >= 1:
                    dve.wait_ge(y_ready, n)
                if n == 2:
                    dve.wait_ge(inv_mm, 4)
                ur, ui = (psf[4 * (n % 2) + r][0:fw, :] for r in range(2))
                yf = f
                for j, (a, r) in enumerate(((ur, 0), (ui, 1), (ur, 1), (ui, 0))):
                    last = nc.vector.tensor_tensor(tmp[0:fw, j, :], a, H[0:fw, r, :], ALU.mult)
                steps.give(last)
                steps.wait(dve)
                nc.vector.tensor_tensor(Y[0:fw, yf, 0, :], tmp[0:fw, 0, :], tmp[0:fw, 1, :], ALU.subtract).then_inc(prod, 1)
                nc.vector.tensor_tensor(Y[0:fw, yf, 1, :], tmp[0:fw, 2, :], tmp[0:fw, 3, :], ALU.add).then_inc(y_ready, 1)
            outputs(1)
            outputs(2)


KT = NT + PAST // P


def key_tile(t):
    return t if t < CT else t + PAST // P


def qkv_in(nc, A, S, hnT, qT, kT, v, out_k, out_v):
    QW, KW = NH * HD, NKV * HD
    NHQ = NH + NKV
    with ExitStack() as ctx:
        sb, ps, sem = scope(nc, ctx, "qkv")
        w = sb("w", [P, KD, QW + 2 * KW])
        z = sb("z", [P, 2, QW + KW])
        sq = sb("sq", [P, 2, QW + KW])
        kd = sb("kd", [P, 2, NKV, 2, HD])
        ck = sb("ck", [P, PAST // P, NKV, HD])
        ckd = sb("ckd", [P, PAST // P, NKV, 2, HD])
        ra, rb = sb("ra", [P, NHQ, 2, 2, 16]), sb("rb", [P, NHQ, 2, 2, 16])
        cos, sin = sb("cos", [P, LL // P, 2, 16]), sb("sin", [P, LL // P, 2, 16])
        gain = sb("gain", [P, 2, HD])
        ss = sb("ss", [P, NT, NHQ])
        psq = [ps(f"psq{i}", [P, 512]) for i in range(2)]
        pskv = [ps(f"pskv{i}", [P, 512]) for i in range(2)]
        ptq = [ps(f"ptq{i}", [P, 512]) for i in range(2)]
        ptk = [ps(f"ptk{i}", [P, 512]) for i in range(2)]
        w_in = [sem(f"w_in{k}") for k in range(KD)]
        k_stored = [sem(f"k_stored{t}") for t in range(CT)]
        loaded, v_steps, mm, z_out, z_sq, inv, root, r_ready, tr, tr_used, c_dup, stored, kv_out, gains = (
            sem("loaded"), sem("v"), sem("mm"), sem("z_out"), sem("z_sq"), sem("inv"), sem("root"), sem("r_ready"),
            sem("tr"), sem("tr_used"), sem("c_dup"), sem("stored"), sem("kv_out"), sem("gains"))
        block = ctx.enter_context(nc.Block())

        @block.sync
        def _(sp):
            for k in range(KD):
                sp.dma_start(w[:, k, :], A["e_w_in"][0, k * P:(k + 1) * P, 3 * HW:]).then_inc(w_in[k], 16)
            sp.dma_start(cos[:, :, :, :].rearrange("p t a f -> p t (a f)"), A["k_cos"]).then_inc(loaded, 16)
            sp.dma_start(sin[:, :, :, :].rearrange("p t a f -> p t (a f)"), A["k_sin"]).then_inc(loaded, 16)
            sp.dma_start(gain[:, 0, :], A["q_norm_g"].broadcast_to([P, HD])).then_inc(loaded, 16)
            sp.dma_start(gain[:, 1, :], A["k_norm_g"].broadcast_to([P, HD])).then_inc(loaded, 16)
            sp.dma_start(ck[:, :, :, :], A["cache_k"][0, 0].rearrange("(t p) g d -> p t g d", p=P)).then_inc(loaded, 16)
            sp.dma_start(v[:, CT:CT + PAST // P, :], A["cache_v"][0, 0].rearrange("(t p) g d -> p t (g d)", p=P)).then_inc(loaded, 16)
            for t in range(CT):
                sp.wait_ge(r_ready, t + 1)
                sp.dma_start(out_k[t * P:(t + 1) * P], z[:, t % 2, QW:]).then_inc(k_stored[t], 16)
                sp.wait_ge(kv_out, t + 1)
                sp.dma_start(out_v[t * P:(t + 1) * P], v[:, t, :]).then_inc(stored, 16)
            sp.wait_ge(stored, 16 * CT)
            for t in range(CT):
                sp.wait_ge(k_stored[t], 16)
            sp.wait_ge(loaded, 6 * 16)

        @block.tensor
        def _(pe):
            def transposes(n, src_q, src_k):
                if n >= 2:
                    pe.wait_ge(tr_used, n - 1)
                if src_q is not None:
                    for pr in range(4):
                        nc.tensor.transpose(ptq[n % 2][:, pr * P:(pr + 1) * P], src_q[:, pr * P:(pr + 1) * P], S["ident"][:, :])
                for g in range(NKV):
                    m = nc.tensor.transpose(ptk[n % 2][:, g * P:(g + 1) * P],
                                            src_k[:, g, :, :].rearrange("p a d -> p (a d)"), S["ident"][:, :])
                m.then_inc(tr, 1)

            for t in range(NT + 1):
                if t < NT:
                    if t >= 2:
                        pe.wait_ge(z_out, t - 1)
                        pe.wait_ge(kv_out, t - 1)
                    for k in range(KD):
                        if t == 0:
                            pe.wait_ge(w_in[k], 16)
                        st = dict(start=(k == 0), stop=(k == KD - 1))
                        x = hnT[:, k, t * P:(t + 1) * P]
                        nc.tensor.matmul(psq[t % 2][:, :], x, w[:, k, 0:QW], **st)
                        m = nc.tensor.matmul(pskv[t % 2][:, 0:2 * KW], x, w[:, k, QW:], **st)
                    m.then_inc(mm, 1)
                if t == 1:
                    pe.wait_ge(c_dup, 1)
                    for i in range(PAST // P):
                        transposes(i, None, ckd[:, i])
                if t >= 1:
                    pe.wait_ge(r_ready, t)
                    transposes(t + 1, z[:, (t - 1) % 2, 0:QW], kd[:, (t - 1) % 2])

        @block.scalar
        def _(act):
            def copies(n, t):
                act.wait_ge(tr, n + 1)
                if t >= 0:
                    nc.scalar.activation(qT[:, :, t * P:(t + 1) * P], ptq[n % 2][:, :].rearrange("p (a c) -> p a c", c=P), ACT.Copy)
                kt = key_tile(t) if t >= 0 else CT + n
                nc.scalar.activation(kT[:, :, kt * P:(kt + 1) * P], ptk[n % 2][:, 0:NKV * P].rearrange("p (a c) -> p a c", c=P),
                                     ACT.Copy).then_inc(tr_used, 1)

            for t in range(NT + 1):
                if t < NT:
                    act.wait_ge(mm, t + 1)
                    if t >= 2:
                        act.wait_ge(tr, t + 1)
                        if t - 2 < CT:
                            act.wait_ge(k_stored[t - 2], 16)
                    nc.scalar.activation(z[:, t % 2, 0:QW], psq[t % 2][:, :], ACT.Copy).then_inc(z_out, 1)
                    nc.scalar.activation(z[:, t % 2, QW:], pskv[t % 2][:, 0:KW], ACT.Copy)
                    nc.scalar.activation(v[:, key_tile(t), :], pskv[t % 2][:, KW:2 * KW], ACT.Copy).then_inc(kv_out, 1)
                    act.wait_ge(kv_out, t + 1)
                    if t >= 2:
                        act.wait_ge(inv, t - 1)
                    nc.scalar.activation(sq[:, t % 2, :], z[:, t % 2, :], ACT.Square).then_inc(z_sq, 1)
                    act.wait_ge(inv, t + 1)
                    nc.scalar.activation(ss[:, t, :], ss[:, t, :], ACT.Sqrt).then_inc(root, 1)
                if t == 1:
                    copies(0, -1)
                    copies(1, -1)
                if t >= 1:
                    copies(t + 1, t - 1)

        @block.vector
        def _(dve):
            steps = Count(v_steps)
            dve.wait_ge(loaded, 6 * 16)
            steps.link(dve, nc.vector.tensor_scalar(gain[:, 0, :], gain[:, 0, :], HD ** -0.5, None, ALU.mult))
            for i in range(PAST // P):
                r = nc.vector.tensor_copy(ckd[:, i, :, :, :], ck[:, i, :, :].rearrange("p g (a d) -> p g a d", a=1).broadcast_to([P, NKV, 2, HD]))
            r.then_inc(c_dup, 1)
            for t in range(NT):
                zt = z[:, t % 2, :]
                heads = zt.rearrange("p (h d) -> p h d", d=HD)
                s = ss[:, t, :]
                dve.wait_ge(z_sq, t + 1)
                steps.link(dve, nc.vector.reduce_sum(s, sq[:, t % 2, :].rearrange("p (h d) -> p h d", d=HD), AX_X))
                steps.link(dve, nc.vector.tensor_scalar(s, s, 1.0 / HD, EPS, ALU.mult, ALU.add))
                nc.vector.reciprocal(s, s).then_inc(inv, 1)
                dve.wait_ge(root, t + 1)
                steps.link(dve, nc.vector.tensor_tensor(
                    heads, heads, s.rearrange("p (h a) -> p h a", a=1).broadcast_to([P, NHQ, HD]), ALU.mult))
                for h0, hn, j in ((0, NH, 0), (NH, NKV, 1)):
                    r = nc.vector.tensor_tensor(heads[:, h0:h0 + hn, :], heads[:, h0:h0 + hn, :],
                                                gain[:, j:j + 1, :].broadcast_to([P, hn, HD]), ALU.mult)
                steps.link(dve, r)
                if t >= CT:
                    def half(x, h):
                        return x[:, :, :, h, :]
                    x5 = zt.rearrange("p (h a b f) -> p h a b f", a=2, b=2, f=16)
                    c4 = cos[:, t - CT:t - CT + 1, :, :].broadcast_to([P, NHQ, 2, 16])
                    s4 = sin[:, t - CT:t - CT + 1, :, :].broadcast_to([P, NHQ, 2, 16])
                    for h in range(2):
                        nc.vector.tensor_tensor(half(ra, h), half(x5, h), c4, ALU.mult)
                        r = nc.vector.tensor_tensor(half(rb, h), half(x5, 1 - h), s4, ALU.mult)
                    steps.link(dve, r)
                    nc.vector.tensor_tensor(half(x5, 0), half(ra, 0), half(rb, 0), ALU.subtract)
                    steps.link(dve, nc.vector.tensor_tensor(half(x5, 1), half(ra, 1), half(rb, 1), ALU.add))
                if t >= 2:
                    dve.wait_ge(tr, t + 1)
                nc.vector.tensor_copy(kd[:, t % 2, :, :, :], zt[:, QW:].rearrange("p (g a d) -> p g a d", g=NKV, a=1).broadcast_to([P, NKV, 2, HD])
                                      ).then_inc(r_ready, 1)


def attention(nc, A, S, qT, kT, v, yT):
    items = [(2 * pr + r, t, 0 if t < CT else CT, CT if t < CT else KT - CT)
             for pr in range(4) for t in range(NT) for r in range(2)]
    N = len(items)
    chunks = [[(k, min(4, nk - k)) for k in range(0, nk, 4)] for _, _, _, nk in items]
    first = [sum(len(c) for c in chunks[:i]) for i in range(N + 1)]
    KMAX = KT - CT
    with ExitStack() as ctx:
        sb, ps, sem = scope(nc, ctx, "att")
        p = sb("p", [P, 2, KMAX * P])
        pT = sb("pT", [P, 2, KMAX, P])
        nmax, total = sb("nmax", [P, N]), sb("total", [P, N])
        s_ps = ps("s_ps", [P, 3 * 512])
        t_ps = [ps(f"t_ps{i}", [P, 512]) for i in range(4)]
        o_ps = ps("o_ps", [P, 512])
        qk, maxed, exped, normed, inverted, tr, tr_out, pv, o_out = (
            sem("qk"), sem("maxed"), sem("exped"), sem("normed"), sem("inverted"), sem("tr"), sem("tr_out"), sem("pv"), sem("o_out"))
        block = ctx.enter_context(nc.Block())

        @block.tensor
        def _(pe):
            def scores(i):
                h, t, k0, nk = items[i]
                r = h % 2
                if i >= 1:
                    pe.wait_ge(exped, i)
                for c in range(0, nk * P, 512):
                    n = min(512, nk * P - c)
                    m = nc.tensor.matmul(s_ps[:, c:c + n], qT[64 * r:64 * r + HD, h // 2, t * P:(t + 1) * P],
                                         kT[64 * r:64 * r + HD, h // 4, k0 * P + c:k0 * P + c + n], start=True, stop=True)
                m.then_inc(qk, 1)

            scores(0)
            for i in range(N):
                h, t, k0, nk = items[i]
                r = h % 2
                if i + 1 < N:
                    scores(i + 1)
                pe.wait_ge(normed, i + 1)
                for j, (k, n) in enumerate(chunks[i]):
                    c = first[i] + j
                    if c >= 4:
                        pe.wait_ge(tr_out, c - 3)
                    for a in range(n):
                        m = nc.tensor.transpose(t_ps[c % 4][:, a * P:(a + 1) * P], p[:, i % 2, (k + a) * P:(k + a + 1) * P],
                                                S["ident"][:, :])
                    m.then_inc(tr, 1)
                if i >= 2:
                    pe.wait_ge(o_out, i - 1)
                for j, (k, n) in enumerate(chunks[i]):
                    pe.wait_ge(tr_out, first[i] + j + 1)
                    for a in range(k, k + n):
                        m = nc.tensor.matmul(o_ps[64 * r:64 * r + HD, 0:P], v[:, k0 + a, (h // 4) * HD:(h // 4 + 1) * HD],
                                             pT[:, i % 2, a, :], start=(a == 0), stop=(a == nk - 1))
                m.then_inc(pv, 1)

        @block.scalar
        def _(act):
            def exps(i):
                h, t, k0, nk = items[i]
                act.wait_ge(maxed, i + 1)
                if i >= 2:
                    act.wait_ge(tr, first[i - 1])
                nc.scalar.activation(p[:, i % 2, 0:nk * P], s_ps[:, 0:nk * P], ACT.Exp, bias=nmax[:, i:i + 1],
                                     accum_out=total[:, i:i + 1]).then_inc(exped, 1)

            exps(0)
            for i in range(N):
                if i >= 2:
                    act.wait_ge(pv, i - 1)
                for j, (k, n) in enumerate(chunks[i]):
                    c = first[i] + j
                    act.wait_ge(tr, c + 1)
                    nc.scalar.activation(pT[:, i % 2, k:k + n, :].rearrange("p a c -> p (a c)"), t_ps[c % 4][:, 0:n * P],
                                         ACT.Copy).then_inc(tr_out, 1)
                if i + 1 < N:
                    exps(i + 1)

        @block.vector
        def _(dve):
            def softmax(i):
                h, t, k0, nk = items[i]
                dve.wait_ge(qk, i + 1)
                nc.vector.tensor_reduce(nmax[:, i:i + 1], s_ps[:, 0:nk * P], AX_X, ALU.max, negate=True).then_inc(maxed, 1)
                dve.wait_ge(exped, i + 1)
                nc.vector.reciprocal(total[:, i:i + 1], total[:, i:i + 1]).then_inc(inverted, 1)
                dve.wait_ge(inverted, i + 1)
                nc.vector.tensor_scalar(p[:, i % 2, 0:nk * P], p[:, i % 2, 0:nk * P], total[:, i:i + 1], None, ALU.mult).then_inc(normed, 1)

            softmax(0)
            for i in range(N):
                h, t, k0, nk = items[i]
                r = h % 2
                if i + 1 < N:
                    softmax(i + 1)
                dve.wait_ge(pv, i + 1)
                nc.vector.tensor_copy(yT[64 * r:64 * r + HD, h // 2, t * P:(t + 1) * P], o_ps[64 * r:64 * r + HD, 0:P]).then_inc(o_out, 1)


def out_proj(nc, A, S, tag, w_dram, lhs, x_in, x_out, layer, lhs_dram=None):
    with ExitStack() as ctx:
        sb, ps, sem = scope(nc, ctx, tag)
        w = sb("w", [P, KD, D])
        gate = sb("gate", [P, 2, D])
        x = sb("x", [P, 3, D])
        psm = [ps(f"psm{i}", [P, D]) for i in range(4)]
        w_in = [sem(f"w_in{k}") for k in range(KD)]
        l_in = [sem(f"l_in{k}") for k in range(KD)]
        g_in, mm, v_steps, gated = sem("g_in"), sem("mm"), sem("v"), sem("gated")
        x_ins, stored = [sem(f"x_in{i}") for i in range(3)], [sem(f"stored{i}") for i in range(3)]
        block = ctx.enter_context(nc.Block())

        @block.sync
        def _(sp):
            for k in range(KD):
                sp.dma_start(w[:, k, :], w_dram[k * P:(k + 1) * P, :]).then_inc(w_in[k], 16)
                if lhs_dram is not None:
                    sp.dma_start(lhs(k), lhs_dram[k]).then_inc(l_in[k], 16)
            for c in range(2):
                sp.dma_start(gate[:, c, :], S["mod_dram"][layer, c:c + 1, 2 * D:3 * D].broadcast_to([P, D])).then_inc(g_in, 16)
            for t in range(NT):
                if t >= 3:
                    sp.wait_ge(stored[t % 3], 16 * (t // 3))
                sp.dma_start(x[:, t % 3, :], x_in(t)).then_inc(x_ins[t % 3], 16)

        @block.tensor
        def _(pe):
            for t in range(NT):
                if t >= 4:
                    pe.wait_ge(gated, t - 3)
                for k in range(KD):
                    if t == 0:
                        pe.wait_ge(w_in[k], 16)
                        if lhs_dram is not None:
                            pe.wait_ge(l_in[k], 16)
                    for h in range(2):
                        m = nc.tensor.matmul(psm[t % 4][:, h * 512:(h + 1) * 512], lhs(k)[:, t * P:(t + 1) * P],
                                             w[:, k, h * 512:(h + 1) * 512], start=(k == 0), stop=(k == KD - 1))
                m.then_inc(mm, 1)

        @block.vector
        def _(dve):
            dve.wait_ge(g_in, 32)
            for t in range(NT):
                dve.wait_ge(mm, t + 1)
                nc.vector.tensor_tensor(psm[t % 4][:, :], psm[t % 4][:, :], gate[:, 0 if t < CT else 1, :], ALU.mult).then_inc(v_steps, 1)
                dve.wait_ge(v_steps, t + 1)
                dve.wait_ge(x_ins[t % 3], 16 * (t // 3 + 1))
                nc.vector.tensor_tensor(x[:, t % 3, :], psm[t % 4][:, :], x[:, t % 3, :], ALU.add).then_inc(gated, 1)

        @block.scalar
        def _(act):
            for t in range(NT):
                act.wait_ge(gated, t + 1)
                act.dma_start(x_out(t), x[:, t % 3, :]).then_inc(stored[t % 3], 16)
            for i in range(3):
                act.wait_ge(stored[i], 16 * len(range(i, NT, 3)))


def route(nc, A, S, tag, hnT, layer, idx, gates):
    with ExitStack() as ctx:
        sb, ps, sem = scope(nc, ctx, tag)
        w = sb("w", [P, KD, NE])
        lt = sb("lt", [P, 512])
        aff = sb("aff", [P, NT, NE])
        stat = sb("stat", [P, 2, NT])
        work = sb("work", [NE, T])
        top = sb("top", [NE, 2, max(CAP)])
        topi = sb("topi", [NE, 2, max(CAP)], U32)
        topf = sb("topf", [NE, 2, max(CAP)])
        lg = ps("lg", [P, 512])
        tok = ps("tok", [P, NT * NE])
        pa = [ps(f"pa{i}", [P, 512]) for i in range(3)]
        pt = ps("pt", [P, 4 * NE])
        w_in, mm, lt_out, tr, v_steps, subbed, exped, aff_ready, back, copied, picked, tr2 = (
            sem("w_in"), sem("mm"), sem("lt_out"), sem("tr"), sem("v"), sem("subbed"), sem("exped"), sem("aff_ready"),
            sem("back"), sem("copied"), sem("picked"), sem("tr2"))
        block = ctx.enter_context(nc.Block())

        @block.sync
        def _(sp):
            sp.dma_start(w[:, :, :], A["router_w"][layer].rearrange("(k p) e -> p k e", p=P)).then_inc(w_in, 16)

        @block.tensor
        def _(pe):
            pe.wait_ge(w_in, 16)
            for k in range(KD):
                for g, (t0, n, _) in enumerate(PIECES):
                    m = nc.tensor.matmul(lg[32 * g:32 * g + NE, 0:n * P], w[:, k, :], hnT[:, k, t0 * P:(t0 + n) * P],
                                         start=(k == 0), stop=(k == KD - 1), tile_position=(0, 32 * g))
            m.then_inc(mm, 1)
            pe.wait_ge(lt_out, 1)
            for g, (t0, n, _) in enumerate(PIECES):
                q = slice(32 * g, 32 * g + NE)
                if g:
                    pe.wait_ge(tr, g)
                for t in range(n):
                    m = nc.tensor.transpose(tok[:, (t0 + t) * NE:(t0 + t + 1) * NE], lt[q, t * P:(t + 1) * P], S["ident"][q, q])
                m.then_inc(tr, 1)
            pe.wait_ge(aff_ready, 1)
            for g, (t0, n, _) in enumerate(PIECES):
                for t in range(n):
                    m = nc.tensor.transpose(pa[g][0:NE, t * P:(t + 1) * P], aff[:, t0 + t, :], S["ident"][:, :])
            m.then_inc(back, 1)
            pe.wait_ge(picked, 1)
            for c in range(2):
                cap = CAP[c]
                nc.tensor.transpose(pt[0:cap, (2 * c) * NE:(2 * c + 1) * NE], top[:, c, 0:cap], S["ident"][0:NE, 0:NE])
                m = nc.tensor.transpose(pt[0:cap, (2 * c + 1) * NE:(2 * c + 2) * NE], topf[:, c, 0:cap], S["ident"][0:NE, 0:NE])
            m.then_inc(tr2, 1)

        @block.scalar
        def _(act):
            act.wait_ge(subbed, 1)
            nc.scalar.activation(aff[:, :, :], aff[:, :, :], ACT.Exp).then_inc(exped, 1)

        @block.vector
        def _(dve):
            steps = Count(v_steps)
            dve.wait_ge(mm, 1)
            for g, (t0, n, _) in enumerate(PIECES):
                r = nc.vector.tensor_copy(lt[32 * g:32 * g + NE, 0:n * P], lg[32 * g:32 * g + NE, 0:n * P])
            r.then_inc(lt_out, 1)
            dve.wait_ge(tr, len(PIECES))
            logits = tok[:, :].rearrange("p (t e) -> p t e", e=NE)

            def per_token(j):
                return stat[:, j, :].rearrange("p (t a) -> p t a", a=1).broadcast_to([P, NT, NE])
            steps.link(dve, nc.vector.reduce_max(stat[:, 0, :], logits, AX_X))
            nc.vector.tensor_tensor(aff[:, :, :], logits, per_token(0), ALU.subtract).then_inc(subbed, 1)
            dve.wait_ge(exped, 1)
            steps.link(dve, nc.vector.reduce_sum(stat[:, 1, :], aff[:, :, :], AX_X))
            steps.link(dve, nc.vector.reciprocal(stat[:, 1, :], stat[:, 1, :]))
            nc.vector.tensor_tensor(aff[:, :, :], aff[:, :, :], per_token(1), ALU.mult).then_inc(aff_ready, 1)
            dve.wait_ge(back, 1)
            for g, (t0, n, _) in enumerate(PIECES):
                r = nc.vector.tensor_copy(work[:, t0 * P:(t0 + n) * P], pa[g][0:NE, 0:n * P])
            steps.link(dve, r)
            for c, (o, ln) in enumerate(SEQS):
                cols = work[:, o:o + ln]
                for r8 in range(0, CAP[c], 8):
                    t8 = top[:, c, r8:r8 + 8]
                    steps.link(dve, nc.vector.max(t8, cols))
                    nc.vector.max_index(topi[:, c, r8:r8 + 8], t8, cols)
                    steps.link(dve, nc.vector.match_replace(cols, t8, cols, -1.0))
            for c, (o, ln) in enumerate(SEQS):
                steps.link(dve, nc.vector.tensor_copy(topf[:, c, 0:CAP[c]], topi[:, c, 0:CAP[c]]))
                if c == 1:
                    steps.link(dve, nc.vector.tensor_scalar(topf[:, c, 0:CAP[c]], topf[:, c, 0:CAP[c]], float(o), None, ALU.add))
            nc.vector.tensor_copy(stat[:, 0, 0:1], stat[:, 1, 0:1]).then_inc(picked, 1)
            dve.wait_ge(tr2, 1)
            for c in range(2):
                cap = CAP[c]
                nc.vector.tensor_copy(gates[c][0:cap, :], pt[0:cap, (2 * c) * NE:(2 * c + 1) * NE])
                nc.vector.tensor_copy(idx[c][0:cap, :], pt[0:cap, (2 * c + 1) * NE:(2 * c + 2) * NE])


def experts(nc, A, S, tag, layer, xn_dram, y_dram, idx, gates):
    CP, CL = CAP
    CC = CP + CL
    SW = 256
    with ExitStack() as ctx:
        sb, ps, sem = scope(nc, ctx, tag)
        w = sb("w", [P, 12, KD, SW])
        xl, xc = sb("xl", [P, D]), sb("xc", [CP, D])
        xT = sb("xT", [P, KD, CC])
        sg = sb("sg", [P, 2, CC])
        hT = sb("hT", [P, KD, CC])
        ol, oc = sb("ol", [P, D]), sb("oc", [CP, D])
        icg, ics = [sb("icg0", [CP, 1], U32), sb("icg1", [P, 1], U32)], [sb("ics0", [CP, 1], U32), sb("ics1", [P, 1], U32)]
        zero = sb("zero", [P, D])
        pgu = [ps(f"pgu{i}", [P, CC]) for i in range(4)]
        pxt = ps("pxt", [P, 2 * CC])
        pol = [ps("pol0", [P, 512]), ps("pol1", [P, 512])]
        poc = ps("poc", [P, SW])
        w_in = [sem(f"w_in{j}") for j in range(12)]
        xl_in, xc_in, gu_mm, silued, multiplied, tr, xT_out, ol_mm, oc_mm, ol_out, oc_out, l_added, c_added = (
            sem("xl_in"), sem("xc_in"), sem("gu_mm"), sem("silued"), sem("multiplied"), sem("tr"), sem("xT_out"),
            sem("ol_mm"), sem("oc_mm"), sem("ol_out"), sem("oc_out"), sem("l_added"), sem("c_added"))
        zeroed, y_zero, p_steps, o_free, issued = (
            sem("zeroed"), sem("y_zero"), sem("p_steps"), sem("o_free"), sem("issued"))
        block = ctx.enter_context(nc.Block())
        gu_w, down_w = A["moe_w_gu"][layer], A["moe_w_down"][layer]

        @block.sync
        def _(sp):
            def load(j, e):
                if j < 8:
                    jj, part = divmod(j, 2)
                    c0 = part * FH + jj * SW
                    src = gu_w[bass.ds(e, 1), :, c0:c0 + SW]
                else:
                    src = down_w[bass.ds(e, 1), :, (j - 8) * SW:(j - 7) * SW]
                sp.dma_start(w[:, j, :, :], src.rearrange("a (k p) n -> p (a k) n", p=P)).then_inc(w_in[j], 16)

            for j in range(12):
                load(j, 0)
            with sp.Fori(1, NE) as e:
                for j in range(12):
                    if j < 8 and j % 2 == 0:
                        sp.wait_ge(gu_mm, e * 16 + (4 * (j // 2) + 4 - 16))
                    if j == 8:
                        sp.wait_ge(oc_mm, e)
                    load(j, e)

        @block.gpsimd
        def _(pool):
            def gather(e, first=False):
                if not first:
                    pool.wait_ge(tr, e * 4)
                    pool.wait_ge(xl_in, e * 16)
                    pool.wait_ge(xc_in, e * 16)
                nc.gpsimd.tensor_copy(icg[0][:, :], idx[0][0:CP, bass.ds(e, 1)])
                nc.gpsimd.tensor_copy(icg[1][:, :], idx[1][:, bass.ds(e, 1)]).then_inc(p_steps, 1)
                pool.wait_ge(p_steps, 1 if first else e * 2)
                pool.sem_inc(issued, 1)
                pool.indirect_dma_start(xc[:, :], None, xn_dram, bass.IndirectOffsetOnAxis(icg[0][:, 0:1], 0)).then_inc(xc_in, 16)
                pool.indirect_dma_start(xl[:, :], None, xn_dram, bass.IndirectOffsetOnAxis(icg[1][:, 0:1], 0)).then_inc(xl_in, 16)

            def scatter(e):
                nc.gpsimd.tensor_copy(ics[0][:, :], idx[0][0:CP, bass.ds(e, 1)])
                nc.gpsimd.tensor_copy(ics[1][:, :], idx[1][:, bass.ds(e, 1)]).then_inc(p_steps, 1)
                pool.wait_ge(p_steps, e * 2 + 3 if not isinstance(e, int) or e < NE - 1 else 2 * NE)
                pool.wait_ge(ol_out, e * 2 + 4)
                pool.sem_inc(issued, 1)
                pool.indirect_dma_start(y_dram, bass.IndirectOffsetOnAxis(ics[1][:, 0:1], 0), ol[:, :], None,
                                        compute_op=ALU.add).then_inc(l_added, 16)
                pool.wait_ge(oc_out, e + 2)
                pool.sem_inc(issued, 1)
                pool.indirect_dma_start(y_dram, bass.IndirectOffsetOnAxis(ics[0][:, 0:1], 0), oc[:, :], None,
                                        compute_op=ALU.add).then_inc(c_added, 16)
                pool.wait_ge(l_added, e * 16 + 16)
                pool.wait_ge(c_added, e * 16 + 16)
                pool.sem_inc(o_free, 1)

            nc.gpsimd.memset(zero[:, :], 0.0).then_inc(zeroed, 1)
            pool.sem_inc(o_free, 1)
            gather(0, first=True)
            pool.wait_ge(y_zero, 16 * NT)
            with pool.Fori(0, NE - 1) as e:
                gather(e + 1)
                scatter(e)
            scatter(NE - 1)

        @block.tensor
        def _(pe):
            def transposes(e, g):
                for j in range(2):
                    k = 2 * g + j
                    nc.tensor.transpose(pxt[:, j * CC:j * CC + CL], xl[:, k * P:(k + 1) * P], S["ident"][:, :])
                    m = nc.tensor.transpose(pxt[:, j * CC + CL:(j + 1) * CC], xc[:, k * P:(k + 1) * P], S["ident"][0:CP, 0:CP])
                m.then_inc(tr, 1)

            def expert(e, last):
                for f in range(FH // P):
                    for part in range(2):
                        j = 2 * (f // 2) + part
                        if f % 2 == 0:
                            pe.wait_ge(w_in[j], e * 16 + 16)
                        if f == 0 and part == 0:
                            pe.wait_ge(xT_out, e * 4 + 4)
                        pe.wait_ge(multiplied if part else silued, e * 8 + (f + 1))
                        for k in range(KD):
                            m = nc.tensor.matmul(pgu[2 * (f % 2) + part][:, :], w[:, j, k, (f % 2) * P:(f % 2 + 1) * P], xT[:, k, :],
                                                 start=(k == 0), stop=(k == KD - 1))
                        m.then_inc(gu_mm, 1)
                pe.wait_ge(multiplied, e * 8 + 10)
                if not last:
                    pe.wait_ge(xl_in, e * 16 + 32)
                    pe.wait_ge(xc_in, e * 16 + 32)
                for q in range(4):
                    pe.wait_ge(w_in[8 + q], e * 16 + 16)
                    if q % 2 == 0:
                        pe.wait_ge(ol_out, e * 2 + (q // 2 + 1))
                    for k in range(KD):
                        m = nc.tensor.matmul(pol[q // 2][:, (q % 2) * SW:(q % 2 + 1) * SW], hT[:, k, 0:CL], w[:, 8 + q, k, :],
                                             start=(k == 0), stop=(k == KD - 1))
                    if q % 2:
                        m.then_inc(ol_mm, 1)
                    if not last:
                        pe.wait_ge(xT_out, e * 4 + (4 + q))
                        transposes(e + 1, q)
                pe.wait_ge(oc_out, e + 1)
                for k in range(KD):
                    for q in range(4):
                        m = nc.tensor.matmul(poc[32 * q:32 * q + CP, :], hT[:, k, CL:CC], w[:, 8 + q, k, :],
                                             start=(k == 0), stop=(k == KD - 1), tile_position=(0, 32 * q))
                m.then_inc(oc_mm, 1)

            pe.wait_ge(xl_in, 16)
            pe.wait_ge(xc_in, 16)
            for g in range(4):
                if g:
                    pe.wait_ge(xT_out, g)
                transposes(0, g)
            with pe.Fori(0, NE - 1) as e:
                expert(e, False)
            expert(NE - 1, True)

        mc = S["modcol"]

        @block.scalar
        def _(act):
            def to_xT(e, g):
                act.wait_ge(tr, e * 4 + (g + 1))
                for j in range(2):
                    k = 2 * g + j
                    for c, c0, n in ((1, 0, CL), (0, CL, CP)):
                        r = nc.scalar.activation(xT[:, k, c0:c0 + n], pxt[:, j * CC + c0:j * CC + c0 + n], ACT.Identity,
                                                 bias=mc[:, layer, 3, c, k:k + 1], scale=mc[:, layer, 4, c, k:k + 1])
                r.then_inc(xT_out, 1)

            def expert(e, last):
                for f in range(FH // P):
                    act.wait_ge(multiplied, e * 8 + (f + 1))
                    act.wait_ge(gu_mm, e * 16 + (2 * f + 1))
                    nc.scalar.activation(sg[:, f % 2, :], pgu[2 * (f % 2)][:, :], ACT.Silu).then_inc(silued, 1)
                if not last:
                    for g in range(4):
                        to_xT(e + 1, g)

            act.sem_inc(silued, 2)
            act.wait_ge(zeroed, 1)
            for t in range(NT):
                act.dma_start(y_dram[t * P:(t + 1) * P, :], zero[:, :]).then_inc(y_zero, 16)
            for g in range(4):
                to_xT(0, g)
            with act.Fori(0, NE - 1) as e:
                expert(e, False)
            expert(NE - 1, True)

        @block.vector
        def _(dve):
            dve.sem_inc(multiplied, 2)
            dve.sem_inc(ol_out, 2)
            dve.sem_inc(oc_out, 1)
            with dve.Fori(0, NE) as e:
                for f in range(FH // P):
                    dve.wait_ge(silued, e * 8 + (f + 3))
                    dve.wait_ge(gu_mm, e * 16 + (2 * f + 2))
                    nc.vector.tensor_tensor(hT[:, f, :], sg[:, f % 2, :], pgu[2 * (f % 2) + 1][:, :], ALU.mult).then_inc(multiplied, 1)
                dve.wait_ge(o_free, e + 1)
                for b in range(2):
                    dve.wait_ge(ol_mm, e * 2 + (b + 1))
                    nc.vector.tensor_scalar(ol[:, b * 512:(b + 1) * 512], pol[b][:, :], gates[1][:, bass.ds(e, 1)], None,
                                            ALU.mult).then_inc(ol_out, 1)
                dve.wait_ge(oc_mm, e + 1)
                for q in range(4):
                    r = nc.vector.tensor_scalar(oc[:, q * SW:(q + 1) * SW], poc[32 * q:32 * q + CP, :], gates[0][0:CP, bass.ds(e, 1)], None,
                                                ALU.mult)
                r.then_inc(oc_out, 1)


LEVELS = (64, 32, 16, 8)
FLOOR = -20.0
SIG_FLOOR = -40.0
RT = RH * RD
L64, INTER, L32, L16, L8, DQ, DK = range(7)
ITEM_LEVEL = {L64: 64, L32: 32, L16: 16, L8: 8}
ITEM_BUF = {L64: 2, INTER: 3, L32: 4, L16: 0, L8: 1, DQ: 2, DK: 3}
USES = [(d, i) for d in range(2) for i in (L64, L32, INTER, L16, L8, DK)] + ["o", "yT"]
NU = len(USES)
BANKS = [(0, 4), (4, 4), (8, 2)]
PARTS = ("q", "f0", "f1")
NP_STEPS = 9 + NT


def rec_order():
    def direction(d, ps):
        o = [("prep", d)]
        o += [("p", n) for n in ps[0:3]]
        o += [("pre", d, L64), ("pre", d, INTER), ("post", d, L64), ("prod", d, L64), ("pre", d, L32), ("post", d, INTER),
              ("kt", d), ("p", ps[3]), ("pre", d, L16), ("post", d, L32), ("fin", d, L64), ("prod", d, L32), ("pre", d, L8),
              ("p", ps[4]), ("post", d, L16), ("fin", d, L32), ("prod", d, INTER), ("pre", d, DQ), ("p", ps[5]),
              ("post", d, L8), ("pre", d, DK), ("fin", d, INTER), ("prod", d, L16), ("post", d, DQ), ("post", d, DK),
              ("p", ps[6]), ("fin", d, L16), ("prod", d, L8), ("p", ps[7]), ("fin", d, L8), ("prod", d, DK)]
        return o
    o = [("qprep",)] + direction(0, list(range(0, 8))) + direction(1, list(range(8, 16)))
    o.insert(o.index(("prep", 1)), ("fin", 0, DK))
    return o + [("fin", 1, DK), ("p", 16), ("gate",), ("prod_o",), ("fin_o",), ("p", 17), ("norm",), ("p", 18), ("prod_y",), ("fin_y",)]


def recurrence(nc, A, S, hnT, y_dram, out_state):
    with ExitStack() as ctx:
        sb, ps, sem = scope(nc, ctx, "rec")
        U8 = mybir.dt.uint8
        w = sb("w", [P, KD, 5, RD])
        zc = sb("zc", [P, 2, 3, T])
        zv = sb("zv", [P, 2, NT, RD])
        zg = sb("zg", [P, 2, NT, RD])
        kk = sb("kk", [P, T])
        X, X8 = sb("X", [P, T]), sb("X8", [P, T])
        ring = sb("ring", [P, 5, T])
        Qi = sb("Qi", [P, 2, T])
        St = sb("St", [P, 2, NT, RD])
        kT = sb("kT", [P, NT, RD])
        AT = sb("AT", [P, NT, P])
        dtmp = sb("dtmp", [P, 4, P])
        y = sb("y", [P, NT, RD])
        fin = sb("fin", [P, 2, RD])
        s0 = sb("s0", [P, 2, 2, RD])
        tot, etot, tot8 = sb("tot", [P, NT, 2]), sb("etot", [P, NT, 2]), sb("tot8", [P, NT, 2])
        decay = sb("decay", [P, NT])
        ms = sb("ms", [P, NT])
        restart = sb("restart", [P, T], U8)
        maskb = sb("maskb", [P, 8, P], U8)
        maskf = sb("maskf", [P, 2, P])
        lb = sb("lb", [P, 2, RH])
        oml = sb("oml", [P, 2, RH])
        lbt = sb("lbt", [P, 2, RH])
        pz = [ps(f"pz{i}", [P, 512]) for i in range(3)]
        pk = [ps(f"pk{i}", [P, 512]) for i in range(2)]
        pg = [ps(f"pg{i}", [P, 512]) for i in range(3)]
        w_in, s0_in, consts, fin_out, y_out = (
            [sem(f"w_in{j}") for j in range(5)], [sem("s0_in0"), sem("s0_in1")], sem("consts"), sem("fin_out"), sem("y_out"))
        (z_mm, z_out, v_steps, lb_e, lb_d, q_clamped, q_sig, zc_clamped, lse, s_ready, k_exp, f_exp, f_ready, log_f, x_ready,
         tot_e, pre, exped, post, k_tr, kT_out, g_full, g_free, g_clamped, g_sig, o_out, o_sq, ms_ready, rstd, y_ready,
         yT_ready, fin_ready) = (sem(n) for n in (
             "z_mm z_out v lb_e lb_d q_clamped q_sig zc_clamped lse s_ready k_exp f_exp f_ready log_f x_ready tot_e pre exped "
             "post k_tr kT_out g_full g_free g_clamped g_sig o_out o_sq ms_ready rstd y_ready yT_ready fin_ready").split())
        a_steps = sem("a")
        block = ctx.enter_context(nc.Block())
        ORDER = rec_order()

        def blocks(x, h):
            return x.rearrange("p (b s h) -> p b s h", s=2, h=h)

        def qhalf(d):
            return 1 - d

        def reference(x, d, h):
            b = blocks(x, h)
            return b[:, :, d, h - 1:h] if d == 0 else b[:, :, d, 0:1]

        def totals(x, d):
            b = blocks(x, 64)
            return b[:, :, :, 63] if d == 0 else b[:, :, :, 0]

        def use(h, key):
            return NU * h + USES.index(key)

        steps_of_head = lambda h: ([t for t in ORDER if h + 1 < RH or t[0] != "p"])

        def store(sp, h):
            for d in range(2):
                sp.wait_ge(fin_ready, 2 * h + d + 1)
                sp.dma_start(out_state[d, h], fin[:, d, :]).then_inc(fin_out, 16)
            sp.wait_ge(yT_ready, 3 * (h + 1))
            sp.dma_start(y_dram[h], X8[:, :]).then_inc(y_out, 16)

        @block.sync
        def _(sp):
            sp.dma_start(ring[:, 0, 0:8 * P], A["k_maskb"].rearrange("p m c -> p (m c)")).then_inc(consts, 16)
            sp.dma_start(maskf[:, :, :], A["k_maskf"]).then_inc(consts, 16)
            for h in range(RH):
                for j, part in enumerate((0, 2, 3, 1, 4)):
                    if h:
                        sp.wait_ge(z_mm, NP_STEPS * (h - 1) + (3 * (j + 1) if j < 3 else NP_STEPS))
                    sp.dma_start(w[:, :, j, :], A["r_w_in"][0, :, part * D + h * RD:part * D + (h + 1) * RD]
                                 .rearrange("(k p) n -> p k n", p=P)).then_inc(w_in[j], 16)
                if h >= 2:
                    sp.wait_ge(g_free, 3 * use(h - 2, (1, INTER)) + 3)
                sp.dma_start(s0[:, h % 2, :, :], A["state_rec"][0, 0, :, h].rearrange("s d e -> d s e")).then_inc(s0_in[h % 2], 16)
                if h:
                    store(sp, h - 1)
            store(sp, RH - 1)
            sp.wait_ge(fin_out, 32 * RH)
            sp.wait_ge(y_out, 16 * RH)

        @block.tensor
        def _(pe):
            def project(h, n):
                i = NP_STEPS * h + n
                if n in (0, 3, 6):
                    pe.wait_ge(w_in[n // 3], 16 * (h + 1))
                if n == 9:
                    pe.wait_ge(w_in[3], 16 * (h + 1))
                    pe.wait_ge(w_in[4], 16 * (h + 1))
                if i >= 3:
                    pe.wait_ge(z_out, i - 2)
                for k in range(KD):
                    if n < 9:
                        t0, nt, _ = PIECES[n % 3]
                        m = nc.tensor.matmul(pz[i % 3][:, 0:nt * P], w[:, k, n // 3, :], hnT[:, k, t0 * P:(t0 + nt) * P],
                                             start=(k == 0), stop=(k == KD - 1))
                    else:
                        t = n - 9
                        m = nc.tensor.matmul(pz[i % 3][:, 0:2 * RD], hnT[:, k, t * P:(t + 1) * P],
                                             w[:, k, 3:5, :].rearrange("p a c -> p (a c)"), start=(k == 0), stop=(k == KD - 1))
                m.then_inc(z_mm, 1)

            def into_banks(h, key, mm):
                u = use(h, key)
                for b, (t0, nt) in enumerate(BANKS):
                    if u:
                        pe.wait_ge(g_free, 3 * (u - 1) + b + 1)
                    for t in range(t0, t0 + nt):
                        m = mm(pg[b][:, (t - t0) * P:(t - t0 + 1) * P], t)
                    m.then_inc(g_full, 1)

            def step(h, tok):
                kind = tok[0]
                if kind == "p":
                    project(h + 1, tok[1])
                elif kind == "prod" and tok[2] == INTER:
                    d = tok[1]
                    pe.wait_ge(kT_out, 3 * (2 * h + d + 1))
                    into_banks(h, (d, INTER), lambda o, t: nc.tensor.matmul(o, kT[:, t, :], zv[:, h % 2, t, :], start=True, stop=True))
                elif kind == "prod":
                    d, i = tok[1:]
                    pe.wait_ge(post, 7 * (2 * h + d) + i + 1)
                    kb, qb = ring[:, ITEM_BUF[i], :], ring[:, ITEM_BUF[DQ if i == DK else i], :]
                    into_banks(h, (d, i), lambda o, t: nc.tensor.matmul(o, kb[:, t * P:(t + 1) * P], qb[:, t * P:(t + 1) * P],
                                                                       start=True, stop=True))
                elif kind == "kt":
                    d = tok[1]
                    n = 3 * (2 * h + d)
                    pe.wait_ge(post, 7 * (2 * h + d) + INTER + 1)
                    for b, (t0, nt) in enumerate(BANKS):
                        if n + b >= 2:
                            pe.wait_ge(kT_out, n + b - 1)
                        for t in range(t0, t0 + nt):
                            m = nc.tensor.transpose(pk[(n + b) % 2][:, (t - t0) * P:(t - t0 + 1) * P],
                                                    ring[:, ITEM_BUF[INTER], t * P:(t + 1) * P], S["ident"][:, :])
                        m.then_inc(k_tr, 1)
                elif kind == "prod_o":
                    pe.wait_ge(g_free, 3 * use(h, (1, DK)) + 3)

                    def mm(o, t):
                        nc.tensor.matmul(o, AT[:, t, :], zv[:, h % 2, t, :], start=True, stop=False)
                        nc.tensor.matmul(o, Qi[:, 0, t * P:(t + 1) * P], St[:, 0, t, :], start=False, stop=False)
                        return nc.tensor.matmul(o, Qi[:, 1, t * P:(t + 1) * P], St[:, 1, t, :], start=False, stop=True)
                    into_banks(h, "o", mm)
                elif kind == "prod_y":
                    pe.wait_ge(y_ready, h + 1)
                    into_banks(h, "yT", lambda o, t: nc.tensor.transpose(o, y[:, t, :], S["ident"][:, :]))

            for n in range(NP_STEPS):
                project(0, n)
            for h in range(RH):
                for tok in steps_of_head(h):
                    step(h, tok)

        @block.scalar
        def _(act):
            chain = Count(a_steps)

            def z_copy(h, n):
                i = NP_STEPS * h + n
                act.wait_ge(z_mm, i + 1)
                if n == 0 and h >= 2:
                    act.wait_ge(post, 14 * (h - 1))
                    act.wait_ge(g_full, 3 * use(h - 2, "o") + 3)
                    act.wait_ge(y_ready, h - 1)
                if n < 9:
                    t0, nt, _ = PIECES[n % 3]
                    nc.scalar.activation(zc[:, h % 2, n // 3, t0 * P:(t0 + nt) * P], pz[i % 3][:, 0:nt * P], ACT.Copy).then_inc(z_out, 1)
                else:
                    chain.link(act, nc.scalar.activation(zv[:, h % 2, n - 9, :], pz[i % 3][:, 0:RD], ACT.Copy))
                    nc.scalar.activation(zg[:, h % 2, n - 9, :], pz[i % 3][:, RD:2 * RD], ACT.Copy).then_inc(z_out, 1)

            def sigmoid(x, done):
                chain.link(act, nc.scalar.activation(x, x, ACT.Exp, scale=-1.0))
                chain.link(act, nc.scalar.activation(x, x, ACT.Ln, bias=1.0))
                nc.scalar.activation(x, x, ACT.Exp, scale=-1.0).then_inc(done, 1)

            def step(h, tok):
                kind = tok[0]
                n2 = 2 * h + (tok[1] if len(tok) > 1 else 0)
                if kind == "p":
                    z_copy(h + 1, tok[1])
                elif kind == "qprep":
                    act.wait_ge(q_clamped, h + 1)
                    sigmoid(ring[:, 0, :], q_sig)
                elif kind == "prep":
                    d = tok[1]
                    z = zc[:, h % 2, 1 + d, :]
                    r0, r1 = ring[:, 0, :], ring[:, 1, :]
                    act.wait_ge(zc_clamped, n2 + 1)
                    chain.link(act, nc.scalar.activation(r0, z, ACT.Exp, scale=-1.0))
                    nc.scalar.activation(r0, r0, ACT.Ln, bias=1.0).then_inc(lse, 1)
                    act.wait_ge(s_ready, n2 + 1)
                    act.wait_ge(lse, n2 + 1)
                    nc.scalar.activation(z, r0, ACT.Exp, scale=-1.0).then_inc(f_exp, 1)
                    nc.scalar.activation(kk[:, :], r1, ACT.Exp, scale=-1.0).then_inc(k_exp, 1)
                    act.wait_ge(f_ready, n2 + 1)
                    nc.scalar.activation(z, z, ACT.Ln).then_inc(log_f, 1)
                    act.wait_ge(x_ready, n2 + 1)
                    nc.scalar.activation(etot[:, :, :], tot[:, :, :], ACT.Exp).then_inc(tot_e, 1)
                elif kind == "pre":
                    d, i = tok[1:]
                    act.wait_ge(pre, 7 * n2 + i + 1)
                    r = ring[:, ITEM_BUF[i], :]
                    nc.scalar.activation(r, r, ACT.Exp).then_inc(exped, 1)
                elif kind == "kt":
                    for b, (t0, nt) in enumerate(BANKS):
                        n = 3 * n2 + b
                        act.wait_ge(k_tr, n + 1)
                        if n2 and b == 0:
                            act.wait_ge(g_full, 3 * use((n2 - 1) // 2, ((n2 - 1) % 2, INTER)) + 3)
                        nc.scalar.activation(kT[:, t0:t0 + nt, :].rearrange("p t c -> p (t c)"), pk[n % 2][:, 0:nt * P],
                                             ACT.Copy).then_inc(kT_out, 1)
                elif kind == "gate":
                    act.wait_ge(g_clamped, h + 1)
                    sigmoid(ring[:, 0, :], g_sig)
                elif kind == "norm":
                    act.wait_ge(o_out, h + 1)
                    nc.scalar.activation(ring[:, 1, :], y[:, :, :].rearrange("p t e -> p (t e)"), ACT.Square).then_inc(o_sq, 1)
                    act.wait_ge(ms_ready, h + 1)
                    chain.link(act, nc.scalar.activation(ms[:, :], ms[:, :], ACT.Ln))
                    nc.scalar.activation(ms[:, :], ms[:, :], ACT.Exp, scale=-0.5).then_inc(rstd, 1)

            act.wait_ge(lb_d, 1)
            nc.scalar.activation(lbt[:, :, :], lbt[:, :, :], ACT.Exp).then_inc(lb_e, 1)
            for n in range(NP_STEPS):
                z_copy(0, n)
            for h in range(RH):
                for tok in steps_of_head(h):
                    step(h, tok)

        @block.vector
        def _(dve):
            steps = Count(v_steps)
            TT, TS, STT = nc.vector.tensor_tensor, nc.vector.tensor_scalar, nc.vector.scalar_tensor_tensor

            def wide(x, n):
                return x.broadcast_to([P, x.shape[1], n])

            def take(h, key, b):
                dve.wait_ge(g_full, 3 * use(h, key) + b + 1)

            def states(h, d):
                take(h, (d, INTER), 2)
                dve.wait_ge(s0_in[h % 2], 16 * (h // 2 + 1))
                if h and d == 0:
                    dve.wait_ge(g_full, 3 * use(h - 1, "o") + 3)
                for o, ln in SEQS:
                    tiles = list(range(o // P, (o + ln) // P))
                    if d:
                        tiles.reverse()
                    if o == 0:
                        r = nc.vector.memset(St[:, d, tiles[0], :], 0.0)
                    else:
                        r = nc.vector.tensor_copy(St[:, d, tiles[0], :], s0[:, h % 2, d, :])
                    steps.link(dve, r)
                    for j, t in enumerate(tiles):
                        if j + 1 < len(tiles):
                            dst = St[:, d, tiles[j + 1], :]
                        elif o == 0:
                            dst = fin[:, d, :]
                            if h:
                                dve.wait_ge(fin_out, 32 * h)
                        else:
                            break
                        b = t // 4
                        r = STT(dst, St[:, d, t, :], decay[:, t:t + 1], pg[b][:, (t - 4 * b) * P:(t - 4 * b + 1) * P], ALU.mult, ALU.add)
                        if j + 1 < len(tiles):
                            steps.link(dve, r)
                        else:
                            r.then_inc(fin_ready, 1)
                steps.link(dve, TS(tot8[:, 0, :], tot8[:, 0, :], 1.0, None, ALU.mult))
                nc.vector.tensor_copy(tot8[:, 1, :], tot8[:, 0, :]).then_inc(g_free, 3)

            def step(h, tok):
                kind = tok[0]
                if kind == "p":
                    return
                d = tok[1] if len(tok) > 1 else 0
                n2 = 2 * h + d
                q = zc[:, h % 2, 0, :]
                k = kk[:, :]
                z = zc[:, h % 2, 1 + d, :]
                r0, r1 = ring[:, 0, :], ring[:, 1, :]
                qh, kh = qhalf(d), d
                if kind == "qprep":
                    dve.wait_ge(z_out, NP_STEPS * (h + 1))
                    TS(r0, q, SIG_FLOOR, None, ALU.max).then_inc(q_clamped, 1)
                elif kind == "prep":
                    if d == 0:
                        dve.wait_ge(q_sig, h + 1)
                        steps.link(dve, TT(q, q, r0, ALU.mult))
                    if d == 1:
                        dve.wait_ge(g_full, 3 * use(h, (0, L8)) + 3)
                    TS(z, z, SIG_FLOOR, None, ALU.max).then_inc(zc_clamped, 1)
                    dve.wait_ge(lse, n2 + 1)
                    TT(r1, z, r0, ALU.add).then_inc(s_ready, 1)
                    dve.wait_ge(f_exp, n2 + 1)
                    TS(z, z, oml[:, d, h:h + 1], lb[:, d, h:h + 1], ALU.mult, ALU.add).then_inc(f_ready, 1)
                    dve.wait_ge(k_exp, n2 + 1)
                    steps.link(dve, TS(k, k, oml[:, d, h:h + 1], None, ALU.mult))
                    dve.wait_ge(log_f, n2 + 1)
                    if h and d == 0:
                        dve.wait_ge(y_out, 16 * h)
                    steps.give(TS(r0, z, FLOOR, None, ALU.max))
                    nc.vector.tensor_tensor_scan(X[:, :], restart[:, :], z, 0.0, ALU.mult, ALU.add).then_inc(v_steps, 1)
                    steps.n += 1
                    steps.wait(dve)
                    steps.link(dve, nc.vector.tensor_tensor_scan(X8[:, :], restart[:, :], r0, 0.0, ALU.mult, ALU.add))
                    if d == 1:
                        for x, g, tt in ((X[:, :], z, tot), (X8[:, :], r0, tot8)):
                            steps.link(dve, nc.vector.tensor_copy(tt[:, :, :], totals(x, 0)))
                            steps.link(dve, STT(x, x, -1.0, g, ALU.mult, ALU.add))
                            xv = x.rearrange("p (b h) -> p b h", h=64)
                            steps.link(dve, TT(xv, xv, wide(tt[:, :, :].rearrange("p t (s a) -> p (t s) a", a=1), 64), ALU.add))
                    nc.vector.tensor_copy(tot[:, :, :], totals(X[:, :], d)).then_inc(x_ready, 1)
                    dve.wait_ge(tot_e, n2 + 1)
                    steps.link(dve, TT(decay[:, :], etot[:, :, 0], etot[:, :, 1], ALU.mult))
                elif kind == "pre":
                    i = tok[2]
                    r = ring[:, ITEM_BUF[i], :]
                    if i == L64 and n2:
                        dve.wait_ge(g_full, 3 * use((n2 - 1) // 2, ((n2 - 1) % 2, DK)) + 3)
                    if i == L32 and n2:
                        dve.wait_ge(g_full, 3 * use((n2 - 1) // 2, ((n2 - 1) % 2, L32)) + 3)
                    if i == DQ:
                        dve.wait_ge(g_full, 3 * use(h, (d, L64)) + 3)
                    if i == DK:
                        dve.wait_ge(k_tr, 3 * (n2 + 1))
                    if i in (DQ, DK):
                        b8 = X8[:, :].rearrange("p (b h) -> p b h", h=8)
                        m = 3 + d
                        ref = wide(b8[:, :, m:m + 1], 8)
                        rb = r.rearrange("p (b h) -> p b h", h=8)
                        last = TT(rb, b8, ref, ALU.subtract) if i == DQ else TT(rb, ref, b8, ALU.subtract)
                    else:
                        hh = 64 if i == INTER else ITEM_LEVEL[i]
                        xb, rb = blocks(X[:, :], hh), blocks(r, hh)
                        ref = wide(reference(X[:, :], d, hh), hh)
                        if i == INTER:
                            own = xb[:, :, qh, 63:64] if d == 0 else xb[:, :, qh, 0:1]
                            nc.vector.tensor_copy(rb[:, :, kh, :], xb[:, :, kh, :])
                            last = TT(rb[:, :, qh, :], wide(own, 64), xb[:, :, qh, :], ALU.subtract)
                        else:
                            if i == L64:
                                nc.vector.tensor_copy(rb[:, :, qh, :], xb[:, :, qh, :])
                            else:
                                TT(rb[:, :, qh, :], xb[:, :, qh, :], ref, ALU.subtract)
                            last = TT(rb[:, :, kh, :], ref, xb[:, :, kh, :], ALU.subtract)
                    last.then_inc(pre, 1)
                elif kind == "post":
                    i = tok[2]
                    r = ring[:, ITEM_BUF[i], :]
                    dve.wait_ge(exped, 7 * n2 + i + 1)
                    if i in (DQ, DK):
                        last = TT(r, r, q if i == DQ else k, ALU.mult)
                    elif i == INTER:
                        if h and d == 0:
                            dve.wait_ge(g_full, 3 * use(h - 1, "o") + 3)
                        rb, qb, kb, w64, qi = (blocks(a, 64) for a in (r, q, k, ring[:, ITEM_BUF[L64], :], Qi[:, d, :]))
                        e = etot[:, :, :]
                        dve.wait_ge(post, 7 * n2 + L64 + 1)
                        steps.give(TT(qi[:, :, kh, :], qb[:, :, kh, :], rb[:, :, kh, :], ALU.mult))
                        steps.give(TT(qi[:, :, qh, :], w64[:, :, qh, :], wide(e[:, :, kh:kh + 1], 64), ALU.mult))
                        steps.wait(dve)
                        TT(rb[:, :, qh, :], kb[:, :, qh, :], rb[:, :, qh, :], ALU.mult)
                        last = TT(rb[:, :, kh, :], w64[:, :, kh, :], wide(e[:, :, qh:qh + 1], 64), ALU.mult)
                    else:
                        hh = ITEM_LEVEL[i]
                        rb, qb, kb = (blocks(a, hh) for a in (r, q, k))
                        TT(rb[:, :, qh, :], rb[:, :, qh, :], qb[:, :, qh, :], ALU.mult)
                        last = TT(rb[:, :, kh, :], rb[:, :, kh, :], kb[:, :, kh, :], ALU.mult)
                    last.then_inc(post, 1)
                elif kind == "fin" and tok[2] == INTER:
                    states(h, d)
                elif kind == "fin":
                    i = tok[2]
                    if d == 0 and i == L64 and h:
                        dve.wait_ge(g_full, 3 * use(h - 1, "o") + 3)
                    for b, (t0, nt) in enumerate(BANKS):
                        take(h, (d, i), b)
                        src = pg[b][:, 0:nt * P].rearrange("p (t c) -> p t c", c=P)
                        at = AT[:, t0:t0 + nt, :]
                        if d == 0 and i == L64:
                            last = TT(at, src, maskf[:, 0:1, :].broadcast_to([P, nt, P]), ALU.mult)
                        elif d == 1 and i == DK:
                            if b:
                                dve.wait_ge(g_free, 3 * use(h, (d, i)) + b)
                            steps.link(dve, TT(dtmp[:, 0:nt, :], src, maskf[:, 1:2, :].broadcast_to([P, nt, P]), ALU.mult))
                            last = TT(at, at, dtmp[:, 0:nt, :], ALU.add)
                        else:
                            j = {(0, L32): 0, (0, L16): 1, (0, L8): 2, (0, DK): 3, (1, L64): 4, (1, L32): 5, (1, L16): 6, (1, L8): 7}[(d, i)]
                            last = nc.vector.copy_predicated(at, maskb[:, j:j + 1, :].broadcast_to([P, nt, P]), src)
                        last.then_inc(g_free, 1)
                    dve.wait_ge(g_free, 3 * use(h, (d, i)) + 3)
                elif kind == "gate":
                    dve.wait_ge(g_full, 3 * use(h, (1, L8)) + 3)
                    TS(r0, zg[:, h % 2, :, :].rearrange("p t e -> p (t e)"), SIG_FLOOR, None, ALU.max).then_inc(g_clamped, 1)
                elif kind == "fin_o":
                    if h:
                        dve.wait_ge(g_full, 3 * use(h - 1, "yT") + 3)
                    for b, (t0, nt) in enumerate(BANKS):
                        take(h, "o", b)
                        nc.vector.tensor_copy(y[:, t0:t0 + nt, :].rearrange("p t e -> p (t e)"), pg[b][:, 0:nt * P]).then_inc(g_free, 1)
                    dve.wait_ge(g_free, 3 * use(h, "o") + 3)
                    steps.give(nc.vector.tensor_copy(dtmp[:, 0, 0:1], tot8[:, 0, 0:1]))
                    nc.vector.tensor_copy(dtmp[:, 0, 1:2], tot8[:, 0, 0:1]).then_inc(o_out, 1)
                elif kind == "norm":
                    yy = y[:, :, :]
                    dve.wait_ge(o_sq, h + 1)
                    steps.link(dve, nc.vector.reduce_sum(ms[:, :], ring[:, 1, :].rearrange("p (t e) -> p t e", e=RD), AX_X))
                    TS(ms[:, :], ms[:, :], 1.0 / RD, EPS, ALU.mult, ALU.add).then_inc(ms_ready, 1)
                    dve.wait_ge(g_sig, h + 1)
                    g = zg[:, h % 2, :, :]
                    steps.link(dve, TT(g, g, r0.rearrange("p (t e) -> p t e", e=RD), ALU.mult))
                    steps.link(dve, TT(g, g, yy, ALU.mult))
                    dve.wait_ge(rstd, h + 1)
                    TT(yy, g, wide(ms[:, :].rearrange("p (t a) -> p t a", a=1), RD), ALU.mult).then_inc(y_ready, 1)
                elif kind == "fin_y":
                    at = ROWS["r_onorm_g"][0] + h
                    for b, (t0, nt) in enumerate(BANKS):
                        take(h, "yT", b)
                        steps.link(dve, TS(X8[:, t0 * P:(t0 + nt) * P], pg[b][:, 0:nt * P], S["vec"][:, at:at + 1], None, ALU.mult))
                        nc.vector.tensor_copy(dtmp[:, 0, 2:3], tot8[:, 0, 0:1]).then_inc(g_free, 1)
                        dve.wait_ge(g_free, 3 * use(h, "yT") + b + 1)
                        nc.vector.tensor_copy(dtmp[:, 0, 3:4], tot8[:, 0, 0:1]).then_inc(yT_ready, 1)
                        dve.wait_ge(yT_ready, 3 * h + b + 1)

            at = ROWS["r_lb_logits"][0]
            logits = S["vec"][:, at:at + 2 * RH].rearrange("p (s h) -> p s h", s=2)
            steps.link(dve, nc.vector.memset(tot8[:, :, :], 0.0))
            TT(lbt[:, :, :], logits, logits, ALU.subtract).then_inc(lb_d, 1)
            dve.wait_ge(lb_e, 1)
            steps.link(dve, nc.vector.reciprocal(lb[:, :, :], lbt[:, :, :]))
            steps.link(dve, TT(lbt[:, :, :], lbt[:, :, :], lb[:, :, :], ALU.mult))
            steps.link(dve, TT(lb[:, :, :], lbt[:, :, :], lbt[:, :, :], ALU.subtract))
            steps.link(dve, TS(lb[:, :, :], lb[:, :, :], 0.0, None, ALU.max))
            steps.link(dve, TS(oml[:, :, :], lb[:, :, :], -1.0, 1.0, ALU.mult, ALU.add))
            dve.wait_ge(consts, 32)
            steps.give(nc.vector.tensor_copy(maskb[:, :, :].rearrange("p m c -> p (m c)"), ring[:, 0, 0:8 * P]))
            steps.link(dve, nc.vector.memset(restart[:, :], 1.0))
            steps.link(dve, nc.vector.memset(restart[:, :].rearrange("p (b h) -> p b h", h=64)[:, :, 0:1], 0.0))
            for h in range(RH):
                for tok in steps_of_head(h):
                    step(h, tok)


def rec_constants():
    s, t = np.arange(P)[:, None], np.arange(P)[None, :]
    lev = lambda h: ((s // (2 * h) == t // (2 * h)) & (s // h < t // h))
    fw = [lev(h) for h in LEVELS]
    d8 = (s // 8 == t // 8) & (s <= t)
    maskb = np.stack([fw[1], fw[2], fw[3], d8] + [m.T for m in fw], 1)
    maskf = np.stack([fw[0], d8.T], 1)
    return {"k_maskb": np.ascontiguousarray(maskb.astype(np.float32)), "k_maskf": np.ascontiguousarray(maskf.astype(np.float32))}


def final_norm(nc, A, S, x_dram, y_dram, out):
    with ExitStack() as ctx:
        sb, ps, sem = scope(nc, ctx, "fn")
        x, y = sb("x", [P, NT, D]), sb("y", [P, NT, D])
        gate, gain = sb("gate", [P, 2, D]), sb("gain", [P, D])
        junk = sb("junk", [P, 2, D])
        ssq = sb("ssq", [P, NT])
        x_in, y_in = [sem(f"x{t}") for t in range(NT)], [sem(f"y{t}") for t in range(NT)]
        g_in, gated, summed, squared, v_steps, inverted, rooted, scaled, ready, stored = (sem(n) for n in (
            "g_in gated summed squared v inverted rooted scaled ready stored").split())
        block = ctx.enter_context(nc.Block())

        @block.sync
        def _(sp):
            for c in range(2):
                sp.dma_start(gate[:, c, :], S["mod_dram"][DEPTH - 1, c:c + 1, 5 * D:6 * D].broadcast_to([P, D])).then_inc(g_in, 16)
            sp.dma_start(gain[:, :], A["final_norm_g"].rearrange("(a d) -> a d", a=1).broadcast_to([P, D])).then_inc(g_in, 16)
            for t in range(NT):
                sp.dma_start(x[:, t, :], x_dram[t * P:(t + 1) * P, :]).then_inc(x_in[t], 16)
                sp.dma_start(y[:, t, :], y_dram[t * P:(t + 1) * P, :]).then_inc(y_in[t], 16)
            for t in range(NT):
                sp.wait_ge(ready, t + 1)
                sp.dma_start(out(t), y[:, t, :]).then_inc(stored, 16)
            sp.wait_ge(stored, 16 * NT)

        @block.scalar
        def _(act):
            for g, (t0, n, _) in enumerate(PIECES):
                for t in range(t0, t0 + n):
                    act.wait_ge(summed, t + 1)
                    if t >= 2:
                        act.wait_ge(squared, t - 1)
                    nc.scalar.activation(junk[:, t % 2, :], y[:, t, :], ACT.Square, accum_out=ssq[:, t:t + 1]).then_inc(squared, 1)
                act.wait_ge(inverted, g + 1)
                nc.scalar.activation(ssq[:, t0:t0 + n], ssq[:, t0:t0 + n], ACT.Sqrt).then_inc(rooted, 1)

        @block.vector
        def _(dve):
            steps = Count(v_steps)
            dve.wait_ge(g_in, 48)
            for g, (t0, n, _) in enumerate(PIECES):
                for t in range(t0, t0 + n):
                    dve.wait_ge(y_in[t], 16)
                    nc.vector.tensor_tensor(y[:, t, :], y[:, t, :], gate[:, 0 if t < CT else 1, :], ALU.mult).then_inc(gated, 1)
                    dve.wait_ge(gated, t + 1)
                    dve.wait_ge(x_in[t], 16)
                    nc.vector.tensor_tensor(y[:, t, :], y[:, t, :], x[:, t, :], ALU.add).then_inc(summed, 1)
                dve.wait_ge(squared, t0 + n)
                s = ssq[:, t0:t0 + n]
                steps.link(dve, nc.vector.tensor_scalar(s, s, 1.0 / D, EPS, ALU.mult, ALU.add))
                nc.vector.reciprocal(s, s).then_inc(inverted, 1)
                dve.wait_ge(rooted, g + 1)
                for t in range(t0, t0 + n):
                    nc.vector.scalar_tensor_tensor(y[:, t, :], y[:, t, :], ssq[:, t:t + 1], gain[:, :], ALU.mult, ALU.mult).then_inc(ready, 1)


def build_step(nc, A, O, W):
    def rows(t_dram):
        return lambda t: t_dram[t * P:(t + 1) * P, :]

    def x_tile(prompt, sample):
        return lambda t: (prompt[0, t * P:(t + 1) * P, :] if t < CT else sample[0, (t - CT) * P:(t - CT + 1) * P, :])

    with ExitStack() as ctx:
        sb, _, _ = scope(nc, ctx, "step")
        S = {"ident": sb("ident", [P, P]), "vec": sb("vec", [P, NROWS]), "modcol": sb("modcol", [P, DEPTH, 6, 2, KD]),
             "mod_dram": W["mod"]}
        modulation(nc, A, S)

        with ExitStack() as layer0:
            sb0, _, _ = scope(nc, layer0, "l0")
            yh = sb0("yh", [P, 4, T])
            with ExitStack() as proj:
                sb1, _, _ = scope(nc, proj, "l0p")
                hnT = sb1("hnT", [P, KD, T])
                norm_transpose(nc, A, S, "n0", x_tile(A["x_prompt"], A["x_sample"]), 0, 0, 1, hnT)
                with ExitStack() as hy:
                    sb2, _, _ = scope(nc, hy, "l0h")
                    u, uT, filt = sb2("u", [P, 4, T]), sb2("uT", [P, NT, HW]), sb2("filt", [P, NT, HW])
                    hyena_in(nc, A, S, hnT, yh, u, uT)
                    hyena_filter(nc, A, S, filt)
                    hyena_conv(nc, A, S, yh, u, uT, filt)
                qT, kT, v = sb1("qT", [P, 4, T]), sb1("kT", [P, NKV, KT * P]), sb1("v", [P, KT, NKV * HD])
                qkv_in(nc, A, S, hnT, qT, kT, v, O["new_k"].rearrange("b a t g d -> (b a t) (g d)"),
                       O["new_v"].rearrange("b a t g d -> (b a t) (g d)"))
                ya = sb1("ya", [P, 4, T])
                attention(nc, A, S, qT, kT, v, ya)
                out_proj(nc, A, S, "op0", A["e_w_out"][0], lambda k: (yh if k < 4 else ya)[:, k % 4, :],
                         x_tile(A["x_prompt"], A["x_sample"]), rows(W["xm0"]), 0)

        idx = [sb("idx0", [CAP[0], NE], U32), sb("idx1", [CAP[1], NE], U32)]
        gates = [sb("gates0", [CAP[0], NE]), sb("gates1", [CAP[1], NE])]

        def mixer(layer):
            with ExitStack() as norm:
                sb1, _, _ = scope(nc, norm, f"f{layer}")
                hnT = sb1("hnT", [P, KD, T])
                norm_transpose(nc, A, S, f"nf{layer}", rows(W[f"xm{layer}"]), layer, 3, 4, hnT, W["xn"])
                route(nc, A, S, f"rt{layer}", hnT, layer, idx, gates)
            experts(nc, A, S, f"moe{layer}", layer, W["xn"], W["y"], idx, gates)

        mixer(0)

        with ExitStack() as layer1:
            sb1, _, _ = scope(nc, layer1, "l1")
            hnT = sb1("hnT", [P, KD, T])
            norm_transpose(nc, A, S, "n2", rows(W["xm0"]), 1, 0, 1, hnT, residual=(W["y"], 0, W["x1"]))
            recurrence(nc, A, S, hnT, W["yr"], O["new_state"].rearrange("b r s h d e -> (b r s) h d e"))
        with ExitStack() as layer1:
            sb1, _, _ = scope(nc, layer1, "l1o")
            yr = sb1("yr", [P, RH, T])
            out_proj(nc, A, S, "op1", A["r_w_out"][0], lambda k: yr[:, k, :], rows(W["x1"]), rows(W["xm1"]), 1, W["yr"])

        mixer(1)
        final_norm(nc, A, S, W["xm1"], W["y"], x_tile(O["y_prompt"], O["y_sample"]))


def constants():
    f32 = np.float32
    out = {"k_ident": np.eye(P, dtype=f32)}
    feats, offs = [], []
    for _, ln in SEQS:
        t = np.arange(ln, dtype=np.float64)
        tn = t / ln
        ang = 2 * math.pi * tn[:, None] * np.arange(1, 17)[None, :]
        feats.append(np.concatenate([tn[:, None], np.sin(ang), np.cos(ang)], axis=-1))
        offs.append(-np.abs(t - ln // 2) / (ln // 2))
    out["k_feats"] = np.ascontiguousarray(np.concatenate(feats).T.astype(f32))
    out["k_offsets"] = np.ascontiguousarray(np.concatenate(offs).reshape(NT, P).T.astype(f32))
    for tag, (o, ln), (n, fw, nf) in (("c", SEQS[0], CONV[0]), ("l", SEQS[1], CONV[1])):
        w = 2 * math.pi * (np.arange(n // 2) + 0.5) / n
        t = np.arange(ln)
        fw_m = np.stack([np.cos(np.outer(t, w)), -np.sin(np.outer(t, w))], 1)
        fw_m = fw_m.reshape(ln // P, P, 2, nf, fw).transpose(3, 1, 0, 2, 4)
        out["k_fwd_" + tag] = np.ascontiguousarray(fw_m.reshape(nf, P, -1).astype(f32))
        tau = np.arange(ln) + ln // 2
        inv = np.stack([2 / n * np.cos(np.outer(w, tau)), -2 / n * np.sin(np.outer(w, tau))], 1)
        inv = inv.reshape(nf, fw, 2, ln).transpose(1, 0, 2, 3).reshape(fw, 2 * nf, ln)
        if tag == "c":
            out["k_inv_c"] = np.ascontiguousarray(inv.astype(f32))
        else:
            out["k_inv_l"] = np.ascontiguousarray(inv.reshape(fw, 2 * nf, 2, 512).transpose(2, 0, 1, 3).astype(f32))
    pos = np.arange(LL)
    inv_f = 10000.0 ** (-np.arange(0, 32, 2, dtype=np.float64) / 32)
    ang = np.stack([(pos // 64)[:, None] * inv_f, (pos % 64)[:, None] * inv_f], 1)
    for name, f in (("k_cos", np.cos), ("k_sin", np.sin)):
        out[name] = np.ascontiguousarray(f(ang).reshape(LL // P, P, 32).transpose(1, 0, 2).astype(f32))
    return out


_INS = ["x_prompt", "x_sample", "cache_k", "cache_v", "state_rec", "c", "c_ctx", "mod_w", "mod_b", "norm_mix_g", "norm_ffn_g",
        "e_w_in", "e_conv_w", "e_conv_b", "f_w1", "f_b1", "f_freq", "f_w2", "f_b2", "f_w3", "f_decay", "hy_bias", "q_norm_g",
        "k_norm_g", "e_w_out", "r_w_in", "r_lb_logits", "r_onorm_g", "r_w_out", "router_w", "moe_w_gu", "moe_w_down",
        "final_norm_g"]
_OUTS = [("y_prompt", (1, LC, D)), ("y_sample", (1, LL, D)), ("new_k", (1, 1, LC, NKV, HD)), ("new_v", (1, 1, LC, NKV, HD)),
         ("new_state", (1, 1, 2, RH, RD, RD))]
_SCRATCH = [("mod", (DEPTH, 2, 6 * D)), ("xm0", (T, D)), ("x1", (T, D)), ("xm1", (T, D)), ("xn", (T, D)), ("y", (T, D)),
            ("yr", (RH, P, T))]


def kernel(**inputs):
    import concourse.bacc as _bacc
    from concourse.bass_utils import run_bass_kernel_spmd as _run

    nc = _bacc.Bacc("TRN2", target_bir_lowering=False, num_devices=1)
    arrays, A = {}, {}
    data = {name: np.ascontiguousarray(inputs[name]) for name in _INS}
    data.update(constants())
    data.update(rec_constants())
    for name, a in data.items():
        arrays[f"in_{name}"] = a
        A[name] = nc.dram_tensor(f"in_{name}", a.shape, mybir.dt.from_np(a.dtype), kind="ExternalInput").ap()
    O = {name: nc.dram_tensor(f"out_{name}", shape, F32, kind="ExternalOutput").ap() for name, shape in _OUTS}
    W = {name: nc.dram_tensor(f"scratch_{name}", shape, F32, kind="Internal").ap() for name, shape in _SCRATCH}
    build_step(nc, A, O, W)
    r = _run(nc, [arrays], core_ids=[0])
    return tuple(r.results[0][f"out_{name}"] for name, _ in _OUTS)
```

```python
import math
from contextlib import ExitStack

import numpy as np
import concourse.bass as bass
from concourse import mybir

F32 = mybir.dt.float32
U32 = mybir.dt.uint32
ALU = mybir.AluOpType
ACT = mybir.ActivationFunctionType
AX_X = mybir.AxisListType.X

P = 128
D = 1024
KD = D // P
LC, LL = 256, 1024
T = LC + LL
NT = T // P
CT = LC // P
DEPTH = 2
EPS = 1e-6
HW = D // 2
HD, NH, NKV = 64, 8, 2
PAST = 256
RH, RD = 8, 128
NE = 16
FH = D
CAP = [2 * LC // NE, 2 * LL // NE]
PIECES = [(0, 2, 0), (2, 4, 1), (6, 4, 1)]
SEQS = [(0, LC), (LC, LL)]

ROWS = {}
_at = 0
for _name, _n in [("norm_mix_g", 2 * KD), ("norm_ffn_g", 2 * KD), ("e_conv_w", 36), ("e_conv_b", 12),
                  ("hy_bias", 4), ("r_onorm_g", KD), ("r_lb_logits", 2 * KD), ("c_ctx", KD), ("c", KD)]:
    ROWS[_name] = (_at, _n)
    _at += _n
NROWS = _at


class Count:

    def __init__(self, sem, start=0):
        self.sem, self.start, self.n = sem, start, 0

    def give(self, ins, by=1):
        ins.then_inc(self.sem, by)
        self.n += by
        return self.n

    def wait(self, eng, n=None):
        eng.wait_ge(self.sem, self.start + (self.n if n is None else n))

    def link(self, eng, ins):
        self.give(ins)
        self.wait(eng)


def scope(nc, ctx, tag):
    sems = []

    def clear():
        if sems:
            nc.clear_and_free_semaphores(sems)
            nc.all_engine_barrier()

    ctx.callback(clear)

    def sb(name, shape, dt=F32):
        return ctx.enter_context(nc.sbuf_tensor(f"{tag}_{name}", shape, dt))

    def ps(name, shape, dt=F32):
        return ctx.enter_context(nc.psum_tensor(f"{tag}_{name}", shape, dt))

    def sem(name):
        sems.append(nc.alloc_semaphore(f"{tag}_{name}"))
        return sems[-1]
    return sb, ps, sem


def modulation(nc, A, S, filt):
    NB = 12
    G = 3
    KH = KD // 2
    RING = 3
    NS = DEPTH * G * 2
    with ExitStack() as ctx:
        sb, ps, sem = scope(nc, ctx, "mod")
        pack = sb("pack", [P, P])
        w = sb("w_ring", [P, RING, 4, KH, 512])
        row = sb("row", [P, DEPTH, G, 512])
        brow = sb("brow", [P, DEPTH, G, 512])
        scond = sb("scond", [P, 2, KD])
        pst = ps("pst", [P, 512])
        psm = [ps(f"psm{i}", [P, 512]) for i in range(2)]
        pack_in, bias_in, bias_zero = sem("pack_in"), sem("bias_in"), sem("bias_zero")
        w_in = [sem(f"w_in{i}") for i in range(RING)]
        w_used, packed, col_ready, cond_ready = sem("w_used"), sem("packed"), sem("col_ready"), sem("cond_ready")
        row_ready, tr_done, tr_used, stored = sem("row_ready"), sem("tr"), sem("tr_used"), sem("stored")
        block = ctx.enter_context(nc.Block())

        @block.sync
        def _(sp):
            n = 0
            for name, (at, rows) in ROWS.items():
                src = A[name]
                flat = {1: "(r p) -> r p", 2: "a (r p) -> (a r) p", 3: "a b (r p) -> (a b r) p"}[len(src.shape)]
                sp.dma_start(pack[at:at + rows, :], src.rearrange(flat, p=P)).then_inc(pack_in, 16)
                n += 16
            assert n == 16 * len(ROWS)
            sp.dma_start(S["ident"][:, :], A["k_ident"]).then_inc(pack_in, 16)

        @block.scalar
        def _(act):
            act.wait_ge(bias_zero, 1)
            for j in range(4):
                for l in range(DEPTH):
                    src = A["mod_b"][l, :].rearrange("(g j n) -> j g n", j=4, n=512)[j:j + 1]
                    for c in range(2):
                        act.dma_start(brow[32 * j + c:32 * j + c + 1, l, :, :], src).then_inc(bias_in, 16)

        @block.vector
        def _(dve):
            nc.vector.memset(brow[:, :, :, :], 0.0).then_inc(bias_zero, 1)
            nc.vector.memset(row[:, :, :, :], 0.0).then_inc(bias_zero, 1)

        filter_tensor, filter_scalar, filter_vector = hyena_filter(nc, A, filt, block, sb, ps, sem)

        @block.sync
        def _(sp):
            for s in range(NS):
                gh, kh = divmod(s, 2)
                l, g = divmod(gh, G)
                if s >= RING:
                    sp.wait_ge(w_used, 4 * (s - RING + 1))
                for j in range(4):
                    b = 4 * g + j
                    sp.dma_start(w[:, s % RING, j, :, :], A["mod_w"][l, kh * KH * P:(kh + 1) * KH * P, b * 512:(b + 1) * 512]
                                 .rearrange("(k p) n -> p k n", p=P)).then_inc(w_in[s % RING], 16)

        @block.scalar
        def _(act):
            act.wait_ge(col_ready, 1)
            at = ROWS["c_ctx"][0]
            nc.scalar.activation(scond[:, :, :].rearrange("p c k -> p (c k)"), S["vec"][:, at:at + 2 * KD],
                                 ACT.Silu).then_inc(cond_ready, 1)
            for part in range(4):
                filter_scalar(act, part)
            act.wait_ge(row_ready, DEPTH * G)
            for j in range(4):
                for l in range(DEPTH):
                    dst = S["mod_dram"][l].rearrange("c (g j n) -> j c g n", j=4, n=512)[j]
                    act.dma_start(dst, row[32 * j:32 * j + 2, l, :, :]).then_inc(stored, 16)
            act.wait_ge(stored, 16 * 4 * DEPTH)

        @block.tensor
        def _(pe):
            pe.wait_ge(pack_in, 16 * (len(ROWS) + 1))
            nc.tensor.transpose(pst[:, 0:NROWS], pack[0:NROWS, :], S["ident"][0:NROWS, 0:NROWS]).then_inc(packed, 1)
            pe.wait_ge(cond_ready, 1)
            for s in range(NS):
                g, kh = divmod(s, 2)
                if kh == 0 and g >= 2:
                    pe.wait_ge(row_ready, g - 1)
                pe.wait_ge(w_in[s % RING], 64 * (s // RING + 1))
                for k in range(KH):
                    for j in range(4):
                        m = nc.tensor.matmul(psm[g % 2][32 * j:32 * j + 2, :], scond[:, :, kh * KH + k], w[:, s % RING, j, k, :],
                                             start=(kh + k == 0), stop=(kh == 1 and k == KH - 1), tile_position=(0, 32 * j))
                        if k == KH - 1:
                            m.then_inc(w_used, 1)
                if kh == 1 and g < 4:
                    filter_tensor(pe, g)
            pe.wait_ge(row_ready, DEPTH * G)
            for l in range(DEPTH):
                for g in range(G):
                    i = l * G + g
                    if i >= 1:
                        pe.wait_ge(tr_used, i)
                    for q in range(4):
                        m = nc.tensor.transpose(pst[:, q * P:(q + 1) * P], row[:, l, g, q * P:(q + 1) * P],
                                                S["ident"][:, :])
                    m.then_inc(tr_done, 1)

        @block.vector
        def _(dve):
            dve.wait_ge(bias_zero, 2)
            dve.wait_ge(packed, 1)
            nc.vector.tensor_copy(S["vec"][:, :], pst[:, 0:NROWS]).then_inc(col_ready, 1)
            dve.wait_ge(bias_in, 16 * 4 * DEPTH * 2)
            for g in range(DEPTH * G):
                dve.wait_ge(w_used, 8 * (g + 1))
                for j in range(4):
                    r = nc.vector.tensor_tensor(row[32 * j:32 * j + 2, g // G, g % G, :], psm[g % 2][32 * j:32 * j + 2, :],
                                                brow[32 * j:32 * j + 2, g // G, g % G, :], ALU.add)
                r.then_inc(row_ready, 1)
                if g < 4:
                    filter_vector(dve, g)
            mc = S["modcol"]
            for l in range(DEPTH):
                for g in range(G):
                    dve.wait_ge(tr_done, l * G + g + 1)
                    for j in range(4):
                        b = 4 * g + j
                        src = pst[:, :].rearrange("p (q r) -> p q r", r=P)[:, :, 32 * j:32 * j + 2]
                        r = nc.vector.tensor_copy(
                            mc[:, l, b // 2, :, 4 * (b % 2):4 * (b % 2) + 4].rearrange("p c q -> p q c"), src)
                    r.then_inc(tr_used, 1)
            dve.wait_ge(tr_used, DEPTH * G)
            dve.wait_ge(col_ready, 1)
            for l in range(DEPTH):
                for s, gain in ((1, "norm_mix_g"), (4, "norm_ffn_g")):
                    at = ROWS[gain][0] + l * KD
                    for c in range(2):
                        r = nc.vector.scalar_tensor_tensor(mc[:, l, s, c, :], mc[:, l, s, c, :], 1.0,
                                                           S["vec"][:, at:at + KD], ALU.add, ALU.mult)


def norm_transpose(nc, A, S, tag, x_dram, layer, shift, scale, hnT, xn_dram=None, residual=None):
    with ExitStack() as ctx:
        sb, ps, sem = scope(nc, ctx, tag)
        x = sb("x", [P, NT, D])
        src = x
        if residual is not None:
            src = sb("y", [P, NT, D])
            gate = sb("gate", [P, 2, D])
            y_in, g_in, x_stored, gated, summed = [sem(f"y{t}") for t in range(NT)], sem("g_in"), sem("x_stored"), sem("gated"), sem("summed")
        junk = sb("junk", [P, 2, D])
        ssq, rstd = sb("ssq", [P, NT]), sb("rstd", [P, NT])
        NPS = 6
        pst = [ps(f"ps{i}", [P, 512]) for i in range(NPS)]
        x_in = [sem(f"x{t}") for t in range(NT)]
        squared, inverted, v_steps, rooted, scaled, tr, ev_a, ev_v, stored = (
            sem("squared"), sem("inverted"), sem("v"), sem("rooted"), sem("scaled"), sem("tr"),
            sem("ev_a"), sem("ev_v"), sem("stored"))
        block = ctx.enter_context(nc.Block())
        units = [(t0, n, c, k) for t0, n, c in PIECES for k in range(KD)]
        groups = [(t0, n) for t0, n, _ in PIECES]

        @block.sync
        def _(sp):
            for t in range(NT):
                sp.dma_start(x[:, t, :], x_dram(t)).then_inc(x_in[t], 16)
                if residual is not None:
                    if t == 0:
                        for c in range(2):
                            sp.dma_start(gate[:, c, :], S["mod_dram"][residual[1], c:c + 1, 5 * D:6 * D].broadcast_to([P, D])).then_inc(g_in, 16)
                    sp.dma_start(src[:, t, :], residual[0][t * P:(t + 1) * P, :]).then_inc(y_in[t], 16)
            if residual is not None:
                for t in range(NT):
                    sp.wait_ge(summed, t + 1)
                    sp.dma_start(residual[2][t * P:(t + 1) * P, :], src[:, t, :]).then_inc(x_stored, 16)
                sp.wait_ge(x_stored, 16 * NT)
            if xn_dram is not None:
                for t in range(NT):
                    sp.wait_ge(scaled, t + 1)
                    sp.dma_start(xn_dram[t * P:(t + 1) * P, :], x[:, t, :]).then_inc(stored, 16)
                sp.wait_ge(stored, 16 * NT)

        @block.scalar
        def _(act):
            for g, (t0, n) in enumerate(groups):
                for t in range(t0, t0 + n):
                    if residual is None:
                        act.wait_ge(x_in[t], 16)
                    else:
                        act.wait_ge(summed, t + 1)
                    if t >= 2:
                        act.wait_ge(squared, t - 1)
                    nc.scalar.activation(junk[:, t % 2, :], src[:, t, :], ACT.Square,
                                         accum_out=ssq[:, t:t + 1]).then_inc(squared, 1)
                act.wait_ge(inverted, g + 1)
                nc.scalar.activation(rstd[:, t0:t0 + n], rstd[:, t0:t0 + n], ACT.Sqrt).then_inc(rooted, 1)
            for u, (t0, n, c, k) in enumerate(units):
                if u % 2 == 0:
                    act.wait_ge(tr, u + 1)
                    nc.scalar.activation(hnT[:, k, t0 * P:(t0 + n) * P], pst[u % NPS][:, 0:n * P], ACT.Identity,
                                         bias=S["modcol"][:, layer, shift, c, k:k + 1],
                                         scale=S["modcol"][:, layer, scale, c, k:k + 1]).then_inc(ev_a, 1)

        @block.vector
        def _(dve):
            steps = Count(v_steps)
            if residual is not None:
                dve.wait_ge(g_in, 32)
            for g, (t0, n) in enumerate(groups):
                if residual is not None:
                    for t in range(t0, t0 + n):
                        dve.wait_ge(y_in[t], 16)
                        nc.vector.tensor_tensor(src[:, t, :], src[:, t, :], gate[:, 0 if t < CT else 1, :], ALU.mult).then_inc(gated, 1)
                        dve.wait_ge(gated, t + 1)
                        dve.wait_ge(x_in[t], 16)
                        nc.vector.tensor_tensor(src[:, t, :], src[:, t, :], x[:, t, :], ALU.add).then_inc(summed, 1)
                    dve.wait_ge(summed, t0 + n)
                dve.wait_ge(squared, t0 + n)
                steps.link(dve, nc.vector.tensor_scalar(rstd[:, t0:t0 + n], ssq[:, t0:t0 + n], 1.0 / D, EPS, ALU.mult, ALU.add))
                nc.vector.reciprocal(rstd[:, t0:t0 + n], rstd[:, t0:t0 + n]).then_inc(inverted, 1)
                dve.wait_ge(rooted, g + 1)
                for t in range(t0, t0 + n):
                    nc.vector.tensor_scalar(x[:, t, :], src[:, t, :], rstd[:, t:t + 1], None, ALU.mult).then_inc(scaled, 1)
            for u, (t0, n, c, k) in enumerate(units):
                if u % 2 == 1:
                    dve.wait_ge(tr, u + 1)
                    nc.vector.tensor_scalar(hnT[:, k, t0 * P:(t0 + n) * P], pst[u % NPS][:, 0:n * P],
                                            S["modcol"][:, layer, scale, c, k:k + 1],
                                            S["modcol"][:, layer, shift, c, k:k + 1], ALU.mult, ALU.add).then_inc(ev_v, 1)

        @block.tensor
        def _(pe):
            for u, (t0, n, c, k) in enumerate(units):
                pe.wait_ge(scaled, t0 + n)
                if u >= NPS:
                    prev = u - NPS
                    pe.wait_ge(ev_v if prev % 2 else ev_a, prev // 2 + 1)
                for i in range(n):
                    m = nc.tensor.transpose(pst[u % NPS][:, i * P:(i + 1) * P], x[:, t0 + i, k * P:(k + 1) * P],
                                            S["ident"][:, :])
                m.then_inc(tr, 1)


def hyena_in(nc, A, S, hnT, x0, u, uT):
    NPS, NTR, NZ = 5, 3, 3
    with ExitStack() as ctx:
        sb, ps, sem = scope(nc, ctx, "hin")
        w = sb("w", [P, 2, KD, 3, P])
        z = sb("z", [P, NZ, LC + 2 + LL + 2])
        x1 = sb("x1", [P, 2, T])
        hv = sb("hv", [P, 2, T])
        psm = [ps(f"psm{i}", [P, 512]) for i in range(NPS)]
        pst = [ps(f"pst{i}", [P, 512]) for i in range(NTR)]
        w_in = [sem("w_in0"), sem("w_in1")]
        mm, z_ready, z_used, v_steps, u_ready, tr, tr_used, zeroed = (
            sem("mm"), sem("z_ready"), sem("z_used"), sem("v"), sem("u_ready"),
            sem("tr"), sem("tr_used"), sem("zeroed"))
        ZAT = {0: 1, LC: LC + 3}
        block = ctx.enter_context(nc.Block())

        @block.sync
        def _(sp):
            for i in range(4):
                if i >= 2:
                    sp.wait_ge(mm, 9 * (i - 1))
                for part in range(3):
                    c0 = part * HW + i * P
                    sp.dma_start(w[:, i % 2, :, part, :],
                                 A["e_w_in"][0, :, c0:c0 + P].rearrange("(k p) n -> p k n", p=P)).then_inc(w_in[i % 2], 16)

        @block.tensor
        def _(pe):
            def transposes(i):
                pe.wait_ge(u_ready, i + 1)
                for g, (t0, n, _) in enumerate(PIECES):
                    if i >= 1:
                        pe.wait_ge(tr_used, 3 * (i - 1) + g + 1)
                    for t in range(n):
                        m = nc.tensor.transpose(pst[g][:, t * P:(t + 1) * P],
                                                u[:, i, (t0 + t) * P:(t0 + t + 1) * P], S["ident"][:, :])
                    m.then_inc(tr, 1)

            for i in range(4):
                pe.wait_ge(w_in[i % 2], 48 * (i // 2 + 1))
                for part in range(3):
                    for g, (t0, n, _) in enumerate(PIECES):
                        j = 9 * i + 3 * part + g
                        if j >= NPS:
                            pe.wait_ge(z_ready, j - NPS + 1)
                        for k in range(KD):
                            m = nc.tensor.matmul(psm[j % NPS][:, 0:n * P], w[:, i % 2, k, part, :],
                                                 hnT[:, k, t0 * P:(t0 + n) * P], start=(k == 0), stop=(k == KD - 1))
                        m.then_inc(mm, 1)
                    if part == 0 and i >= 1:
                        transposes(i - 1)
            transposes(3)

        @block.scalar
        def _(act):
            act.wait_ge(zeroed, 1)

            def to_uT(i):
                for g, (t0, n, _) in enumerate(PIECES):
                    act.wait_ge(tr, 3 * i + g + 1)
                    nc.scalar.activation(uT[:, t0:t0 + n, i * P:(i + 1) * P],
                                         pst[g][:, 0:n * P].rearrange("p (t c) -> p t c", c=P), ACT.Copy).then_inc(tr_used, 1)

            for tile in range(12):
                i, part = divmod(tile, 3)
                if tile >= NZ:
                    act.wait_ge(z_used, tile - NZ + 1)
                for g, (t0, n, c) in enumerate(PIECES):
                    at = ZAT[SEQS[c][0]] + t0 * P - SEQS[c][0]
                    act.wait_ge(mm, 3 * tile + g + 1)
                    nc.scalar.activation(z[:, tile % NZ, at:at + n * P], psm[(3 * tile + g) % NPS][:, 0:n * P],
                                         ACT.Copy).then_inc(z_ready, 1)
                if part == 1 and i >= 1:
                    to_uT(i - 1)
            to_uT(3)

        @block.vector
        def _(dve):
            steps = Count(v_steps)
            nc.vector.memset(z[:, :, :], 0.0).then_inc(zeroed, 1)
            for tile in range(12):
                i, part = divmod(tile, 3)
                dve.wait_ge(z_ready, 3 * (tile + 1))
                out = (x0[:, i, :], x1[:, i % 2, :], hv[:, i % 2, :])[part]
                wc, bc = ROWS["e_conv_w"][0] + part * 4 + i, ROWS["e_conv_b"][0] + part * 4 + i
                at = [(o, ln, ZAT[o] - 1) for o, ln in SEQS]
                for o, ln, a in at:
                    r = nc.vector.tensor_scalar(out[:, o:o + ln], z[:, tile % NZ, a:a + ln], S["vec"][:, wc:wc + 1],
                                                S["vec"][:, bc:bc + 1], ALU.mult, ALU.add)
                steps.link(dve, r)
                for tap in (1, 2):
                    for o, ln, a in at:
                        r = nc.vector.scalar_tensor_tensor(out[:, o:o + ln], z[:, tile % NZ, a + tap:a + tap + ln],
                                                           S["vec"][:, wc + 12 * tap:wc + 12 * tap + 1],
                                                           out[:, o:o + ln], ALU.mult, ALU.add)
                    if tap == 1:
                        steps.link(dve, r)
                r.then_inc(z_used, 1)
                if part == 2:
                    dve.wait_ge(z_used, tile + 1)
                    nc.vector.tensor_tensor(u[:, i, :], x1[:, i % 2, :], hv[:, i % 2, :], ALU.mult).then_inc(u_ready, 1)


def hyena_filter(nc, A, filt, block, sb, ps, sem):
    MAGIC = 12582912.0
    TWO_PI = 2 * math.pi
    HI = 6.28125
    LO = TWO_PI - HI
    EMB, FHID = 33, 64
    feats = sb("feats", [EMB, T])
    w1, w2, w3 = sb("w1", [EMB, FHID]), sb("w2", [FHID, FHID]), sb("w3", [FHID, HW])
    cols = sb("cols", [FHID, 3])
    arg, turn, hid = sb("arg", [FHID, T]), sb("turn", [FHID, T]), sb("hid", [FHID, T])
    decay, offs = sb("decay", [P, HW]), sb("offs", [P, NT])
    win = sb("win", [P, NT, HW])
    ones = sb("ones", [P, P])
    rsum = sb("rsum", [P, 2, HW])
    psl = [ps(f"psl{i}", [P, 512]) for i in range(3)]
    psw = psl
    pss = [ps("pss0", [P, 512]), ps("pss1", [P, 512])]
    loaded, v_steps, mm, sined, w_ready, h_mm, h_ready, a_ready, summed, ab, abs_ready = (
        sem("loaded"), sem("f_v"), sem("mm"), sem("sined"), sem("w_ready"), sem("h_mm"), sem("h_ready"),
        sem("a_ready"), sem("summed"), sem("ab"), sem("abs_ready"))

    LOADS = 9 * 16
    steps = Count(v_steps)

    @block.sync
    def _(sp):
        for dst, src in ((feats, A["k_feats"]), (w1, A["f_w1"][0]), (w2, A["f_w2"][0]), (w3, A["f_w3"][0]),
                         (offs, A["k_offsets"])):
            sp.dma_start(dst[:, :], src).then_inc(loaded, 16)
        for j, name in enumerate(("f_b1", "f_freq", "f_b2")):
            sp.dma_start(cols[:, j:j + 1], A[name][0].rearrange("(p a) -> p a", a=1)).then_inc(loaded, 16)
        sp.dma_start(decay[:, :], A["f_decay"].broadcast_to([P, HW])).then_inc(loaded, 16)

    def tensor(pe, part):
        if part < 2:
            if part == 0:
                pe.wait_ge(loaded, LOADS)
            else:
                pe.wait_ge(sined, 1)
            wt, x = ((w1, feats), (w2, hid))[part]
            for g, (t0, n, _) in enumerate(PIECES):
                m = nc.tensor.matmul(psl[g][0:FHID, 0:n * P], wt[:, :], x[:, t0 * P:(t0 + n) * P], start=True, stop=True)
            m.then_inc(mm, 1)
        elif part == 2:
            pe.wait_ge(sined, 2)
            for t in range(NT):
                if t >= 3:
                    pe.wait_ge(h_ready, t - 2)
                nc.tensor.matmul(psw[t % 3][:, :], hid[:, t * P:(t + 1) * P], w3[:, :], start=True, stop=True).then_inc(h_mm, 1)
        else:
            pe.wait_ge(abs_ready, NT)
            for c, (o, ln) in enumerate(SEQS):
                for t in range(o // P, (o + ln) // P):
                    m = nc.tensor.matmul(pss[c][:, :], ones[:, :], win[:, t, :], start=(t == o // P), stop=((t + 1) * P == o + ln))
                m.then_inc(summed, 1)

    def scalar(act, part):
        if part < 2:
            if part == 0:
                act.wait_ge(loaded, LOADS)
                nc.scalar.activation(decay[:, :], decay[:, :], ACT.Abs).then_inc(ab, 1)
            act.wait_ge(a_ready, part + 1)
            nc.scalar.activation(hid[:, :], arg[:, :], ACT.Sin).then_inc(sined, 1)
        elif part == 2:
            act.wait_ge(ab, 1)
            for t in range(NT):
                nc.scalar.activation(win[:, t, :], decay[:, :], ACT.Exp, scale=offs[:, t:t + 1]).then_inc(w_ready, 1)
            for t in range(NT):
                act.wait_ge(h_ready, t + 1)
                nc.scalar.activation(win[:, t, :], filt[:, t, :], ACT.Abs).then_inc(abs_ready, 1)

    def vector(dve, part):
        if part < 2:
            if part == 0:
                nc.vector.memset(ones[:, :], 1.0)
                dve.wait_ge(loaded, LOADS)
            dve.wait_ge(mm, part + 1)
            for g, (t0, n, _) in enumerate(PIECES):
                r = nc.vector.tensor_scalar(arg[:, t0 * P:(t0 + n) * P], psl[g][0:FHID, 0:n * P],
                                            cols[:, 2 * part:2 * part + 1], cols[:, 1:2], ALU.add, ALU.mult)
            steps.link(dve, r)
            steps.link(dve, nc.vector.tensor_scalar(turn[:, :], arg[:, :], 1.0 / TWO_PI, MAGIC, ALU.mult, ALU.add))
            steps.link(dve, nc.vector.tensor_scalar(turn[:, :], turn[:, :], MAGIC, None, ALU.subtract))
            steps.link(dve, nc.vector.scalar_tensor_tensor(arg[:, :], turn[:, :], -HI, arg[:, :], ALU.mult, ALU.add))
            steps.link(dve, nc.vector.scalar_tensor_tensor(arg[:, :], turn[:, :], -LO, arg[:, :], ALU.mult, ALU.add))
            nc.vector.tensor_scalar(arg[:, :], arg[:, :], 3.1415925, -3.1415925, ALU.min, ALU.max).then_inc(a_ready, 1)
        elif part == 2:
            for t in range(NT):
                dve.wait_ge(h_mm, t + 1)
                dve.wait_ge(w_ready, t + 1)
                nc.vector.tensor_tensor(filt[:, t, :], psw[t % 3][:, :], win[:, t, :], ALU.mult).then_inc(h_ready, 1)
        else:
            dve.wait_ge(summed, 2)
            for c in range(2):
                steps.link(dve, nc.vector.tensor_scalar(rsum[:, c, :], pss[c][:, :], EPS, None, ALU.add))
                steps.link(dve, nc.vector.reciprocal(rsum[:, c, :], rsum[:, c, :]))
            for t in range(NT):
                nc.vector.tensor_tensor(filt[:, t, :], filt[:, t, :], rsum[:, 0 if t < CT else 1, :], ALU.mult)

    return tensor, scalar, vector


CONV = [
    (3 * LC // 2, 96, 2), (3 * LL // 2, 128, 6)]


def hyena_conv(nc, A, S, x0, u, uT, filt):
    NF, NG = 2, 2
    NFT = [c[2] for c in CONV]
    with ExitStack() as ctx:
        sb, ps, sem = scope(nc, ctx, "cv")
        fwd = sb("fwd", [P, NF, 8, 2, P])
        inv = sb("inv", [P, 12, 512])
        Y = sb("Y", [P, 6, 2, HW])
        H = sb("H", [P, 2, HW])
        tmp = sb("tmp", [P, 4, HW])
        psf = [ps(f"psf{i}", [P, 512]) for i in range(8)]
        f_in = [sem(f"f_in{i}") for i in range(NF)]
        i_in = sem("i_in")
        u_mm, h_mm, h_out, prod, v_steps, y_ready, inv_mm, out_ready = (
            sem("u_mm"), sem("h_mm"), sem("h_out"), sem("prod"), sem("v"), sem("y_ready"), sem("inv_mm"), sem("out_ready"))
        block = ctx.enter_context(nc.Block())
        ftiles = [(c, f) for c in range(2) for f in range(NFT[c])]
        halves = [(0, 0, LC)] + [(1, h * 512, 512) for h in range(2)]

        def inverse_in(sp, h):
            if h:
                sp.wait_ge(inv_mm, 4 * h)
            if h == 0:
                sp.dma_start(inv[0:96, 0:4, 0:LC], A["k_inv_c"]).then_inc(i_in, 16)
            else:
                sp.dma_start(inv[:, :, :], A["k_inv_l"][h - 1]).then_inc(i_in, 16)

        @block.sync
        def _(sp):
            for n, (c, f) in enumerate(ftiles):
                if n >= NF:
                    sp.wait_ge(h_mm, n - NF + 1)
                tt, fw = (2, 96) if c == 0 else (8, 128)
                src = A["k_fwd_c"][f] if c == 0 else A["k_fwd_l"][f]
                sp.dma_start(fwd[:, n % NF, 0:tt, :, 0:fw], src.rearrange("p (t r f) -> p t r f", t=tt, r=2)).then_inc(f_in[n % NF], 16)
                if n in (1, 6):
                    inverse_in(sp, 0 if n == 1 else 1)
            inverse_in(sp, 2)

        @block.tensor
        def _(pe):
            def forward(n):
                c, f = ftiles[n]
                t0, tt, fw = (0, 2, 96) if c == 0 else (2, 8, 128)
                pe.wait_ge(f_in[n % NF], 16 * (n // NF + 1))
                if n == 2:
                    pe.wait_ge(out_ready, 4)
                if n >= 2:
                    pe.wait_ge(prod, n - 1)
                for q, (src, done) in enumerate(((uT, u_mm), (filt, h_mm))):
                    for r in range(2):
                        for t in range(tt):
                            m = nc.tensor.matmul(psf[4 * (n % 2) + 2 * q + r][0:fw, :], fwd[:, n % NF, t, r, 0:fw], src[:, t0 + t, :],
                                                 start=(t == 0), stop=(t == tt - 1))
                    m.then_inc(done, 1)

            def inverse(h):
                c, o, ln = halves[h]
                fw, nf = CONV[c][1], NFT[c]
                pe.wait_ge(i_in, 16 * (h + 1))
                pe.wait_ge(y_ready, 2 if c == 0 else 8)
                for ch in range(4):
                    n = 4 * h + ch
                    bank = psf[4 + ch if h < 2 else ch]
                    for j in range(2 * nf):
                        m = nc.tensor.matmul(bank[:, 0:ln], Y[0:fw, j // 2, j % 2, ch * P:(ch + 1) * P], inv[0:fw, j, 0:ln],
                                             start=(j == 0), stop=(j == 2 * nf - 1))
                    m.then_inc(inv_mm, 1)

            forward(0)
            forward(1)
            pe.wait_ge(prod, 2)
            inverse(0)
            for n in range(2, 8):
                forward(n)
            pe.wait_ge(prod, 8)
            inverse(1)
            inverse(2)

        @block.scalar
        def _(act):
            for n, (c, f) in enumerate(ftiles):
                fw = CONV[c][1]
                act.wait_ge(h_mm, n + 1)
                if n >= 1:
                    act.wait_ge(prod, n)
                for r in range(2):
                    h = nc.scalar.activation(H[0:fw, r, :], psf[4 * (n % 2) + 2 + r][0:fw, :], ACT.Copy)
                h.then_inc(h_out, 1)

        @block.vector
        def _(dve):
            steps = Count(v_steps)

            def outputs(h):
                c, o, ln = halves[h]
                o += SEQS[c][0]
                at = ROWS["hy_bias"][0]
                for ch in range(4):
                    n = 4 * h + ch
                    dve.wait_ge(inv_mm, n + 1)
                    bank = psf[4 + ch if h < 2 else ch]
                    steps.link(dve, nc.vector.scalar_tensor_tensor(u[:, ch, o:o + ln], u[:, ch, o:o + ln],
                                                                   S["vec"][:, at + ch:at + ch + 1], bank[:, 0:ln], ALU.mult, ALU.add))
                    nc.vector.tensor_tensor(x0[:, ch, o:o + ln], x0[:, ch, o:o + ln], u[:, ch, o:o + ln], ALU.mult).then_inc(out_ready, 1)

            for n, (c, f) in enumerate(ftiles):
                if n == 2:
                    outputs(0)
                fw = CONV[c][1]
                dve.wait_ge(u_mm, n + 1)
                dve.wait_ge(h_out, n + 1)
                if n >= 1:
                    dve.wait_ge(y_ready, n)
                if n == 2:
                    dve.wait_ge(inv_mm, 4)
                ur, ui = (psf[4 * (n % 2) + r][0:fw, :] for r in range(2))
                yf = f
                for j, (a, r) in enumerate(((ur, 0), (ui, 1), (ur, 1), (ui, 0))):
                    last = nc.vector.tensor_tensor(tmp[0:fw, j, :], a, H[0:fw, r, :], ALU.mult)
                steps.give(last)
                steps.wait(dve)
                nc.vector.tensor_tensor(Y[0:fw, yf, 0, :], tmp[0:fw, 0, :], tmp[0:fw, 1, :], ALU.subtract).then_inc(prod, 1)
                nc.vector.tensor_tensor(Y[0:fw, yf, 1, :], tmp[0:fw, 2, :], tmp[0:fw, 3, :], ALU.add).then_inc(y_ready, 1)
            outputs(1)
            outputs(2)


KT = NT + PAST // P


def key_tile(t):
    return t if t < CT else t + PAST // P


def qkv_in(nc, A, S, hnT, qT, kT, v, out_k, out_v):
    QW, KW = NH * HD, NKV * HD
    NHQ = NH + NKV
    with ExitStack() as ctx:
        sb, ps, sem = scope(nc, ctx, "qkv")
        w = sb("w", [P, KD, QW + 2 * KW])
        z = sb("z", [P, 2, QW + KW])
        sq = sb("sq", [P, 2, QW + KW])
        kd = sb("kd", [P, 2, NKV, 2, HD])
        ck = sb("ck", [P, PAST // P, NKV, HD])
        ckd = sb("ckd", [P, PAST // P, NKV, 2, HD])
        ra, rb = sb("ra", [P, NHQ, 2, 2, 16]), sb("rb", [P, NHQ, 2, 2, 16])
        cos, sin = sb("cos", [P, LL // P, 2, 16]), sb("sin", [P, LL // P, 2, 16])
        gain = sb("gain", [P, 2, HD])
        ss = sb("ss", [P, NT, NHQ])
        psq = [ps(f"psq{i}", [P, 512]) for i in range(2)]
        pskv = [ps(f"pskv{i}", [P, 512]) for i in range(2)]
        ptq = [ps(f"ptq{i}", [P, 512]) for i in range(2)]
        ptk = [ps(f"ptk{i}", [P, 512]) for i in range(2)]
        w_in = [sem(f"w_in{k}") for k in range(KD)]
        k_stored = [sem(f"k_stored{t}") for t in range(CT)]
        loaded, v_steps, mm, z_out, z_sq, inv, root, r_ready, tr, tr_used, c_dup, stored, kv_out, gains = (
            sem("loaded"), sem("v"), sem("mm"), sem("z_out"), sem("z_sq"), sem("inv"), sem("root"), sem("r_ready"),
            sem("tr"), sem("tr_used"), sem("c_dup"), sem("stored"), sem("kv_out"), sem("gains"))
        block = ctx.enter_context(nc.Block())

        @block.sync
        def _(sp):
            for k in range(KD):
                sp.dma_start(w[:, k, :], A["e_w_in"][0, k * P:(k + 1) * P, 3 * HW:]).then_inc(w_in[k], 16)
            sp.dma_start(cos[:, :, :, :].rearrange("p t a f -> p t (a f)"), A["k_cos"]).then_inc(loaded, 16)
            sp.dma_start(sin[:, :, :, :].rearrange("p t a f -> p t (a f)"), A["k_sin"]).then_inc(loaded, 16)
            sp.dma_start(gain[:, 0, :], A["q_norm_g"].broadcast_to([P, HD])).then_inc(loaded, 16)
            sp.dma_start(gain[:, 1, :], A["k_norm_g"].broadcast_to([P, HD])).then_inc(loaded, 16)
            sp.dma_start(ck[:, :, :, :], A["cache_k"][0, 0].rearrange("(t p) g d -> p t g d", p=P)).then_inc(loaded, 16)
            sp.dma_start(v[:, CT:CT + PAST // P, :], A["cache_v"][0, 0].rearrange("(t p) g d -> p t (g d)", p=P)).then_inc(loaded, 16)
            for t in range(CT):
                sp.wait_ge(r_ready, t + 1)
                sp.dma_start(out_k[t * P:(t + 1) * P], z[:, t % 2, QW:]).then_inc(k_stored[t], 16)
                sp.wait_ge(kv_out, t + 1)
                sp.dma_start(out_v[t * P:(t + 1) * P], v[:, t, :]).then_inc(stored, 16)
            sp.wait_ge(stored, 16 * CT)
            for t in range(CT):
                sp.wait_ge(k_stored[t], 16)
            sp.wait_ge(loaded, 6 * 16)

        @block.tensor
        def _(pe):
            def transposes(n, src_q, src_k):
                if n >= 2:
                    pe.wait_ge(tr_used, n - 1)
                if src_q is not None:
                    for pr in range(4):
                        nc.tensor.transpose(ptq[n % 2][:, pr * P:(pr + 1) * P], src_q[:, pr * P:(pr + 1) * P], S["ident"][:, :])
                for g in range(NKV):
                    m = nc.tensor.transpose(ptk[n % 2][:, g * P:(g + 1) * P],
                                            src_k[:, g, :, :].rearrange("p a d -> p (a d)"), S["ident"][:, :])
                m.then_inc(tr, 1)

            for t in range(NT + 1):
                if t < NT:
                    if t >= 2:
                        pe.wait_ge(z_out, t - 1)
                        pe.wait_ge(kv_out, t - 1)
                    for k in range(KD):
                        if t == 0:
                            pe.wait_ge(w_in[k], 16)
                        st = dict(start=(k == 0), stop=(k == KD - 1))
                        x = hnT[:, k, t * P:(t + 1) * P]
                        nc.tensor.matmul(psq[t % 2][:, :], x, w[:, k, 0:QW], **st)
                        m = nc.tensor.matmul(pskv[t % 2][:, 0:2 * KW], x, w[:, k, QW:], **st)
                    m.then_inc(mm, 1)
                if t == 1:
                    pe.wait_ge(c_dup, 1)
                    for i in range(PAST // P):
                        transposes(i, None, ckd[:, i])
                if t >= 1:
                    pe.wait_ge(r_ready, t)
                    transposes(t + 1, z[:, (t - 1) % 2, 0:QW], kd[:, (t - 1) % 2])

        @block.scalar
        def _(act):
            def copies(n, t):
                act.wait_ge(tr, n + 1)
                if t >= 0:
                    nc.scalar.activation(qT[:, :, t * P:(t + 1) * P], ptq[n % 2][:, :].rearrange("p (a c) -> p a c", c=P), ACT.Copy)
                kt = key_tile(t) if t >= 0 else CT + n
                nc.scalar.activation(kT[:, :, kt * P:(kt + 1) * P], ptk[n % 2][:, 0:NKV * P].rearrange("p (a c) -> p a c", c=P),
                                     ACT.Copy).then_inc(tr_used, 1)

            for t in range(NT + 1):
                if t < NT:
                    act.wait_ge(mm, t + 1)
                    if t >= 2:
                        act.wait_ge(tr, t + 1)
                        if t - 2 < CT:
                            act.wait_ge(k_stored[t - 2], 16)
                    nc.scalar.activation(z[:, t % 2, 0:QW], psq[t % 2][:, :], ACT.Copy).then_inc(z_out, 1)
                    nc.scalar.activation(z[:, t % 2, QW:], pskv[t % 2][:, 0:KW], ACT.Copy)
                    nc.scalar.activation(v[:, key_tile(t), :], pskv[t % 2][:, KW:2 * KW], ACT.Copy).then_inc(kv_out, 1)
                    act.wait_ge(kv_out, t + 1)
                    if t >= 2:
                        act.wait_ge(inv, t - 1)
                    nc.scalar.activation(sq[:, t % 2, :], z[:, t % 2, :], ACT.Square).then_inc(z_sq, 1)
                    act.wait_ge(inv, t + 1)
                    nc.scalar.activation(ss[:, t, :], ss[:, t, :], ACT.Sqrt).then_inc(root, 1)
                if t == 1:
                    copies(0, -1)
                    copies(1, -1)
                if t >= 1:
                    copies(t + 1, t - 1)

        @block.vector
        def _(dve):
            steps = Count(v_steps)
            dve.wait_ge(loaded, 6 * 16)
            steps.link(dve, nc.vector.tensor_scalar(gain[:, 0, :], gain[:, 0, :], HD ** -0.5, None, ALU.mult))
            for i in range(PAST // P):
                r = nc.vector.tensor_copy(ckd[:, i, :, :, :], ck[:, i, :, :].rearrange("p g (a d) -> p g a d", a=1).broadcast_to([P, NKV, 2, HD]))
            r.then_inc(c_dup, 1)
            for t in range(NT):
                zt = z[:, t % 2, :]
                heads = zt.rearrange("p (h d) -> p h d", d=HD)
                s = ss[:, t, :]
                dve.wait_ge(z_sq, t + 1)
                steps.link(dve, nc.vector.reduce_sum(s, sq[:, t % 2, :].rearrange("p (h d) -> p h d", d=HD), AX_X))
                steps.link(dve, nc.vector.tensor_scalar(s, s, 1.0 / HD, EPS, ALU.mult, ALU.add))
                nc.vector.reciprocal(s, s).then_inc(inv, 1)
                dve.wait_ge(root, t + 1)
                steps.link(dve, nc.vector.tensor_tensor(
                    heads, heads, s.rearrange("p (h a) -> p h a", a=1).broadcast_to([P, NHQ, HD]), ALU.mult))
                for h0, hn, j in ((0, NH, 0), (NH, NKV, 1)):
                    r = nc.vector.tensor_tensor(heads[:, h0:h0 + hn, :], heads[:, h0:h0 + hn, :],
                                                gain[:, j:j + 1, :].broadcast_to([P, hn, HD]), ALU.mult)
                steps.link(dve, r)
                if t >= CT:
                    def half(x, h):
                        return x[:, :, :, h, :]
                    x5 = zt.rearrange("p (h a b f) -> p h a b f", a=2, b=2, f=16)
                    c4 = cos[:, t - CT:t - CT + 1, :, :].broadcast_to([P, NHQ, 2, 16])
                    s4 = sin[:, t - CT:t - CT + 1, :, :].broadcast_to([P, NHQ, 2, 16])
                    for h in range(2):
                        nc.vector.tensor_tensor(half(ra, h), half(x5, h), c4, ALU.mult)
                        r = nc.vector.tensor_tensor(half(rb, h), half(x5, 1 - h), s4, ALU.mult)
                    steps.link(dve, r)
                    nc.vector.tensor_tensor(half(x5, 0), half(ra, 0), half(rb, 0), ALU.subtract)
                    steps.link(dve, nc.vector.tensor_tensor(half(x5, 1), half(ra, 1), half(rb, 1), ALU.add))
                if t >= 2:
                    dve.wait_ge(tr, t + 1)
                nc.vector.tensor_copy(kd[:, t % 2, :, :, :], zt[:, QW:].rearrange("p (g a d) -> p g a d", g=NKV, a=1).broadcast_to([P, NKV, 2, HD])
                                      ).then_inc(r_ready, 1)


def attention(nc, A, S, qT, kT, v, yT):
    items = [(2 * pr + r, t, 0 if t < CT else CT, CT if t < CT else KT - CT)
             for pr in range(4) for t in range(NT) for r in range(2)]
    N = len(items)
    chunks = [[(k, min(4, nk - k)) for k in range(0, nk, 4)] for _, _, _, nk in items]
    first = [sum(len(c) for c in chunks[:i]) for i in range(N + 1)]
    KMAX = KT - CT
    with ExitStack() as ctx:
        sb, ps, sem = scope(nc, ctx, "att")
        p = sb("p", [P, 2, KMAX * P])
        pT = sb("pT", [P, 2, KMAX, P])
        top, part = sb("top", [P, N, 3]), sb("part", [P, N, 3])
        nmax, total = sb("nmax", [P, N]), sb("total", [P, N])
        s_ps = ps("s_ps", [P, 3 * 512])
        t_ps = [ps(f"t_ps{i}", [P, 512]) for i in range(4)]
        o_ps = ps("o_ps", [P, 512])
        qk, maxed, exped, normed, v_steps, tr, tr_out, pv, o_out = (
            sem("qk"), sem("maxed"), sem("exped"), sem("normed"), sem("v"), sem("tr"), sem("tr_out"), sem("pv"), sem("o_out"))
        block = ctx.enter_context(nc.Block())

        @block.tensor
        def _(pe):
            def scores(i):
                h, t, k0, nk = items[i]
                r = h % 2
                for j, (k, n) in enumerate(chunks[i]):
                    if i >= 1:
                        pe.wait_ge(exped, min(first[i - 1] + j + 1, first[i]))
                    nc.tensor.matmul(s_ps[:, k * P:(k + n) * P], qT[64 * r:64 * r + HD, h // 2, t * P:(t + 1) * P],
                                     kT[64 * r:64 * r + HD, h // 4, (k0 + k) * P:(k0 + k + n) * P], start=True, stop=True).then_inc(qk, 1)

            def products(i):
                h, t, k0, nk = items[i]
                r = h % 2
                if i >= 2:
                    pe.wait_ge(o_out, i - 1)
                for j, (k, n) in enumerate(chunks[i]):
                    pe.wait_ge(tr_out, first[i] + j + 1)
                    for a in range(k, k + n):
                        m = nc.tensor.matmul(o_ps[64 * r:64 * r + HD, 0:P], v[:, k0 + a, (h // 4) * HD:(h // 4 + 1) * HD],
                                             pT[:, i % 2, a, :], start=(a == 0), stop=(a == nk - 1))
                m.then_inc(pv, 1)

            scores(0)
            for i in range(N):
                h, t, k0, nk = items[i]
                r = h % 2
                if i + 1 < N:
                    scores(i + 1)
                pe.wait_ge(normed, i + 1)
                for j, (k, n) in enumerate(chunks[i]):
                    c = first[i] + j
                    if c >= 4:
                        pe.wait_ge(tr_out, c - 3)
                    for a in range(n):
                        m = nc.tensor.transpose(t_ps[c % 4][:, a * P:(a + 1) * P], p[:, i % 2, (k + a) * P:(k + a + 1) * P],
                                                S["ident"][:, :])
                    m.then_inc(tr, 1)
                if i >= 1:
                    products(i - 1)
            products(N - 1)

        @block.scalar
        def _(act):
            def exps(i):
                h, t, k0, nk = items[i]
                act.wait_ge(maxed, i + 1)
                if i >= 2:
                    act.wait_ge(tr, first[i - 1])
                for j, (k, n) in enumerate(chunks[i]):
                    nc.scalar.activation(p[:, i % 2, k * P:(k + n) * P], s_ps[:, k * P:(k + n) * P], ACT.Exp, bias=nmax[:, i:i + 1],
                                         accum_out=part[:, i, j:j + 1]).then_inc(exped, 1)

            exps(0)
            for i in range(N):
                if i + 1 < N:
                    exps(i + 1)
                if i >= 2:
                    act.wait_ge(pv, i - 1)
                for j, (k, n) in enumerate(chunks[i]):
                    c = first[i] + j
                    act.wait_ge(tr, c + 1)
                    nc.scalar.activation(pT[:, i % 2, k:k + n, :].rearrange("p a c -> p (a c)"), t_ps[c % 4][:, 0:n * P],
                                         ACT.Copy).then_inc(tr_out, 1)

        @block.vector
        def _(dve):
            steps = Count(v_steps)

            def softmax(i):
                h, t, k0, nk = items[i]
                nch = len(chunks[i])
                for j, (k, n) in enumerate(chunks[i]):
                    dve.wait_ge(qk, first[i] + j + 1)
                    r = nc.vector.tensor_reduce(top[:, i, j:j + 1], s_ps[:, k * P:(k + n) * P], AX_X, ALU.max)
                steps.link(dve, r)
                nc.vector.tensor_reduce(nmax[:, i:i + 1], top[:, i, 0:nch], AX_X, ALU.max, negate=True).then_inc(maxed, 1)
                dve.wait_ge(exped, first[i + 1])
                steps.link(dve, nc.vector.reduce_sum(total[:, i:i + 1], part[:, i, 0:nch], AX_X))
                steps.link(dve, nc.vector.reciprocal(total[:, i:i + 1], total[:, i:i + 1]))
                nc.vector.tensor_scalar(p[:, i % 2, 0:nk * P], p[:, i % 2, 0:nk * P], total[:, i:i + 1], None, ALU.mult).then_inc(normed, 1)

            def output(i):
                h, t, _, _ = items[i]
                r = h % 2
                dve.wait_ge(pv, i + 1)
                nc.vector.tensor_copy(yT[64 * r:64 * r + HD, h // 2, t * P:(t + 1) * P], o_ps[64 * r:64 * r + HD, 0:P]).then_inc(o_out, 1)

            softmax(0)
            for i in range(N):
                if i + 1 < N:
                    softmax(i + 1)
                if i >= 1:
                    output(i - 1)
            output(N - 1)


def out_proj(nc, A, S, tag, w_dram, lhs, x_in, x_out, layer, lhs_dram=None):
    with ExitStack() as ctx:
        sb, ps, sem = scope(nc, ctx, tag)
        w = sb("w", [P, KD, D])
        gate = sb("gate", [P, 2, D])
        x = sb("x", [P, 3, D])
        psm = [ps(f"psm{i}", [P, D]) for i in range(4)]
        w_in = [sem(f"w_in{k}") for k in range(KD)]
        l_in = [sem(f"l_in{k}") for k in range(KD)]
        g_in, mm, v_steps, gated = sem("g_in"), sem("mm"), sem("v"), sem("gated")
        x_ins, stored = [sem(f"x_in{i}") for i in range(3)], [sem(f"stored{i}") for i in range(3)]
        block = ctx.enter_context(nc.Block())

        @block.sync
        def _(sp):
            for k in range(KD):
                sp.dma_start(w[:, k, :], w_dram[k * P:(k + 1) * P, :]).then_inc(w_in[k], 16)
                if lhs_dram is not None:
                    sp.dma_start(lhs(k), lhs_dram[k]).then_inc(l_in[k], 16)
            for c in range(2):
                sp.dma_start(gate[:, c, :], S["mod_dram"][layer, c:c + 1, 2 * D:3 * D].broadcast_to([P, D])).then_inc(g_in, 16)
            for t in range(NT):
                if t >= 3:
                    sp.wait_ge(stored[t % 3], 16 * (t // 3))
                sp.dma_start(x[:, t % 3, :], x_in(t)).then_inc(x_ins[t % 3], 16)

        @block.tensor
        def _(pe):
            for t in range(NT):
                if t >= 4:
                    pe.wait_ge(gated, t - 3)
                for k in range(KD):
                    if t == 0:
                        pe.wait_ge(w_in[k], 16)
                        if lhs_dram is not None:
                            pe.wait_ge(l_in[k], 16)
                    for h in range(2):
                        m = nc.tensor.matmul(psm[t % 4][:, h * 512:(h + 1) * 512], lhs(k)[:, t * P:(t + 1) * P],
                                             w[:, k, h * 512:(h + 1) * 512], start=(k == 0), stop=(k == KD - 1))
                m.then_inc(mm, 1)

        @block.vector
        def _(dve):
            dve.wait_ge(g_in, 32)
            for t in range(NT):
                dve.wait_ge(mm, t + 1)
                nc.vector.tensor_tensor(psm[t % 4][:, :], psm[t % 4][:, :], gate[:, 0 if t < CT else 1, :], ALU.mult).then_inc(v_steps, 1)
                dve.wait_ge(v_steps, t + 1)
                dve.wait_ge(x_ins[t % 3], 16 * (t // 3 + 1))
                nc.vector.tensor_tensor(x[:, t % 3, :], psm[t % 4][:, :], x[:, t % 3, :], ALU.add).then_inc(gated, 1)

        @block.scalar
        def _(act):
            for t in range(NT):
                act.wait_ge(gated, t + 1)
                act.dma_start(x_out(t), x[:, t % 3, :]).then_inc(stored[t % 3], 16)
            for i in range(3):
                act.wait_ge(stored[i], 16 * len(range(i, NT, 3)))


SW = 256


def load_expert(sp, A, layer, w, w_in, j, e):
    if j < 8:
        jj, part = divmod(j, 2)
        c0 = part * FH + jj * SW
        src = A["moe_w_gu"][layer][bass.ds(e, 1), :, c0:c0 + SW]
    else:
        src = A["moe_w_down"][layer][bass.ds(e, 1), :, (j - 8) * SW:(j - 7) * SW]
    sp.dma_start(w[:, j, :, :], src.rearrange("a (k p) n -> p (a k) n", p=P)).then_inc(w_in[j], 16)


def route(nc, A, S, tag, hnT, layer, idx, gates, expert_w, expert_w_in):
    with ExitStack() as ctx:
        sb, ps, sem = scope(nc, ctx, tag)
        w = sb("w", [P, KD, NE])
        lt = sb("lt", [P, 512])
        aff = sb("aff", [P, NT, NE])
        stat = sb("stat", [P, 2, NT])
        work = sb("work", [NE, T])
        top = sb("top", [NE, 2, max(CAP)])
        topi = sb("topi", [NE, 2, max(CAP)], U32)
        topf = sb("topf", [NE, 2, max(CAP)])
        lg = ps("lg", [P, 512])
        tok = ps("tok", [P, NT * NE])
        pa = [ps(f"pa{i}", [P, 512]) for i in range(3)]
        pt = ps("pt", [P, 4 * NE])
        w_in, mm, lt_out, tr, v_steps, subbed, exped, aff_ready, back, copied, picked, tr2 = (
            sem("w_in"), sem("mm"), sem("lt_out"), sem("tr"), sem("v"), sem("subbed"), sem("exped"), sem("aff_ready"),
            sem("back"), sem("copied"), sem("picked"), sem("tr2"))
        block = ctx.enter_context(nc.Block())

        @block.sync
        def _(sp):
            sp.dma_start(w[:, :, :], A["router_w"][layer].rearrange("(k p) e -> p k e", p=P)).then_inc(w_in, 16)
            for j in range(12):
                load_expert(sp, A, layer, expert_w, expert_w_in, j, 0)

        @block.tensor
        def _(pe):
            pe.wait_ge(w_in, 16)
            for k in range(KD):
                for g, (t0, n, _) in enumerate(PIECES):
                    m = nc.tensor.matmul(lg[32 * g:32 * g + NE, 0:n * P], w[:, k, :], hnT[:, k, t0 * P:(t0 + n) * P],
                                         start=(k == 0), stop=(k == KD - 1), tile_position=(0, 32 * g))
            m.then_inc(mm, 1)
            pe.wait_ge(lt_out, 1)
            for g, (t0, n, _) in enumerate(PIECES):
                q = slice(32 * g, 32 * g + NE)
                if g:
                    pe.wait_ge(tr, g)
                for t in range(n):
                    m = nc.tensor.transpose(tok[:, (t0 + t) * NE:(t0 + t + 1) * NE], lt[q, t * P:(t + 1) * P], S["ident"][q, q])
                m.then_inc(tr, 1)
            pe.wait_ge(aff_ready, 1)
            for g, (t0, n, _) in enumerate(PIECES):
                for t in range(n):
                    m = nc.tensor.transpose(pa[g][0:NE, t * P:(t + 1) * P], aff[:, t0 + t, :], S["ident"][:, :])
            m.then_inc(back, 1)
            pe.wait_ge(picked, 1)
            for c in range(2):
                cap = CAP[c]
                nc.tensor.transpose(pt[0:cap, (2 * c) * NE:(2 * c + 1) * NE], top[:, c, 0:cap], S["ident"][0:NE, 0:NE])
                m = nc.tensor.transpose(pt[0:cap, (2 * c + 1) * NE:(2 * c + 2) * NE], topf[:, c, 0:cap], S["ident"][0:NE, 0:NE])
            m.then_inc(tr2, 1)

        @block.scalar
        def _(act):
            act.wait_ge(subbed, 1)
            nc.scalar.activation(aff[:, :, :], aff[:, :, :], ACT.Exp).then_inc(exped, 1)

        @block.vector
        def _(dve):
            steps = Count(v_steps)
            dve.wait_ge(mm, 1)
            for g, (t0, n, _) in enumerate(PIECES):
                r = nc.vector.tensor_copy(lt[32 * g:32 * g + NE, 0:n * P], lg[32 * g:32 * g + NE, 0:n * P])
            r.then_inc(lt_out, 1)
            dve.wait_ge(tr, len(PIECES))
            logits = tok[:, :].rearrange("p (t e) -> p t e", e=NE)

            def per_token(j):
                return stat[:, j, :].rearrange("p (t a) -> p t a", a=1).broadcast_to([P, NT, NE])
            steps.link(dve, nc.vector.reduce_max(stat[:, 0, :], logits, AX_X))
            nc.vector.tensor_tensor(aff[:, :, :], logits, per_token(0), ALU.subtract).then_inc(subbed, 1)
            dve.wait_ge(exped, 1)
            steps.link(dve, nc.vector.reduce_sum(stat[:, 1, :], aff[:, :, :], AX_X))
            steps.link(dve, nc.vector.reciprocal(stat[:, 1, :], stat[:, 1, :]))
            nc.vector.tensor_tensor(aff[:, :, :], aff[:, :, :], per_token(1), ALU.mult).then_inc(aff_ready, 1)
            dve.wait_ge(back, 1)
            for g, (t0, n, _) in enumerate(PIECES):
                r = nc.vector.tensor_copy(work[:, t0 * P:(t0 + n) * P], pa[g][0:NE, 0:n * P])
            steps.link(dve, r)
            for c, (o, ln) in enumerate(SEQS):
                cols = work[:, o:o + ln]
                for r8 in range(0, CAP[c], 8):
                    t8 = top[:, c, r8:r8 + 8]
                    steps.link(dve, nc.vector.max(t8, cols))
                    nc.vector.max_index(topi[:, c, r8:r8 + 8], t8, cols)
                    steps.link(dve, nc.vector.match_replace(cols, t8, cols, -1.0))
            for c, (o, ln) in enumerate(SEQS):
                steps.link(dve, nc.vector.tensor_copy(topf[:, c, 0:CAP[c]], topi[:, c, 0:CAP[c]]))
                if c == 1:
                    steps.link(dve, nc.vector.tensor_scalar(topf[:, c, 0:CAP[c]], topf[:, c, 0:CAP[c]], float(o), None, ALU.add))
            nc.vector.tensor_copy(stat[:, 0, 0:1], stat[:, 1, 0:1]).then_inc(picked, 1)
            dve.wait_ge(tr2, 1)
            for c in range(2):
                cap = CAP[c]
                nc.vector.tensor_copy(gates[c][0:cap, :], pt[0:cap, (2 * c) * NE:(2 * c + 1) * NE])
                nc.vector.tensor_copy(idx[c][0:cap, :], pt[0:cap, (2 * c + 1) * NE:(2 * c + 2) * NE])


def experts(nc, A, S, tag, layer, xn_dram, y_dram, idx, gates, w, w_in):
    CP, CL = CAP
    CC = CP + CL
    with ExitStack() as ctx:
        sb, ps, sem = scope(nc, ctx, tag)
        xl, xc = sb("xl", [P, D]), sb("xc", [CP, D])
        xT = sb("xT", [P, KD, CC])
        sg = sb("sg", [P, 2, CC])
        hT = sb("hT", [P, KD, CC])
        ol, oc = sb("ol", [P, D]), sb("oc", [CP, D])
        icg, ics = [sb("icg0", [CP, 1], U32), sb("icg1", [P, 1], U32)], [sb("ics0", [CP, 1], U32), sb("ics1", [P, 1], U32)]
        zero = sb("zero", [P, D])
        pgu = [ps(f"pgu{i}", [P, CC]) for i in range(4)]
        pxt = ps("pxt", [P, 2 * CC])
        pol = [ps("pol0", [P, 512]), ps("pol1", [P, 512])]
        poc = ps("poc", [P, SW])
        xl_in, xc_in, gu_mm, silued, multiplied, tr, xT_out, ol_mm, oc_mm, ol_out, oc_out, l_added, c_added = (
            sem("xl_in"), sem("xc_in"), sem("gu_mm"), sem("silued"), sem("multiplied"), sem("tr"), sem("xT_out"),
            sem("ol_mm"), sem("oc_mm"), sem("ol_out"), sem("oc_out"), sem("l_added"), sem("c_added"))
        zeroed, y_zero, p_steps, o_free, issued = (
            sem("zeroed"), sem("y_zero"), sem("p_steps"), sem("o_free"), sem("issued"))
        block = ctx.enter_context(nc.Block())

        @block.sync
        def _(sp):
            with sp.Fori(1, NE) as e:
                for j in range(12):
                    if j < 8 and j % 2 == 0:
                        sp.wait_ge(gu_mm, e * 16 + (4 * (j // 2) + 4 - 16))
                    if j == 8:
                        sp.wait_ge(oc_mm, e)
                    load_expert(sp, A, layer, w, w_in, j, e)

        @block.gpsimd
        def _(pool):
            def gather(e, first=False):
                if not first:
                    pool.wait_ge(tr, e * 4)
                    pool.wait_ge(xl_in, e * 16)
                    pool.wait_ge(xc_in, e * 16)
                nc.gpsimd.tensor_copy(icg[0][:, :], idx[0][0:CP, bass.ds(e, 1)])
                nc.gpsimd.tensor_copy(icg[1][:, :], idx[1][:, bass.ds(e, 1)]).then_inc(p_steps, 1)
                pool.wait_ge(p_steps, 1 if first else e * 2)
                pool.sem_inc(issued, 1)
                pool.indirect_dma_start(xc[:, :], None, xn_dram, bass.IndirectOffsetOnAxis(icg[0][:, 0:1], 0)).then_inc(xc_in, 16)
                pool.indirect_dma_start(xl[:, :], None, xn_dram, bass.IndirectOffsetOnAxis(icg[1][:, 0:1], 0)).then_inc(xl_in, 16)

            def scatter(e):
                nc.gpsimd.tensor_copy(ics[0][:, :], idx[0][0:CP, bass.ds(e, 1)])
                nc.gpsimd.tensor_copy(ics[1][:, :], idx[1][:, bass.ds(e, 1)]).then_inc(p_steps, 1)
                pool.wait_ge(p_steps, e * 2 + 3 if not isinstance(e, int) or e < NE - 1 else 2 * NE)
                pool.wait_ge(ol_out, e * 2 + 4)
                pool.sem_inc(issued, 1)
                pool.indirect_dma_start(y_dram, bass.IndirectOffsetOnAxis(ics[1][:, 0:1], 0), ol[:, :], None,
                                        compute_op=ALU.add).then_inc(l_added, 16)
                pool.wait_ge(oc_out, e + 2)
                pool.sem_inc(issued, 1)
                pool.indirect_dma_start(y_dram, bass.IndirectOffsetOnAxis(ics[0][:, 0:1], 0), oc[:, :], None,
                                        compute_op=ALU.add).then_inc(c_added, 16)
                pool.wait_ge(l_added, e * 16 + 16)
                pool.wait_ge(c_added, e * 16 + 16)
                pool.sem_inc(o_free, 1)

            nc.gpsimd.memset(zero[:, :], 0.0).then_inc(zeroed, 1)
            pool.sem_inc(o_free, 1)
            gather(0, first=True)
            pool.wait_ge(y_zero, 16 * NT)
            with pool.Fori(0, NE - 1) as e:
                gather(e + 1)
                scatter(e)
            scatter(NE - 1)

        @block.tensor
        def _(pe):
            def transposes(e, g):
                for j in range(2):
                    k = 2 * g + j
                    nc.tensor.transpose(pxt[:, j * CC:j * CC + CL], xl[:, k * P:(k + 1) * P], S["ident"][:, :])
                    m = nc.tensor.transpose(pxt[:, j * CC + CL:(j + 1) * CC], xc[:, k * P:(k + 1) * P], S["ident"][0:CP, 0:CP])
                m.then_inc(tr, 1)

            def expert(e, last):
                for f in range(FH // P):
                    for part in range(2):
                        j = 2 * (f // 2) + part
                        if f % 2 == 0:
                            pe.wait_ge(w_in[j], e * 16 + 16)
                        if f == 0 and part == 0:
                            pe.wait_ge(xT_out, e * 4 + 4)
                        pe.wait_ge(multiplied if part else silued, e * 8 + (f + 1))
                        for k in range(KD):
                            m = nc.tensor.matmul(pgu[2 * (f % 2) + part][:, :], w[:, j, k, (f % 2) * P:(f % 2 + 1) * P], xT[:, k, :],
                                                 start=(k == 0), stop=(k == KD - 1))
                        m.then_inc(gu_mm, 1)
                pe.wait_ge(multiplied, e * 8 + 10)
                if not last:
                    pe.wait_ge(xl_in, e * 16 + 32)
                    pe.wait_ge(xc_in, e * 16 + 32)
                for q in range(4):
                    pe.wait_ge(w_in[8 + q], e * 16 + 16)
                    if q % 2 == 0:
                        pe.wait_ge(ol_out, e * 2 + (q // 2 + 1))
                    for k in range(KD):
                        m = nc.tensor.matmul(pol[q // 2][:, (q % 2) * SW:(q % 2 + 1) * SW], hT[:, k, 0:CL], w[:, 8 + q, k, :],
                                             start=(k == 0), stop=(k == KD - 1))
                    if q % 2:
                        m.then_inc(ol_mm, 1)
                    if not last:
                        pe.wait_ge(xT_out, e * 4 + (4 + q))
                        transposes(e + 1, q)
                pe.wait_ge(oc_out, e + 1)
                for k in range(KD):
                    for q in range(4):
                        m = nc.tensor.matmul(poc[32 * q:32 * q + CP, :], hT[:, k, CL:CC], w[:, 8 + q, k, :],
                                             start=(k == 0), stop=(k == KD - 1), tile_position=(0, 32 * q))
                m.then_inc(oc_mm, 1)

            pe.wait_ge(xl_in, 16)
            pe.wait_ge(xc_in, 16)
            for g in range(4):
                if g:
                    pe.wait_ge(xT_out, g)
                transposes(0, g)
            with pe.Fori(0, NE - 1) as e:
                expert(e, False)
            expert(NE - 1, True)

        mc = S["modcol"]

        @block.scalar
        def _(act):
            def to_xT(e, g):
                act.wait_ge(tr, e * 4 + (g + 1))
                for j in range(2):
                    k = 2 * g + j
                    for c, c0, n in ((1, 0, CL), (0, CL, CP)):
                        r = nc.scalar.activation(xT[:, k, c0:c0 + n], pxt[:, j * CC + c0:j * CC + c0 + n], ACT.Identity,
                                                 bias=mc[:, layer, 3, c, k:k + 1], scale=mc[:, layer, 4, c, k:k + 1])
                r.then_inc(xT_out, 1)

            def expert(e, last):
                for f in range(FH // P):
                    act.wait_ge(multiplied, e * 8 + (f + 1))
                    act.wait_ge(gu_mm, e * 16 + (2 * f + 1))
                    nc.scalar.activation(sg[:, f % 2, :], pgu[2 * (f % 2)][:, :], ACT.Silu).then_inc(silued, 1)
                if not last:
                    for g in range(4):
                        to_xT(e + 1, g)

            act.sem_inc(silued, 2)
            act.wait_ge(zeroed, 1)
            for t in range(NT):
                act.dma_start(y_dram[t * P:(t + 1) * P, :], zero[:, :]).then_inc(y_zero, 16)
            for g in range(4):
                to_xT(0, g)
            with act.Fori(0, NE - 1) as e:
                expert(e, False)
            expert(NE - 1, True)

        @block.vector
        def _(dve):
            dve.sem_inc(multiplied, 2)
            dve.sem_inc(ol_out, 2)
            dve.sem_inc(oc_out, 1)
            with dve.Fori(0, NE) as e:
                for f in range(FH // P):
                    dve.wait_ge(silued, e * 8 + (f + 3))
                    dve.wait_ge(gu_mm, e * 16 + (2 * f + 2))
                    nc.vector.tensor_tensor(hT[:, f, :], sg[:, f % 2, :], pgu[2 * (f % 2) + 1][:, :], ALU.mult).then_inc(multiplied, 1)
                dve.wait_ge(o_free, e + 1)
                for b in range(2):
                    dve.wait_ge(ol_mm, e * 2 + (b + 1))
                    nc.vector.tensor_scalar(ol[:, b * 512:(b + 1) * 512], pol[b][:, :], gates[1][:, bass.ds(e, 1)], None,
                                            ALU.mult).then_inc(ol_out, 1)
                dve.wait_ge(oc_mm, e + 1)
                for q in range(4):
                    r = nc.vector.tensor_scalar(oc[:, q * SW:(q + 1) * SW], poc[32 * q:32 * q + CP, :], gates[0][0:CP, bass.ds(e, 1)], None,
                                                ALU.mult)
                r.then_inc(oc_out, 1)


LEVELS = (64, 32, 16, 8)
FLOOR = -20.0
SIG_FLOOR = -40.0
RT = RH * RD
L64, INTER, L32, L16, L8, DQ, DK = range(7)
ITEM_LEVEL = {L64: 64, L32: 32, L16: 16, L8: 8}
ITEM_BUF = {L64: 2, INTER: 3, L32: 4, L16: 0, L8: 1, DQ: 2, DK: 3}
USES = [(d, i) for d in range(2) for i in (L64, L32, INTER, L16, L8, DK)] + ["o", "yT"]
NU = len(USES)
BANKS = [(0, 4), (4, 4), (8, 2)]
PARTS = ("q", "f0", "f1")
NZU = NT // 2
NP_STEPS = 3 * NZU + NT


def rec_order():
    def unit(h, d, ps, tail):
        nh, nd = (h, 1) if d == 0 else (h + 1, 0)
        here = lambda *toks: [(h, t) for t in toks]
        following = lambda *kinds: [(nh, (k, nd)) for k in kinds if nh < RH]
        proj = lambda i: [((h, ("p", n - NP_STEPS)) if n >= NP_STEPS else (h + 1, ("p", n))) for n in ps[i] if n >= NP_STEPS or h + 1 < RH]
        o = here(*([("z_last",)] if h == RH - 1 and d == 0 else [])) + here(("post", d, L64)) + proj(0) + here(("prod", d, L64), ("pre", d, L32), ("post", d, INTER), ("kt", d)) + proj(1)
        o += here(("pre", d, L16), ("post", d, L32), ("fin", d, L64)) + proj(2)
        o += here(("prod", d, L32), ("pre", d, L8), ("post", d, L16)) + following("sig")
        o += here(("fin", d, L32)) + proj(3) + here(("prod", d, INTER), ("pre", d, DQ), ("post", d, L8), ("pre", d, DK))
        o += here(("fin", d, INTER)) + following("fk") + proj(4) + here(("prod", d, L16), ("post", d, DQ), ("post", d, DK))
        o += following("logf") + here(("fin", d, L16)) + proj(5) + here(("prod", d, L8))
        o += here(("fin", d, L8)) + proj(6) + here(("prod", d, DK))
        if d == 0:
            return o + proj(8) + following("scan") + here(("fin", d, DK)) + following("etot") + proj(7) + [(nh, ("pre", nd, L64)), (nh, ("pre", nd, INTER))]
        last = h == RH - 1
        o += ([] if last else [(nh, ("q",))]) + here(("g",)) + ([] if last else [(nh, ("q_ln",))]) + here(("g_ln",), ("fin", d, DK))
        o += [(h + 1, ("p", n)) for n in tail[0] if not last] + here(("prod_o",))
        o += following("scan", "etot") + ([] if last else [(nh, ("q_sig",))]) + here(("g_sig",), ("fin_o",)) + here(("gate",), ("norm",))
        o += [(h + 1, ("p", n)) for n in tail[1] if not last]
        o += ([] if last else [(nh, ("pre", nd, L64)), (nh, ("pre", nd, INTER))])
        return o + here(("y",), ("prod_y",), ("fin_y",)) + [(h + 1, ("p", n)) for n in tail[2] if not last]

    o = [(0, ("p", n)) for n in range(11)] + [(0, ("q",)), (0, ("q_ln",))] + [(0, (k, 0)) for k in ("sig", "fk", "logf", "scan")]
    o += [(0, ("q_sig",)), (0, ("etot", 0))] + [(0, ("p", n)) for n in range(11, 18)] + [(0, ("pre", 0, L64)), (0, ("pre", 0, INTER))]
    for h in range(RH):
        ps0 = [[0], [1], [2], [3], [4, 5], [], [], [9, 10], [6, 7, 8]]
        if h == 0:
            ps0[0:2] = [[NP_STEPS + n for n in range(18, 21)], [NP_STEPS + n for n in range(21, NP_STEPS)] + [0, 1]]
        o += unit(h, 0, ps0, None) + unit(h, 1, [[11], [12], [13], [14], [15, 16], [], []], [[17, 18], [19, 20, 21], [22, 23, 24]])
    return o


def recurrence(nc, A, S, hnT, y_dram, out_state):
    with ExitStack() as ctx:
        sb, ps, sem = scope(nc, ctx, "rec")
        U8 = mybir.dt.uint8
        w = sb("w", [P, KD, 5, RD])
        zc = sb("zc", [P, 2, 3, T])
        zv = sb("zv", [P, 2, NT, RD])
        zg = sb("zg", [P, 2, NT, RD])
        kk = sb("kk", [P, T])
        X, X8 = sb("X", [P, T]), sb("X8", [P, T])
        ring = sb("ring", [P, 5, T])
        Qi = sb("Qi", [P, 2, T])
        St = sb("St", [P, 2, NT, RD])
        kT = sb("kT", [P, NT, RD])
        AT = sb("AT", [P, NT, P])
        dtmp = sb("dtmp", [P, 4, P])
        y = sb("y", [P, NT, RD])
        fin = sb("fin", [P, 2, RD])
        s0 = sb("s0", [P, 2, 2, RD])
        tot, etot, tot8 = sb("tot", [P, NT, 2]), sb("etot", [P, NT, 2]), sb("tot8", [P, NT, 2])
        decay = sb("decay", [P, NT])
        ms = sb("ms", [P, NT])
        restart = sb("restart", [P, T], U8)
        maskb = sb("maskb", [P, 8, P], U8)
        maskf = sb("maskf", [P, 2, P])
        lb = sb("lb", [P, 2, RH])
        oml = sb("oml", [P, 2, RH])
        lbt = sb("lbt", [P, 2, RH])
        pz = [ps(f"pz{i}", [P, 512]) for i in range(3)]
        pk = [ps(f"pk{i}", [P, 512]) for i in range(2)]
        pg = [ps(f"pg{i}", [P, 512]) for i in range(3)]
        w_in, s0_in, consts, fin_out, y_out = (
            [sem(f"w_in{j}") for j in range(5)], [sem("s0_in0"), sem("s0_in1")], sem("consts"), sem("fin_out"), sem("y_out"))
        (z_mm, z_out, v_steps, lb_e, lb_d, q_clamped, q_sig, zc_clamped, f_exp, f_ready, log_f, x_ready,
         tot_e, pre, exped, post, k_tr, kT_out, g_full, g_free, g_clamped, g_sig, o_out, o_sq, ms_ready, rstd, y_ready,
         yT_ready, fin_ready) = (sem(n) for n in (
             "z_mm z_out v lb_e lb_d q_clamped q_sig zc_clamped f_exp f_ready log_f x_ready tot_e pre exped "
             "post k_tr kT_out g_full g_free g_clamped g_sig o_out o_sq ms_ready rstd y_ready yT_ready fin_ready").split())
        a_steps = sem("a")
        block = ctx.enter_context(nc.Block())
        ORDER = rec_order()

        def blocks(x, h):
            return x.rearrange("p (b s h) -> p b s h", s=2, h=h)

        def qhalf(d):
            return 1 - d

        def reference(x, d, h):
            b = blocks(x, h)
            return b[:, :, d, h - 1:h] if d == 0 else b[:, :, d, 0:1]

        def totals(x, d):
            b = blocks(x, 64)
            return b[:, :, :, 63] if d == 0 else b[:, :, :, 0]

        def use(h, key):
            return NU * h + USES.index(key)

        def unit_before(h, d):
            return (h, 0) if d else (h - 1, 1)

        @block.sync
        def _(sp):
            sp.dma_start(ring[:, 0, 0:8 * P], A["k_maskb"].rearrange("p m c -> p (m c)")).then_inc(consts, 16)
            sp.dma_start(maskf[:, :, :], A["k_maskf"]).then_inc(consts, 16)
            for h in range(RH):
                for j, part in enumerate((0, 2, 3, 1, 4)):
                    if h:
                        sp.wait_ge(z_mm, NP_STEPS * (h - 1) + (NZU * (j + 1) if j < 3 else NP_STEPS))
                    sp.dma_start(w[:, :, j, :], A["r_w_in"][0, :, part * D + h * RD:part * D + (h + 1) * RD]
                                 .rearrange("(k p) n -> p k n", p=P)).then_inc(w_in[j], 16)
                if h >= 2:
                    sp.wait_ge(g_free, 3 * use(h - 2, (1, INTER)) + 3)
                sp.dma_start(s0[:, h % 2, :, :], A["state_rec"][0, 0, :, h].rearrange("s d e -> d s e")).then_inc(s0_in[h % 2], 16)

        @block.gpsimd
        def _(pool):
            for h in range(RH):
                for d in range(2):
                    pool.wait_ge(fin_ready, 2 * h + d + 1)
                    pool.dma_start(out_state[d, h], fin[:, d, :]).then_inc(fin_out, 16)
                pool.wait_ge(yT_ready, 3 * (h + 1))
                pool.dma_start(y_dram[h], ring[:, 1, :]).then_inc(y_out, 16)
            pool.wait_ge(fin_out, 32 * RH)
            pool.wait_ge(y_out, 16 * RH)

        @block.tensor
        def _(pe):
            def project(h, n):
                i = NP_STEPS * h + n
                if n in (0, NZU, 2 * NZU):
                    pe.wait_ge(w_in[n // NZU], 16 * (h + 1))
                if n == 3 * NZU:
                    pe.wait_ge(w_in[3], 16 * (h + 1))
                    pe.wait_ge(w_in[4], 16 * (h + 1))
                if i >= 3:
                    pe.wait_ge(z_out, i - 2)
                for k in range(KD):
                    if n < 3 * NZU:
                        c0 = n % NZU * 2 * P
                        m = nc.tensor.matmul(pz[i % 3][:, 0:2 * P], w[:, k, n // NZU, :], hnT[:, k, c0:c0 + 2 * P],
                                             start=(k == 0), stop=(k == KD - 1))
                    else:
                        t = n - 3 * NZU
                        m = nc.tensor.matmul(pz[i % 3][:, 0:2 * RD], hnT[:, k, t * P:(t + 1) * P],
                                             w[:, k, 3:5, :].rearrange("p a c -> p (a c)"), start=(k == 0), stop=(k == KD - 1))
                m.then_inc(z_mm, 1)

            def into_banks(h, key, mm):
                u = use(h, key)
                for b, (t0, nt) in enumerate(BANKS):
                    if u:
                        pe.wait_ge(g_free, 3 * (u - 1) + b + 1)
                    for t in range(t0, t0 + nt):
                        m = mm(pg[b][:, (t - t0) * P:(t - t0 + 1) * P], t)
                    m.then_inc(g_full, 1)

            def step(h, tok):
                kind = tok[0]
                if kind == "p":
                    project(h, tok[1])
                elif kind == "prod" and tok[2] == INTER:
                    d = tok[1]
                    pe.wait_ge(z_out, NP_STEPS * (h + 1))
                    pe.wait_ge(kT_out, 3 * (2 * h + d + 1))
                    into_banks(h, (d, INTER), lambda o, t: nc.tensor.matmul(o, kT[:, t, :], zv[:, h % 2, t, :], start=True, stop=True))
                elif kind == "prod":
                    d, i = tok[1:]
                    pe.wait_ge(post, 7 * (2 * h + d) + i + 1)
                    kb, qb = ring[:, ITEM_BUF[i], :], ring[:, ITEM_BUF[DQ if i == DK else i], :]
                    into_banks(h, (d, i), lambda o, t: nc.tensor.matmul(o, kb[:, t * P:(t + 1) * P], qb[:, t * P:(t + 1) * P],
                                                                       start=True, stop=True))
                elif kind == "kt":
                    d = tok[1]
                    n = 3 * (2 * h + d)
                    pe.wait_ge(post, 7 * (2 * h + d) + INTER + 1)
                    for b, (t0, nt) in enumerate(BANKS):
                        if n + b >= 2:
                            pe.wait_ge(kT_out, n + b - 1)
                        for t in range(t0, t0 + nt):
                            m = nc.tensor.transpose(pk[(n + b) % 2][:, (t - t0) * P:(t - t0 + 1) * P],
                                                    ring[:, ITEM_BUF[INTER], t * P:(t + 1) * P], S["ident"][:, :])
                        m.then_inc(k_tr, 1)
                elif kind == "prod_o":
                    pe.wait_ge(g_free, 3 * use(h, (1, DK)) + 3)

                    def mm(o, t):
                        nc.tensor.matmul(o, AT[:, t, :], zv[:, h % 2, t, :], start=True, stop=False)
                        nc.tensor.matmul(o, Qi[:, 0, t * P:(t + 1) * P], St[:, 0, t, :], start=False, stop=False)
                        return nc.tensor.matmul(o, Qi[:, 1, t * P:(t + 1) * P], St[:, 1, t, :], start=False, stop=True)
                    into_banks(h, "o", mm)
                elif kind == "prod_y":
                    pe.wait_ge(y_ready, h + 1)
                    into_banks(h, "yT", lambda o, t: nc.tensor.transpose(o, y[:, t, :], S["ident"][:, :]))

            for h, tok in ORDER:
                step(h, tok)

        @block.scalar
        def _(act):
            chain = Count(a_steps)

            def z_copy(h, n):
                i = NP_STEPS * h + n
                act.wait_ge(z_mm, i + 1)
                if n == 0 and h >= 2:
                    act.wait_ge(post, 14 * (h - 1))
                    act.wait_ge(g_full, 3 * use(h - 2, "o") + 3)
                    act.wait_ge(y_ready, h - 1)
                if n < 3 * NZU:
                    c0 = n % NZU * 2 * P
                    nc.scalar.activation(zc[:, h % 2, n // NZU, c0:c0 + 2 * P], pz[i % 3][:, 0:2 * P], ACT.Copy).then_inc(z_out, 1)
                else:
                    chain.link(act, nc.scalar.activation(zv[:, h % 2, n - 3 * NZU, :], pz[i % 3][:, 0:RD], ACT.Copy))
                    nc.scalar.activation(zg[:, h % 2, n - 3 * NZU, :], pz[i % 3][:, RD:2 * RD], ACT.Copy).then_inc(z_out, 1)

            def exp_neg(x):
                chain.link(act, nc.scalar.activation(x, x, ACT.Exp, scale=-1.0))

            def step(h, tok):
                kind = tok[0]
                d = tok[1] if len(tok) > 1 and kind != "p" else 0
                n2 = 2 * h + d
                z = zc[:, h % 2, 1 + d, :]
                r4 = ring[:, 4, :]
                if kind == "p":
                    i = NP_STEPS * h + tok[1] - 1
                    if i >= 0:
                        z_copy(i // NP_STEPS, i % NP_STEPS)
                elif kind == "z_last":
                    z_copy(h, NP_STEPS - 1)
                elif kind == "q":
                    act.wait_ge(q_clamped, h + 1)
                    exp_neg(ring[:, 1, :])
                elif kind == "q_ln":
                    chain.give(nc.scalar.activation(ring[:, 1, :], ring[:, 1, :], ACT.Ln, bias=1.0))
                elif kind == "q_sig":
                    chain.wait(act)
                    nc.scalar.activation(ring[:, 1, :], ring[:, 1, :], ACT.Exp, scale=-1.0).then_inc(q_sig, 1)
                elif kind == "g":
                    act.wait_ge(g_clamped, h + 1)
                    exp_neg(ring[:, 2, :])
                elif kind == "g_ln":
                    chain.give(nc.scalar.activation(ring[:, 2, :], ring[:, 2, :], ACT.Ln, bias=1.0))
                elif kind == "g_sig":
                    chain.wait(act)
                    nc.scalar.activation(ring[:, 2, :], ring[:, 2, :], ACT.Exp, scale=-1.0).then_inc(g_sig, 1)
                elif kind == "sig":
                    act.wait_ge(zc_clamped, n2 + 1)
                    if n2:
                        uh, ud = unit_before(h, d)
                        act.wait_ge(g_full, 3 * use(uh, (ud, L32)) + 3)
                    chain.link(act, nc.scalar.activation(r4, z, ACT.Exp, scale=-1.0))
                    chain.link(act, nc.scalar.activation(z, r4, ACT.Ln, bias=1.0))
                    nc.scalar.activation(z, z, ACT.Exp, scale=-1.0).then_inc(f_exp, 1)
                elif kind == "logf":
                    act.wait_ge(f_ready, n2 + 1)
                    nc.scalar.activation(z, z, ACT.Ln).then_inc(log_f, 1)
                elif kind == "etot":
                    act.wait_ge(x_ready, n2 + 1)
                    nc.scalar.activation(etot[:, :, :], tot[:, :, :], ACT.Exp).then_inc(tot_e, 1)
                elif kind == "pre":
                    d, i = tok[1:]
                    act.wait_ge(pre, 7 * n2 + i + 1)
                    r = ring[:, ITEM_BUF[i], :]
                    nc.scalar.activation(r, r, ACT.Exp).then_inc(exped, 1)
                elif kind == "kt":
                    for b, (t0, nt) in enumerate(BANKS):
                        n = 3 * n2 + b
                        act.wait_ge(k_tr, n + 1)
                        if n2 and b == 0:
                            act.wait_ge(g_full, 3 * use((n2 - 1) // 2, ((n2 - 1) % 2, INTER)) + 3)
                        nc.scalar.activation(kT[:, t0:t0 + nt, :].rearrange("p t c -> p (t c)"), pk[n % 2][:, 0:nt * P],
                                             ACT.Copy).then_inc(kT_out, 1)
                elif kind == "norm":
                    act.wait_ge(o_out, h + 1)
                    nc.scalar.activation(ring[:, 3, :], y[:, :, :].rearrange("p t e -> p (t e)"), ACT.Square).then_inc(o_sq, 1)
                    act.wait_ge(ms_ready, h + 1)
                    chain.link(act, nc.scalar.activation(ms[:, :], ms[:, :], ACT.Ln))
                    nc.scalar.activation(ms[:, :], ms[:, :], ACT.Exp, scale=-0.5).then_inc(rstd, 1)

            act.wait_ge(lb_d, 1)
            nc.scalar.activation(lbt[:, :, :], lbt[:, :, :], ACT.Exp).then_inc(lb_e, 1)
            for h, tok in ORDER:
                step(h, tok)

        @block.vector
        def _(dve):
            steps = Count(v_steps)
            TT, TS, STT = nc.vector.tensor_tensor, nc.vector.tensor_scalar, nc.vector.scalar_tensor_tensor

            def wide(x, n):
                return x.broadcast_to([P, x.shape[1], n])

            def take(h, key, b):
                dve.wait_ge(g_full, 3 * use(h, key) + b + 1)

            def states(h, d):
                take(h, (d, INTER), 2)
                dve.wait_ge(s0_in[h % 2], 16 * (h // 2 + 1))
                if h and d == 0:
                    dve.wait_ge(g_full, 3 * use(h - 1, "o") + 3)
                for o, ln in SEQS:
                    tiles = list(range(o // P, (o + ln) // P))
                    if d:
                        tiles.reverse()
                    if o == 0:
                        r = nc.vector.memset(St[:, d, tiles[0], :], 0.0)
                    else:
                        r = nc.vector.tensor_copy(St[:, d, tiles[0], :], s0[:, h % 2, d, :])
                    steps.link(dve, r)
                    for j, t in enumerate(tiles):
                        if j + 1 < len(tiles):
                            dst = St[:, d, tiles[j + 1], :]
                        elif o == 0:
                            dst = fin[:, d, :]
                            if h:
                                dve.wait_ge(fin_out, 32 * h)
                        else:
                            break
                        b = t // 4
                        r = STT(dst, St[:, d, t, :], decay[:, t:t + 1], pg[b][:, (t - 4 * b) * P:(t - 4 * b + 1) * P], ALU.mult, ALU.add)
                        if j + 1 < len(tiles):
                            steps.link(dve, r)
                        else:
                            r.then_inc(fin_ready, 1)
                steps.link(dve, TS(tot8[:, 0, :], tot8[:, 0, :], 1.0, None, ALU.mult))
                nc.vector.tensor_copy(tot8[:, 1, :], tot8[:, 0, :]).then_inc(g_free, 3)

            def step(h, tok):
                kind = tok[0]
                if kind == "p":
                    return
                d = tok[1] if len(tok) > 1 and kind != "p" else 0
                n2 = 2 * h + d
                q = zc[:, h % 2, 0, :]
                k = kk[:, :]
                z = zc[:, h % 2, 1 + d, :]
                r0, r1 = ring[:, 0, :], ring[:, 1, :]
                qh, kh = qhalf(d), d
                r4 = ring[:, 4, :]
                if kind == "q":
                    dve.wait_ge(z_out, NP_STEPS * h + NZU)
                    if h:
                        dve.wait_ge(g_full, 3 * use(h - 1, (1, L8)) + 3)
                    TS(r1, q, SIG_FLOOR, None, ALU.max).then_inc(q_clamped, 1)
                elif kind == "q_sig":
                    dve.wait_ge(q_sig, h + 1)
                    steps.link(dve, TT(q, q, r1, ALU.mult))
                elif kind == "sig":
                    dve.wait_ge(z_out, NP_STEPS * h + NZU * (2 + d))
                    TS(z, z, SIG_FLOOR, None, ALU.max).then_inc(zc_clamped, 1)
                elif kind == "fk":
                    dve.wait_ge(f_exp, n2 + 1)
                    steps.link(dve, TT(r4, r4, z, ALU.mult))
                    TS(z, z, oml[:, d, h:h + 1], lb[:, d, h:h + 1], ALU.mult, ALU.add).then_inc(f_ready, 1)
                elif kind == "scan":
                    if n2:
                        dve.wait_ge(post, 7 * n2)
                    steps.link(dve, TS(k, r4, oml[:, d, h:h + 1], None, ALU.mult))
                    dve.wait_ge(log_f, n2 + 1)
                    steps.link(dve, TS(r4, z, FLOOR, None, ALU.max))
                    steps.give(nc.vector.tensor_tensor_scan(X[:, :], restart[:, :], z, 0.0, ALU.mult, ALU.add))
                    steps.link(dve, nc.vector.tensor_tensor_scan(X8[:, :], restart[:, :], r4, 0.0, ALU.mult, ALU.add))
                    if d == 1:
                        for x, g, tt in ((X[:, :], z, tot), (X8[:, :], r4, tot8)):
                            steps.link(dve, nc.vector.tensor_copy(tt[:, :, :], totals(x, 0)))
                            steps.link(dve, STT(x, x, -1.0, g, ALU.mult, ALU.add))
                            xv = x.rearrange("p (b h) -> p b h", h=64)
                            steps.link(dve, TT(xv, xv, wide(tt[:, :, :].rearrange("p t (s a) -> p (t s) a", a=1), 64), ALU.add))
                    nc.vector.tensor_copy(tot[:, :, :], totals(X[:, :], d)).then_inc(x_ready, 1)
                elif kind == "etot":
                    dve.wait_ge(tot_e, n2 + 1)
                    steps.link(dve, TT(decay[:, :], etot[:, :, 0], etot[:, :, 1], ALU.mult))
                elif kind == "pre":
                    i = tok[2]
                    r = ring[:, ITEM_BUF[i], :]
                    if i == L64 and n2:
                        dve.wait_ge(g_full, 3 * use((n2 - 1) // 2, ((n2 - 1) % 2, DK)) + 3)
                    if i == L32 and n2:
                        dve.wait_ge(g_full, 3 * use((n2 - 1) // 2, ((n2 - 1) % 2, L32)) + 3)
                    if i == L8 and h and d == 0:
                        dve.wait_ge(y_out, 16 * h)
                    if i == DQ:
                        dve.wait_ge(g_full, 3 * use(h, (d, L64)) + 3)
                    if i == DK:
                        dve.wait_ge(k_tr, 3 * (n2 + 1))
                    if i in (DQ, DK):
                        b8 = X8[:, :].rearrange("p (b h) -> p b h", h=8)
                        m = 3 + d
                        ref = wide(b8[:, :, m:m + 1], 8)
                        rb = r.rearrange("p (b h) -> p b h", h=8)
                        last = TT(rb, b8, ref, ALU.subtract) if i == DQ else TT(rb, ref, b8, ALU.subtract)
                    else:
                        hh = 64 if i == INTER else ITEM_LEVEL[i]
                        xb, rb = blocks(X[:, :], hh), blocks(r, hh)
                        ref = wide(reference(X[:, :], d, hh), hh)
                        if i == INTER:
                            own = xb[:, :, qh, 63:64] if d == 0 else xb[:, :, qh, 0:1]
                            nc.vector.tensor_copy(rb[:, :, kh, :], xb[:, :, kh, :])
                            last = TT(rb[:, :, qh, :], wide(own, 64), xb[:, :, qh, :], ALU.subtract)
                        else:
                            if i == L64:
                                nc.vector.tensor_copy(rb[:, :, qh, :], xb[:, :, qh, :])
                            else:
                                TT(rb[:, :, qh, :], xb[:, :, qh, :], ref, ALU.subtract)
                            last = TT(rb[:, :, kh, :], ref, xb[:, :, kh, :], ALU.subtract)
                    last.then_inc(pre, 1)
                elif kind == "post":
                    i = tok[2]
                    r = ring[:, ITEM_BUF[i], :]
                    dve.wait_ge(exped, 7 * n2 + i + 1)
                    if i in (DQ, DK):
                        last = TT(r, r, q if i == DQ else k, ALU.mult)
                    elif i == INTER:
                        if h and d == 0:
                            dve.wait_ge(g_full, 3 * use(h - 1, "o") + 3)
                        rb, qb, kb, w64, qi = (blocks(a, 64) for a in (r, q, k, ring[:, ITEM_BUF[L64], :], Qi[:, d, :]))
                        e = etot[:, :, :]
                        dve.wait_ge(post, 7 * n2 + L64 + 1)
                        steps.give(TT(qi[:, :, kh, :], qb[:, :, kh, :], rb[:, :, kh, :], ALU.mult))
                        steps.give(TT(qi[:, :, qh, :], w64[:, :, qh, :], wide(e[:, :, kh:kh + 1], 64), ALU.mult))
                        steps.wait(dve)
                        TT(rb[:, :, qh, :], kb[:, :, qh, :], rb[:, :, qh, :], ALU.mult)
                        last = TT(rb[:, :, kh, :], w64[:, :, kh, :], wide(e[:, :, qh:qh + 1], 64), ALU.mult)
                    else:
                        hh = ITEM_LEVEL[i]
                        rb, qb, kb = (blocks(a, hh) for a in (r, q, k))
                        TT(rb[:, :, qh, :], rb[:, :, qh, :], qb[:, :, qh, :], ALU.mult)
                        last = TT(rb[:, :, kh, :], rb[:, :, kh, :], kb[:, :, kh, :], ALU.mult)
                    last.then_inc(post, 1)
                elif kind == "fin" and tok[2] == INTER:
                    states(h, d)
                elif kind == "fin":
                    i = tok[2]
                    if d == 0 and i == L64 and h:
                        dve.wait_ge(g_full, 3 * use(h - 1, "o") + 3)
                    for b, (t0, nt) in enumerate(BANKS):
                        take(h, (d, i), b)
                        src = pg[b][:, 0:nt * P].rearrange("p (t c) -> p t c", c=P)
                        at = AT[:, t0:t0 + nt, :]
                        if d == 0 and i == L64:
                            last = TT(at, src, maskf[:, 0:1, :].broadcast_to([P, nt, P]), ALU.mult)
                        elif d == 1 and i == DK:
                            if b:
                                dve.wait_ge(g_free, 3 * use(h, (d, i)) + b)
                            steps.link(dve, TT(dtmp[:, 0:nt, :], src, maskf[:, 1:2, :].broadcast_to([P, nt, P]), ALU.mult))
                            last = TT(at, at, dtmp[:, 0:nt, :], ALU.add)
                        else:
                            j = {(0, L32): 0, (0, L16): 1, (0, L8): 2, (0, DK): 3, (1, L64): 4, (1, L32): 5, (1, L16): 6, (1, L8): 7}[(d, i)]
                            last = nc.vector.copy_predicated(at, maskb[:, j:j + 1, :].broadcast_to([P, nt, P]), src)
                        last.then_inc(g_free, 1)
                    dve.wait_ge(g_free, 3 * use(h, (d, i)) + 3)
                elif kind == "g":
                    dve.wait_ge(z_out, NP_STEPS * (h + 1))
                    dve.wait_ge(g_full, 3 * use(h, (1, DK)) + 3)
                    TS(ring[:, 2, :], zg[:, h % 2, :, :].rearrange("p t e -> p (t e)"), SIG_FLOOR, None, ALU.max).then_inc(g_clamped, 1)
                elif kind == "gate":
                    g = zg[:, h % 2, :, :]
                    dve.wait_ge(g_sig, h + 1)
                    steps.link(dve, TT(g, g, ring[:, 2, :].rearrange("p (t e) -> p t e", e=RD), ALU.mult))
                elif kind == "fin_o":
                    if h:
                        dve.wait_ge(g_full, 3 * use(h - 1, "yT") + 3)
                    for b, (t0, nt) in enumerate(BANKS):
                        take(h, "o", b)
                        nc.vector.tensor_copy(y[:, t0:t0 + nt, :].rearrange("p t e -> p (t e)"), pg[b][:, 0:nt * P]).then_inc(g_free, 1)
                    dve.wait_ge(g_free, 3 * use(h, "o") + 3)
                    steps.give(nc.vector.tensor_copy(dtmp[:, 0, 0:1], tot8[:, 0, 0:1]))
                    nc.vector.tensor_copy(dtmp[:, 0, 1:2], tot8[:, 0, 0:1]).then_inc(o_out, 1)
                elif kind == "norm":
                    dve.wait_ge(o_sq, h + 1)
                    steps.link(dve, nc.vector.reduce_sum(ms[:, :], ring[:, 3, :].rearrange("p (t e) -> p t e", e=RD), AX_X))
                    TS(ms[:, :], ms[:, :], 1.0 / RD, EPS, ALU.mult, ALU.add).then_inc(ms_ready, 1)
                    g = zg[:, h % 2, :, :]
                    steps.link(dve, TT(g, g, y[:, :, :], ALU.mult))
                elif kind == "y":
                    dve.wait_ge(rstd, h + 1)
                    TT(y[:, :, :], zg[:, h % 2, :, :], wide(ms[:, :].rearrange("p (t a) -> p t a", a=1), RD), ALU.mult).then_inc(y_ready, 1)
                elif kind == "fin_y":
                    at = ROWS["r_onorm_g"][0] + h
                    for b, (t0, nt) in enumerate(BANKS):
                        take(h, "yT", b)
                        steps.link(dve, TS(r1[:, t0 * P:(t0 + nt) * P], pg[b][:, 0:nt * P], S["vec"][:, at:at + 1], None, ALU.mult))
                        nc.vector.tensor_copy(dtmp[:, 0, 2:3], tot8[:, 0, 0:1]).then_inc(g_free, 1)
                        dve.wait_ge(g_free, 3 * use(h, "yT") + b + 1)
                        nc.vector.tensor_copy(dtmp[:, 0, 3:4], tot8[:, 0, 0:1]).then_inc(yT_ready, 1)
                        dve.wait_ge(yT_ready, 3 * h + b + 1)

            at = ROWS["r_lb_logits"][0]
            logits = S["vec"][:, at:at + 2 * RH].rearrange("p (s h) -> p s h", s=2)
            steps.link(dve, nc.vector.memset(tot8[:, :, :], 0.0))
            TT(lbt[:, :, :], logits, logits, ALU.subtract).then_inc(lb_d, 1)
            dve.wait_ge(lb_e, 1)
            steps.link(dve, nc.vector.reciprocal(lb[:, :, :], lbt[:, :, :]))
            steps.link(dve, TT(lbt[:, :, :], lbt[:, :, :], lb[:, :, :], ALU.mult))
            steps.link(dve, TT(lb[:, :, :], lbt[:, :, :], lbt[:, :, :], ALU.subtract))
            steps.link(dve, TS(lb[:, :, :], lb[:, :, :], 0.0, None, ALU.max))
            steps.link(dve, TS(oml[:, :, :], lb[:, :, :], -1.0, 1.0, ALU.mult, ALU.add))
            dve.wait_ge(consts, 32)
            steps.give(nc.vector.tensor_copy(maskb[:, :, :].rearrange("p m c -> p (m c)"), ring[:, 0, 0:8 * P]))
            steps.link(dve, nc.vector.memset(restart[:, :], 1.0))
            steps.link(dve, nc.vector.memset(restart[:, :].rearrange("p (b h) -> p b h", h=64)[:, :, 0:1], 0.0))
            for h, tok in ORDER:
                step(h, tok)


def rec_constants():
    s, t = np.arange(P)[:, None], np.arange(P)[None, :]
    lev = lambda h: ((s // (2 * h) == t // (2 * h)) & (s // h < t // h))
    fw = [lev(h) for h in LEVELS]
    d8 = (s // 8 == t // 8) & (s <= t)
    maskb = np.stack([fw[1], fw[2], fw[3], d8] + [m.T for m in fw], 1)
    maskf = np.stack([fw[0], d8.T], 1)
    return {"k_maskb": np.ascontiguousarray(maskb.astype(np.float32)), "k_maskf": np.ascontiguousarray(maskf.astype(np.float32))}


def final_norm(nc, A, S, x_dram, y_dram, out):
    with ExitStack() as ctx:
        sb, ps, sem = scope(nc, ctx, "fn")
        x, y = sb("x", [P, NT, D]), sb("y", [P, NT, D])
        gate, gain = sb("gate", [P, 2, D]), sb("gain", [P, D])
        junk = sb("junk", [P, 2, D])
        ssq = sb("ssq", [P, NT])
        x_in, y_in = [sem(f"x{t}") for t in range(NT)], [sem(f"y{t}") for t in range(NT)]
        g_in, gated, summed, squared, v_steps, inverted, rooted, scaled, ready, stored = (sem(n) for n in (
            "g_in gated summed squared v inverted rooted scaled ready stored").split())
        block = ctx.enter_context(nc.Block())

        @block.sync
        def _(sp):
            for c in range(2):
                sp.dma_start(gate[:, c, :], S["mod_dram"][DEPTH - 1, c:c + 1, 5 * D:6 * D].broadcast_to([P, D])).then_inc(g_in, 16)
            sp.dma_start(gain[:, :], A["final_norm_g"].rearrange("(a d) -> a d", a=1).broadcast_to([P, D])).then_inc(g_in, 16)
            for t in range(NT):
                sp.dma_start(x[:, t, :], x_dram[t * P:(t + 1) * P, :]).then_inc(x_in[t], 16)
                sp.dma_start(y[:, t, :], y_dram[t * P:(t + 1) * P, :]).then_inc(y_in[t], 16)
            for t in range(NT):
                sp.wait_ge(ready, t + 1)
                sp.dma_start(out(t), y[:, t, :]).then_inc(stored, 16)
            sp.wait_ge(stored, 16 * NT)

        @block.scalar
        def _(act):
            for g, (t0, n, _) in enumerate(PIECES):
                for t in range(t0, t0 + n):
                    act.wait_ge(summed, t + 1)
                    if t >= 2:
                        act.wait_ge(squared, t - 1)
                    nc.scalar.activation(junk[:, t % 2, :], y[:, t, :], ACT.Square, accum_out=ssq[:, t:t + 1]).then_inc(squared, 1)
                act.wait_ge(inverted, g + 1)
                nc.scalar.activation(ssq[:, t0:t0 + n], ssq[:, t0:t0 + n], ACT.Sqrt).then_inc(rooted, 1)

        @block.vector
        def _(dve):
            steps = Count(v_steps)
            dve.wait_ge(g_in, 48)
            for g, (t0, n, _) in enumerate(PIECES):
                for t in range(t0, t0 + n):
                    dve.wait_ge(y_in[t], 16)
                    nc.vector.tensor_tensor(y[:, t, :], y[:, t, :], gate[:, 0 if t < CT else 1, :], ALU.mult).then_inc(gated, 1)
                    dve.wait_ge(gated, t + 1)
                    dve.wait_ge(x_in[t], 16)
                    nc.vector.tensor_tensor(y[:, t, :], y[:, t, :], x[:, t, :], ALU.add).then_inc(summed, 1)
                dve.wait_ge(squared, t0 + n)
                s = ssq[:, t0:t0 + n]
                steps.link(dve, nc.vector.tensor_scalar(s, s, 1.0 / D, EPS, ALU.mult, ALU.add))
                nc.vector.reciprocal(s, s).then_inc(inverted, 1)
                dve.wait_ge(rooted, g + 1)
                for t in range(t0, t0 + n):
                    nc.vector.scalar_tensor_tensor(y[:, t, :], y[:, t, :], ssq[:, t:t + 1], gain[:, :], ALU.mult, ALU.mult).then_inc(ready, 1)


def build_step(nc, A, O, W):
    def rows(t_dram):
        return lambda t: t_dram[t * P:(t + 1) * P, :]

    def x_tile(prompt, sample):
        return lambda t: (prompt[0, t * P:(t + 1) * P, :] if t < CT else sample[0, (t - CT) * P:(t - CT + 1) * P, :])

    with ExitStack() as ctx:
        sb, _, _ = scope(nc, ctx, "step")
        S = {"ident": sb("ident", [P, P]), "vec": sb("vec", [P, NROWS]), "modcol": sb("modcol", [P, DEPTH, 6, 2, KD]),
             "mod_dram": W["mod"]}

        with ExitStack() as layer0:
            sb0, _, _ = scope(nc, layer0, "l0")
            filt = sb0("filt", [P, NT, HW])
            modulation(nc, A, S, filt)
            yh = sb0("yh", [P, 4, T])
            with ExitStack() as proj:
                sb1, _, _ = scope(nc, proj, "l0p")
                hnT = sb1("hnT", [P, KD, T])
                norm_transpose(nc, A, S, "n0", x_tile(A["x_prompt"], A["x_sample"]), 0, 0, 1, hnT)
                with ExitStack() as hy:
                    sb2, _, _ = scope(nc, hy, "l0h")
                    u, uT = sb2("u", [P, 4, T]), sb2("uT", [P, NT, HW])
                    hyena_in(nc, A, S, hnT, yh, u, uT)
                    hyena_conv(nc, A, S, yh, u, uT, filt)
                qT, kT, v = sb1("qT", [P, 4, T]), sb1("kT", [P, NKV, KT * P]), sb1("v", [P, KT, NKV * HD])
                qkv_in(nc, A, S, hnT, qT, kT, v, O["new_k"].rearrange("b a t g d -> (b a t) (g d)"),
                       O["new_v"].rearrange("b a t g d -> (b a t) (g d)"))
                ya = filt[:, :, :].rearrange("p t c -> p (t c)").rearrange("p (k t) -> p k t", k=4)
                attention(nc, A, S, qT, kT, v, ya)
                out_proj(nc, A, S, "op0", A["e_w_out"][0], lambda k: (yh if k < 4 else ya)[:, k % 4, :],
                         x_tile(A["x_prompt"], A["x_sample"]), rows(W["xm0"]), 0)

        idx = [sb("idx0", [CAP[0], NE], U32), sb("idx1", [CAP[1], NE], U32)]
        gates = [sb("gates0", [CAP[0], NE]), sb("gates1", [CAP[1], NE])]

        def mixer(layer):
            with ExitStack() as mix:
                sbw, _, sem = scope(nc, mix, f"mw{layer}")
                w, w_in = sbw("w", [P, 12, KD, SW]), [sem(f"w_in{j}") for j in range(12)]
                with ExitStack() as norm:
                    sb1, _, _ = scope(nc, norm, f"f{layer}")
                    hnT = sb1("hnT", [P, KD, T])
                    norm_transpose(nc, A, S, f"nf{layer}", rows(W[f"xm{layer}"]), layer, 3, 4, hnT, W["xn"])
                    route(nc, A, S, f"rt{layer}", hnT, layer, idx, gates, w, w_in)
                experts(nc, A, S, f"moe{layer}", layer, W["xn"], W["y"], idx, gates, w, w_in)

        mixer(0)

        with ExitStack() as layer1:
            sb1, _, _ = scope(nc, layer1, "l1")
            hnT = sb1("hnT", [P, KD, T])
            norm_transpose(nc, A, S, "n2", rows(W["xm0"]), 1, 0, 1, hnT, residual=(W["y"], 0, W["x1"]))
            recurrence(nc, A, S, hnT, W["yr"], O["new_state"].rearrange("b r s h d e -> (b r s) h d e"))
        with ExitStack() as layer1:
            sb1, _, _ = scope(nc, layer1, "l1o")
            yr = sb1("yr", [P, RH, T])
            out_proj(nc, A, S, "op1", A["r_w_out"][0], lambda k: yr[:, k, :], rows(W["x1"]), rows(W["xm1"]), 1, W["yr"])

        mixer(1)
        final_norm(nc, A, S, W["xm1"], W["y"], x_tile(O["y_prompt"], O["y_sample"]))


def constants():
    f32 = np.float32
    out = {"k_ident": np.eye(P, dtype=f32)}
    feats, offs = [], []
    for _, ln in SEQS:
        t = np.arange(ln, dtype=np.float64)
        tn = t / ln
        ang = 2 * math.pi * tn[:, None] * np.arange(1, 17)[None, :]
        feats.append(np.concatenate([tn[:, None], np.sin(ang), np.cos(ang)], axis=-1))
        offs.append(-np.abs(t - ln // 2) / (ln // 2))
    out["k_feats"] = np.ascontiguousarray(np.concatenate(feats).T.astype(f32))
    out["k_offsets"] = np.ascontiguousarray(np.concatenate(offs).reshape(NT, P).T.astype(f32))
    for tag, (o, ln), (n, fw, nf) in (("c", SEQS[0], CONV[0]), ("l", SEQS[1], CONV[1])):
        w = 2 * math.pi * (np.arange(n // 2) + 0.5) / n
        t = np.arange(ln)
        fw_m = np.stack([np.cos(np.outer(t, w)), -np.sin(np.outer(t, w))], 1)
        fw_m = fw_m.reshape(ln // P, P, 2, nf, fw).transpose(3, 1, 0, 2, 4)
        out["k_fwd_" + tag] = np.ascontiguousarray(fw_m.reshape(nf, P, -1).astype(f32))
        tau = np.arange(ln) + ln // 2
        inv = np.stack([2 / n * np.cos(np.outer(w, tau)), -2 / n * np.sin(np.outer(w, tau))], 1)
        inv = inv.reshape(nf, fw, 2, ln).transpose(1, 0, 2, 3).reshape(fw, 2 * nf, ln)
        if tag == "c":
            out["k_inv_c"] = np.ascontiguousarray(inv.astype(f32))
        else:
            out["k_inv_l"] = np.ascontiguousarray(inv.reshape(fw, 2 * nf, 2, 512).transpose(2, 0, 1, 3).astype(f32))
    pos = np.arange(LL)
    inv_f = 10000.0 ** (-np.arange(0, 32, 2, dtype=np.float64) / 32)
    ang = np.stack([(pos // 64)[:, None] * inv_f, (pos % 64)[:, None] * inv_f], 1)
    for name, f in (("k_cos", np.cos), ("k_sin", np.sin)):
        out[name] = np.ascontiguousarray(f(ang).reshape(LL // P, P, 32).transpose(1, 0, 2).astype(f32))
    return out


_INS = ["x_prompt", "x_sample", "cache_k", "cache_v", "state_rec", "c", "c_ctx", "mod_w", "mod_b", "norm_mix_g", "norm_ffn_g",
        "e_w_in", "e_conv_w", "e_conv_b", "f_w1", "f_b1", "f_freq", "f_w2", "f_b2", "f_w3", "f_decay", "hy_bias", "q_norm_g",
        "k_norm_g", "e_w_out", "r_w_in", "r_lb_logits", "r_onorm_g", "r_w_out", "router_w", "moe_w_gu", "moe_w_down",
        "final_norm_g"]
_OUTS = [("y_prompt", (1, LC, D)), ("y_sample", (1, LL, D)), ("new_k", (1, 1, LC, NKV, HD)), ("new_v", (1, 1, LC, NKV, HD)),
         ("new_state", (1, 1, 2, RH, RD, RD))]
_SCRATCH = [("mod", (DEPTH, 2, 6 * D)), ("xm0", (T, D)), ("x1", (T, D)), ("xm1", (T, D)), ("xn", (T, D)), ("y", (T, D)),
            ("yr", (RH, P, T))]


def kernel(**inputs):
    import concourse.bacc as _bacc
    from concourse.bass_utils import run_bass_kernel_spmd as _run

    nc = _bacc.Bacc("TRN2", target_bir_lowering=False, num_devices=1)
    arrays, A = {}, {}
    data = {name: np.ascontiguousarray(inputs[name]) for name in _INS}
    data.update(constants())
    data.update(rec_constants())
    for name, a in data.items():
        arrays[f"in_{name}"] = a
        A[name] = nc.dram_tensor(f"in_{name}", a.shape, mybir.dt.from_np(a.dtype), kind="ExternalInput").ap()
    O = {name: nc.dram_tensor(f"out_{name}", shape, F32, kind="ExternalOutput").ap() for name, shape in _OUTS}
    W = {name: nc.dram_tensor(f"scratch_{name}", shape, F32, kind="Internal").ap() for name, shape in _SCRATCH}
    build_step(nc, A, O, W)
    r = _run(nc, [arrays], core_ids=[0])
    return tuple(r.results[0][f"out_{name}"] for name, _ in _OUTS)
```

```python
import math
from contextlib import ExitStack

import numpy as np
import concourse.bass as bass
from concourse import mybir

F32 = mybir.dt.float32
U32 = mybir.dt.uint32
ALU = mybir.AluOpType
ACT = mybir.ActivationFunctionType
AX_X = mybir.AxisListType.X

P = 128
D = 1024
KD = D // P
LC, LL = 256, 1024
T = LC + LL
NT = T // P
CT = LC // P
DEPTH = 2
EPS = 1e-6
HW = D // 2
HD, NH, NKV = 64, 8, 2
PAST = 256
RH, RD = 8, 128
NE = 16
FH = D
CAP = [2 * LC // NE, 2 * LL // NE]
PIECES = [(0, 2, 0), (2, 4, 1), (6, 4, 1)]
SEQS = [(0, LC), (LC, LL)]

ROWS = {}
_at = 0
for _name, _n in [("norm_mix_g", 2 * KD), ("norm_ffn_g", 2 * KD), ("e_conv_w", 36), ("e_conv_b", 12),
                  ("hy_bias", 4), ("r_onorm_g", KD), ("r_lb_logits", 2 * KD), ("c_ctx", KD), ("c", KD)]:
    ROWS[_name] = (_at, _n)
    _at += _n
NROWS = _at


class Count:

    def __init__(self, sem, start=0):
        self.sem, self.start, self.n = sem, start, 0

    def give(self, ins, by=1):
        ins.then_inc(self.sem, by)
        self.n += by
        return self.n

    def wait(self, eng, n=None):
        eng.wait_ge(self.sem, self.start + (self.n if n is None else n))

    def link(self, eng, ins):
        self.give(ins)
        self.wait(eng)


def scope(nc, ctx, tag):
    sems = []

    def clear():
        if sems:
            nc.clear_and_free_semaphores(sems)
            nc.all_engine_barrier()

    ctx.callback(clear)

    def sb(name, shape, dt=F32):
        return ctx.enter_context(nc.sbuf_tensor(f"{tag}_{name}", shape, dt))

    def ps(name, shape, dt=F32):
        return ctx.enter_context(nc.psum_tensor(f"{tag}_{name}", shape, dt))

    def sem(name):
        sems.append(nc.alloc_semaphore(f"{tag}_{name}"))
        return sems[-1]
    return sb, ps, sem


MOD_G = 3
MOD_RING = 3
MOD_SLOTS = 2 * MOD_G
KH = KD // 2


class LayerModulation:

    def __init__(self, nc, A, S, layer, w, psm, pst, sb, sem):
        self.nc, self.A, self.S, self.layer, self.w, self.psm, self.pst = nc, A, S, layer, w, psm, pst
        self.row, self.brow = sb("row", [P, MOD_G, 512]), sb("brow", [P, MOD_G, 512])
        self.bias_in, self.bias_zero, self.w_used, self.row_ready = sem("bias_in"), sem("bias_zero"), sem("w_used"), sem("row_ready")
        self.col_tr, self.tr_used, self.stored = sem("col_tr"), sem("tr_used"), sem("stored")
        self.w_in = [sem(f"mod_in{i}") for i in range(MOD_RING)]

    def zero(self, dve):
        self.nc.vector.memset(self.brow[:, :, :], 0.0).then_inc(self.bias_zero, 1)
        self.nc.vector.memset(self.row[:, :, :], 0.0).then_inc(self.bias_zero, 1)

    def load_bias(self, act):
        act.wait_ge(self.bias_zero, 1)
        for j in range(4):
            src = self.A["mod_b"][self.layer, :].rearrange("(g j n) -> j g n", j=4, n=512)[j:j + 1]
            for c in range(2):
                act.dma_start(self.brow[32 * j + c:32 * j + c + 1, :, :], src).then_inc(self.bias_in, 16)

    def load_weights(self, sp):
        for s in range(MOD_SLOTS):
            g, kh = divmod(s, 2)
            if s >= MOD_RING:
                sp.wait_ge(self.w_used, 4 * (s - MOD_RING + 1))
            for j in range(4):
                b = 4 * g + j
                sp.dma_start(self.w[:, s % MOD_RING, j, :, :],
                             self.A["mod_w"][self.layer, kh * KH * P:(kh + 1) * KH * P, b * 512:(b + 1) * 512]
                             .rearrange("(k p) n -> p k n", p=P)).then_inc(self.w_in[s % MOD_RING], 16)

    def multiply(self, pe, g):
        nb = len(self.psm)
        if g >= nb:
            pe.wait_ge(self.row_ready, g - nb + 1)
        for kh in range(2):
            s = 2 * g + kh
            pe.wait_ge(self.w_in[s % MOD_RING], 64 * (s // MOD_RING + 1))
            for k in range(KH):
                for j in range(4):
                    m = self.nc.tensor.matmul(self.psm[g % nb][32 * j:32 * j + 2, :], self.S["scond"][:, :, kh * KH + k],
                                              self.w[:, s % MOD_RING, j, k, :], start=(kh + k == 0),
                                              stop=(kh == 1 and k == KH - 1), tile_position=(0, 32 * j))
                    if k == KH - 1:
                        m.then_inc(self.w_used, 1)

    def add_bias(self, dve, g):
        if g == 0:
            dve.wait_ge(self.bias_zero, 2)
            dve.wait_ge(self.bias_in, 16 * 8)
        dve.wait_ge(self.w_used, 8 * (g + 1))
        for j in range(4):
            r = self.nc.vector.tensor_tensor(self.row[32 * j:32 * j + 2, g, :], self.psm[g % len(self.psm)][32 * j:32 * j + 2, :],
                                             self.brow[32 * j:32 * j + 2, g, :], ALU.add)
        r.then_inc(self.row_ready, 1)

    def store(self, act):
        act.wait_ge(self.row_ready, MOD_G)
        for j in range(4):
            dst = self.S["mod_dram"][self.layer].rearrange("c (g j n) -> j c g n", j=4, n=512)[j]
            act.dma_start(dst, self.row[32 * j:32 * j + 2, :, :]).then_inc(self.stored, 16)
        act.wait_ge(self.stored, 16 * 4)

    def transpose(self, pe):
        pe.wait_ge(self.row_ready, MOD_G)
        for g in range(MOD_G):
            if g:
                pe.wait_ge(self.tr_used, g)
            for q in range(4):
                m = self.nc.tensor.transpose(self.pst[:, q * P:(q + 1) * P], self.row[:, g, q * P:(q + 1) * P],
                                             self.S["ident"][:, :])
            m.then_inc(self.col_tr, 1)

    def columns(self, dve):
        mc, l = self.S["modcol"], self.layer
        for g in range(MOD_G):
            dve.wait_ge(self.col_tr, g + 1)
            for j in range(4):
                b = 4 * g + j
                src = self.pst[:, :].rearrange("p (q r) -> p q r", r=P)[:, :, 32 * j:32 * j + 2]
                r = self.nc.vector.tensor_copy(
                    mc[:, l, b // 2, :, 4 * (b % 2):4 * (b % 2) + 4].rearrange("p c q -> p q c"), src)
            r.then_inc(self.tr_used, 1)
        dve.wait_ge(self.tr_used, MOD_G)
        for s, gain in ((1, "norm_mix_g"), (4, "norm_ffn_g")):
            at = ROWS[gain][0] + l * KD
            for c in range(2):
                self.nc.vector.scalar_tensor_tensor(mc[:, l, s, c, :], mc[:, l, s, c, :], 1.0,
                                                    self.S["vec"][:, at:at + KD], ALU.add, ALU.mult)


def modulation(nc, A, S, filt, room):
    with ExitStack() as ctx:
        sb, ps, sem = scope(nc, ctx, "mod")
        pack = sb("pack", [P, P])
        w = sb("w_ring", [P, MOD_RING, 4, KH, 512])
        pst = ps("pst", [P, 512])
        psm = [ps(f"psm{i}", [P, 512]) for i in range(2)]
        pack_in, packed, col_ready, cond_ready = sem("pack_in"), sem("packed"), sem("col_ready"), sem("cond_ready")
        mod = LayerModulation(nc, A, S, 0, w, psm, pst, sb, sem)
        block = ctx.enter_context(nc.Block())

        @block.sync
        def _(sp):
            n = 0
            for name, (at, rows) in ROWS.items():
                src = A[name]
                flat = {1: "(r p) -> r p", 2: "a (r p) -> (a r) p", 3: "a b (r p) -> (a b r) p"}[len(src.shape)]
                sp.dma_start(pack[at:at + rows, :], src.rearrange(flat, p=P)).then_inc(pack_in, 16)
                n += 16
            assert n == 16 * len(ROWS)
            sp.dma_start(S["ident"][:, :], A["k_ident"]).then_inc(pack_in, 16)

        filter_tensor, filter_scalar, filter_vector = hyena_filter(nc, A, filt, room, block, sb, ps, sem)

        @block.sync
        def _(sp):
            mod.load_weights(sp)

        @block.scalar
        def _(act):
            mod.load_bias(act)
            act.wait_ge(col_ready, 1)
            at = ROWS["c_ctx"][0]
            nc.scalar.activation(S["scond"][:, :, :].rearrange("p c k -> p (c k)"), S["vec"][:, at:at + 2 * KD],
                                 ACT.Silu).then_inc(cond_ready, 1)
            for part in range(4):
                filter_scalar(act, part)
            mod.store(act)

        @block.tensor
        def _(pe):
            pe.wait_ge(pack_in, 16 * (len(ROWS) + 1))
            nc.tensor.transpose(pst[:, 0:NROWS], pack[0:NROWS, :], S["ident"][0:NROWS, 0:NROWS]).then_inc(packed, 1)
            filter_tensor(pe, 0)
            pe.wait_ge(cond_ready, 1)
            for g in range(MOD_G):
                mod.multiply(pe, g)
                filter_tensor(pe, g + 1)
            mod.transpose(pe)

        @block.vector
        def _(dve):
            mod.zero(dve)
            dve.wait_ge(packed, 1)
            nc.vector.tensor_copy(S["vec"][:, :], pst[:, 0:NROWS]).then_inc(col_ready, 1)
            filter_vector(dve, 0)
            for g in range(MOD_G):
                mod.add_bias(dve, g)
                filter_vector(dve, g + 1)
            dve.wait_ge(col_ready, 1)
            mod.columns(dve)


def norm_transpose(nc, A, S, tag, x_dram, layer, shift, scale, hnT):
    with ExitStack() as ctx:
        sb, ps, sem = scope(nc, ctx, tag)
        x = sb("x", [P, NT, D])
        junk = sb("junk", [P, 2, D])
        ssq, rstd = sb("ssq", [P, NT]), sb("rstd", [P, NT])
        NPS = 6
        pst = [ps(f"ps{i}", [P, 512]) for i in range(NPS)]
        x_in = [sem(f"x{t}") for t in range(NT)]
        squared, inverted, v_steps, rooted, scaled, tr, ev_a, ev_v = (sem(n) for n in (
            "squared inverted v rooted scaled tr ev_a ev_v").split())
        block = ctx.enter_context(nc.Block())
        units = [(t0, n, c, k) for t0, n, c in PIECES for k in range(KD)]
        groups = [(t0, n) for t0, n, _ in PIECES]

        @block.sync
        def _(sp):
            for t in range(NT):
                sp.dma_start(x[:, t, :], x_dram(t)).then_inc(x_in[t], 16)

        @block.scalar
        def _(act):
            for g, (t0, n) in enumerate(groups):
                for t in range(t0, t0 + n):
                    act.wait_ge(x_in[t], 16)
                    if t >= 2:
                        act.wait_ge(squared, t - 1)
                    nc.scalar.activation(junk[:, t % 2, :], x[:, t, :], ACT.Square,
                                         accum_out=ssq[:, t:t + 1]).then_inc(squared, 1)
                act.wait_ge(inverted, g + 1)
                nc.scalar.activation(rstd[:, t0:t0 + n], rstd[:, t0:t0 + n], ACT.Sqrt).then_inc(rooted, 1)
            for u, (t0, n, c, k) in enumerate(units):
                if u % 2 == 0:
                    act.wait_ge(tr, u + 1)
                    nc.scalar.activation(hnT[:, k, t0 * P:(t0 + n) * P], pst[u % NPS][:, 0:n * P], ACT.Identity,
                                         bias=S["modcol"][:, layer, shift, c, k:k + 1],
                                         scale=S["modcol"][:, layer, scale, c, k:k + 1]).then_inc(ev_a, 1)

        @block.vector
        def _(dve):
            steps = Count(v_steps)
            for g, (t0, n) in enumerate(groups):
                dve.wait_ge(squared, t0 + n)
                steps.link(dve, nc.vector.tensor_scalar(rstd[:, t0:t0 + n], ssq[:, t0:t0 + n], 1.0 / D, EPS, ALU.mult, ALU.add))
                nc.vector.reciprocal(rstd[:, t0:t0 + n], rstd[:, t0:t0 + n]).then_inc(inverted, 1)
                dve.wait_ge(rooted, g + 1)
                for t in range(t0, t0 + n):
                    nc.vector.tensor_scalar(x[:, t, :], x[:, t, :], rstd[:, t:t + 1], None, ALU.mult).then_inc(scaled, 1)
            for u, (t0, n, c, k) in enumerate(units):
                if u % 2 == 1:
                    dve.wait_ge(tr, u + 1)
                    nc.vector.tensor_scalar(hnT[:, k, t0 * P:(t0 + n) * P], pst[u % NPS][:, 0:n * P],
                                            S["modcol"][:, layer, scale, c, k:k + 1],
                                            S["modcol"][:, layer, shift, c, k:k + 1], ALU.mult, ALU.add).then_inc(ev_v, 1)

        @block.tensor
        def _(pe):
            for u, (t0, n, c, k) in enumerate(units):
                pe.wait_ge(scaled, t0 + n)
                if u >= NPS:
                    prev = u - NPS
                    pe.wait_ge(ev_v if prev % 2 else ev_a, prev // 2 + 1)
                for i in range(n):
                    m = nc.tensor.transpose(pst[u % NPS][:, i * P:(i + 1) * P], x[:, t0 + i, k * P:(k + 1) * P],
                                            S["ident"][:, :])
                m.then_inc(tr, 1)


def hyena_in(nc, A, S, hnT, x0, u, uT):
    NPS, NTR, NZ = 5, 3, 3
    with ExitStack() as ctx:
        sb, ps, sem = scope(nc, ctx, "hin")
        w = sb("w", [P, 2, KD, 3, P])
        z = sb("z", [P, NZ, LC + 2 + LL + 2])
        x1 = sb("x1", [P, 2, T])
        hv = sb("hv", [P, 2, T])
        psm = [ps(f"psm{i}", [P, 512]) for i in range(NPS)]
        pst = [ps(f"pst{i}", [P, 512]) for i in range(NTR)]
        w_in = [sem("w_in0"), sem("w_in1")]
        mm, z_ready, z_used, v_steps, u_ready, tr, tr_used, zeroed = (
            sem("mm"), sem("z_ready"), sem("z_used"), sem("v"), sem("u_ready"),
            sem("tr"), sem("tr_used"), sem("zeroed"))
        ZAT = {0: 1, LC: LC + 3}
        block = ctx.enter_context(nc.Block())

        @block.sync
        def _(sp):
            for i in range(4):
                if i >= 2:
                    sp.wait_ge(mm, 9 * (i - 1))
                for part in range(3):
                    c0 = part * HW + i * P
                    sp.dma_start(w[:, i % 2, :, part, :],
                                 A["e_w_in"][0, :, c0:c0 + P].rearrange("(k p) n -> p k n", p=P)).then_inc(w_in[i % 2], 16)

        @block.tensor
        def _(pe):
            def transposes(i):
                pe.wait_ge(u_ready, i + 1)
                for g, (t0, n, _) in enumerate(PIECES):
                    if i >= 1:
                        pe.wait_ge(tr_used, 3 * (i - 1) + g + 1)
                    for t in range(n):
                        m = nc.tensor.transpose(pst[g][:, t * P:(t + 1) * P],
                                                u[:, i, (t0 + t) * P:(t0 + t + 1) * P], S["ident"][:, :])
                    m.then_inc(tr, 1)

            for i in range(4):
                pe.wait_ge(w_in[i % 2], 48 * (i // 2 + 1))
                for part in range(3):
                    for g, (t0, n, _) in enumerate(PIECES):
                        j = 9 * i + 3 * part + g
                        if j >= NPS:
                            pe.wait_ge(z_ready, j - NPS + 1)
                        for k in range(KD):
                            m = nc.tensor.matmul(psm[j % NPS][:, 0:n * P], w[:, i % 2, k, part, :],
                                                 hnT[:, k, t0 * P:(t0 + n) * P], start=(k == 0), stop=(k == KD - 1))
                        m.then_inc(mm, 1)
                    if part == 0 and i >= 1:
                        transposes(i - 1)
            transposes(3)

        @block.scalar
        def _(act):
            act.wait_ge(zeroed, 1)

            def to_uT(i):
                for g, (t0, n, _) in enumerate(PIECES):
                    act.wait_ge(tr, 3 * i + g + 1)
                    nc.scalar.activation(uT[:, t0:t0 + n, i * P:(i + 1) * P],
                                         pst[g][:, 0:n * P].rearrange("p (t c) -> p t c", c=P), ACT.Copy).then_inc(tr_used, 1)

            for tile in range(12):
                i, part = divmod(tile, 3)
                if tile >= NZ:
                    act.wait_ge(z_used, tile - NZ + 1)
                for g, (t0, n, c) in enumerate(PIECES):
                    at = ZAT[SEQS[c][0]] + t0 * P - SEQS[c][0]
                    act.wait_ge(mm, 3 * tile + g + 1)
                    nc.scalar.activation(z[:, tile % NZ, at:at + n * P], psm[(3 * tile + g) % NPS][:, 0:n * P],
                                         ACT.Copy).then_inc(z_ready, 1)
                if part == 1 and i >= 1:
                    to_uT(i - 1)
            to_uT(3)

        @block.vector
        def _(dve):
            steps = Count(v_steps)
            nc.vector.memset(z[:, :, :], 0.0).then_inc(zeroed, 1)
            for tile in range(12):
                i, part = divmod(tile, 3)
                dve.wait_ge(z_ready, 3 * (tile + 1))
                out = (x0[:, i, :], x1[:, i % 2, :], hv[:, i % 2, :])[part]
                wc, bc = ROWS["e_conv_w"][0] + part * 4 + i, ROWS["e_conv_b"][0] + part * 4 + i
                at = [(o, ln, ZAT[o] - 1) for o, ln in SEQS]
                for o, ln, a in at:
                    r = nc.vector.tensor_scalar(out[:, o:o + ln], z[:, tile % NZ, a:a + ln], S["vec"][:, wc:wc + 1],
                                                S["vec"][:, bc:bc + 1], ALU.mult, ALU.add)
                steps.link(dve, r)
                for tap in (1, 2):
                    for o, ln, a in at:
                        r = nc.vector.scalar_tensor_tensor(out[:, o:o + ln], z[:, tile % NZ, a + tap:a + tap + ln],
                                                           S["vec"][:, wc + 12 * tap:wc + 12 * tap + 1],
                                                           out[:, o:o + ln], ALU.mult, ALU.add)
                    if tap == 1:
                        steps.link(dve, r)
                r.then_inc(z_used, 1)
                if part == 2:
                    dve.wait_ge(z_used, tile + 1)
                    nc.vector.tensor_tensor(u[:, i, :], x1[:, i % 2, :], hv[:, i % 2, :], ALU.mult).then_inc(u_ready, 1)


def hyena_filter(nc, A, filt, room, block, sb, ps, sem):
    MAGIC = 12582912.0
    TWO_PI = 2 * math.pi
    HI = 6.28125
    LO = TWO_PI - HI
    EMB, FHID = 33, 64
    win = room[:, 0:4, :].rearrange("p k t -> p (k t)").rearrange("p (t c) -> p t c", c=HW)
    arg, turn, hid, feats = (room[0:n, 4 + j, :] for j, n in enumerate((FHID, FHID, FHID, EMB)))
    w1, w2, w3 = sb("w1", [EMB, FHID]), sb("w2", [FHID, FHID]), sb("w3", [FHID, HW])
    cols = sb("cols", [FHID, 3])
    decay, offs = sb("decay", [P, HW]), sb("offs", [P, NT])
    ones = sb("ones", [P, P])
    rsum = sb("rsum", [P, 2, HW])
    psl = [ps(f"psl{i}", [P, 512]) for i in range(3)]
    psw = psl
    pss = [ps("pss0", [P, 512]), ps("pss1", [P, 512])]
    loaded, v_steps, mm, sined, w_ready, h_mm, h_ready, a_ready, summed, ab, abs_ready = (
        sem("loaded"), sem("f_v"), sem("mm"), sem("sined"), sem("w_ready"), sem("h_mm"), sem("h_ready"),
        sem("a_ready"), sem("summed"), sem("ab"), sem("abs_ready"))

    LOADS = 9 * 16
    steps = Count(v_steps)

    @block.sync
    def _(sp):
        for dst, src in ((feats, A["k_feats"]), (w1, A["f_w1"][0]), (w2, A["f_w2"][0]), (w3, A["f_w3"][0]),
                         (offs, A["k_offsets"])):
            sp.dma_start(dst[:, :], src).then_inc(loaded, 16)
        for j, name in enumerate(("f_b1", "f_freq", "f_b2")):
            sp.dma_start(cols[:, j:j + 1], A[name][0].rearrange("(p a) -> p a", a=1)).then_inc(loaded, 16)
        sp.dma_start(decay[:, :], A["f_decay"].broadcast_to([P, HW])).then_inc(loaded, 16)

    def tensor(pe, part):
        if part < 2:
            if part == 0:
                pe.wait_ge(loaded, LOADS)
            else:
                pe.wait_ge(sined, 1)
            wt, x = ((w1, feats), (w2, hid))[part]
            for g, (t0, n, _) in enumerate(PIECES):
                m = nc.tensor.matmul(psl[g][0:FHID, 0:n * P], wt[:, :], x[:, t0 * P:(t0 + n) * P], start=True, stop=True)
            m.then_inc(mm, 1)
        elif part == 2:
            pe.wait_ge(sined, 2)
            for t in range(NT):
                if t >= 3:
                    pe.wait_ge(h_ready, t - 2)
                nc.tensor.matmul(psw[t % 3][:, :], hid[:, t * P:(t + 1) * P], w3[:, :], start=True, stop=True).then_inc(h_mm, 1)
        else:
            pe.wait_ge(abs_ready, NT)
            for c, (o, ln) in enumerate(SEQS):
                for t in range(o // P, (o + ln) // P):
                    m = nc.tensor.matmul(pss[c][:, :], ones[:, :], win[:, t, :], start=(t == o // P), stop=((t + 1) * P == o + ln))
                m.then_inc(summed, 1)

    def scalar(act, part):
        if part < 2:
            if part == 0:
                act.wait_ge(loaded, LOADS)
                nc.scalar.activation(decay[:, :], decay[:, :], ACT.Abs).then_inc(ab, 1)
            act.wait_ge(a_ready, part + 1)
            nc.scalar.activation(hid[:, :], arg[:, :], ACT.Sin).then_inc(sined, 1)
        elif part == 2:
            act.wait_ge(ab, 1)
            for t in range(NT):
                nc.scalar.activation(win[:, t, :], decay[:, :], ACT.Exp, scale=offs[:, t:t + 1]).then_inc(w_ready, 1)
            for t in range(NT):
                act.wait_ge(h_ready, t + 1)
                nc.scalar.activation(win[:, t, :], filt[:, t, :], ACT.Abs).then_inc(abs_ready, 1)

    def vector(dve, part):
        if part < 2:
            if part == 0:
                nc.vector.memset(ones[:, :], 1.0)
                dve.wait_ge(loaded, LOADS)
            dve.wait_ge(mm, part + 1)
            for g, (t0, n, _) in enumerate(PIECES):
                r = nc.vector.tensor_scalar(arg[:, t0 * P:(t0 + n) * P], psl[g][0:FHID, 0:n * P],
                                            cols[:, 2 * part:2 * part + 1], cols[:, 1:2], ALU.add, ALU.mult)
            steps.link(dve, r)
            steps.link(dve, nc.vector.tensor_scalar(turn[:, :], arg[:, :], 1.0 / TWO_PI, MAGIC, ALU.mult, ALU.add))
            steps.link(dve, nc.vector.tensor_scalar(turn[:, :], turn[:, :], MAGIC, None, ALU.subtract))
            steps.link(dve, nc.vector.scalar_tensor_tensor(arg[:, :], turn[:, :], -HI, arg[:, :], ALU.mult, ALU.add))
            steps.link(dve, nc.vector.scalar_tensor_tensor(arg[:, :], turn[:, :], -LO, arg[:, :], ALU.mult, ALU.add))
            nc.vector.tensor_scalar(arg[:, :], arg[:, :], 3.1415925, -3.1415925, ALU.min, ALU.max).then_inc(a_ready, 1)
        elif part == 2:
            for t in range(NT):
                dve.wait_ge(h_mm, t + 1)
                dve.wait_ge(w_ready, t + 1)
                nc.vector.tensor_tensor(filt[:, t, :], psw[t % 3][:, :], win[:, t, :], ALU.mult).then_inc(h_ready, 1)
        else:
            dve.wait_ge(summed, 2)
            for c in range(2):
                steps.link(dve, nc.vector.tensor_scalar(rsum[:, c, :], pss[c][:, :], EPS, None, ALU.add))
                steps.link(dve, nc.vector.reciprocal(rsum[:, c, :], rsum[:, c, :]))
            for t in range(NT):
                nc.vector.tensor_tensor(filt[:, t, :], filt[:, t, :], rsum[:, 0 if t < CT else 1, :], ALU.mult)

    return tensor, scalar, vector


CONV = [
    (3 * LC // 2, 96, 2), (3 * LL // 2, 128, 6)]


def hyena_conv(nc, A, S, x0, u, uT, filt):
    NF, NG = 2, 2
    NFT = [c[2] for c in CONV]
    with ExitStack() as ctx:
        sb, ps, sem = scope(nc, ctx, "cv")
        fwd = sb("fwd", [P, NF, 8, 2, P])
        inv = sb("inv", [P, 12, 512])
        Y = sb("Y", [P, 6, 2, HW])
        H = sb("H", [P, 2, HW])
        tmp = sb("tmp", [P, 4, HW])
        psf = [ps(f"psf{i}", [P, 512]) for i in range(8)]
        f_in = [sem(f"f_in{i}") for i in range(NF)]
        i_in = [sem(f"i_in{q}") for q in range(3)]
        u_mm, h_mm, h_out, prod, v_steps, y_ready, inv_mm, out_ready = (
            sem("u_mm"), sem("h_mm"), sem("h_out"), sem("prod"), sem("v"), sem("y_ready"), sem("inv_mm"), sem("out_ready"))
        block = ctx.enter_context(nc.Block())
        ftiles = [(c, f) for c in range(2) for f in range(NFT[c])]
        halves = [(0, 0, LC)] + [(1, h * 512, 512) for h in range(2)]

        def inverse_in(sp, h):
            if h:
                sp.wait_ge(inv_mm, 4 * h)
            if h == 0:
                sp.dma_start(inv[0:96, 0:4, 0:LC], A["k_inv_c"]).then_inc(i_in[0], 16)
            else:
                for q in range(3):
                    sp.dma_start(inv[:, 4 * q:4 * q + 4, :], A["k_inv_l"][h - 1, :, 4 * q:4 * q + 4]).then_inc(i_in[q], 16)

        @block.sync
        def _(sp):
            for n, (c, f) in enumerate(ftiles):
                if n >= NF:
                    sp.wait_ge(h_mm, n - NF + 1)
                tt, fw = (2, 96) if c == 0 else (8, 128)
                src = A["k_fwd_c"][f] if c == 0 else A["k_fwd_l"][f]
                sp.dma_start(fwd[:, n % NF, 0:tt, :, 0:fw], src.rearrange("p (t r f) -> p t r f", t=tt, r=2)).then_inc(f_in[n % NF], 16)
                if n in (1, 6):
                    inverse_in(sp, 0 if n == 1 else 1)
            inverse_in(sp, 2)

        @block.tensor
        def _(pe):
            def forward(n):
                c, f = ftiles[n]
                t0, tt, fw = (0, 2, 96) if c == 0 else (2, 8, 128)
                pe.wait_ge(f_in[n % NF], 16 * (n // NF + 1))
                if n == 2:
                    pe.wait_ge(out_ready, 4)
                if n >= 2:
                    pe.wait_ge(prod, n - 1)
                for q, (src, done) in enumerate(((uT, u_mm), (filt, h_mm))):
                    for r in range(2):
                        for t in range(tt):
                            m = nc.tensor.matmul(psf[4 * (n % 2) + 2 * q + r][0:fw, :], fwd[:, n % NF, t, r, 0:fw], src[:, t0 + t, :],
                                                 start=(t == 0), stop=(t == tt - 1))
                    m.then_inc(done, 1)

            def inverse(h):
                c, o, ln = halves[h]
                fw, nf = CONV[c][1], NFT[c]
                pe.wait_ge(y_ready, 2 if c == 0 else 8)
                for ch in range(4):
                    n = 4 * h + ch
                    bank = psf[4 + ch if h < 2 else ch]
                    for j in range(2 * nf):
                        if ch == 0 and j % 4 == 0:
                            pe.wait_ge(i_in[j // 4], 16 * (h + 1 if j == 0 else h))
                        m = nc.tensor.matmul(bank[:, 0:ln], Y[0:fw, j // 2, j % 2, ch * P:(ch + 1) * P], inv[0:fw, j, 0:ln],
                                             start=(j == 0), stop=(j == 2 * nf - 1))
                    m.then_inc(inv_mm, 1)

            forward(0)
            forward(1)
            pe.wait_ge(prod, 2)
            inverse(0)
            for n in range(2, 8):
                forward(n)
            pe.wait_ge(prod, 8)
            inverse(1)
            inverse(2)

        @block.scalar
        def _(act):
            for n, (c, f) in enumerate(ftiles):
                fw = CONV[c][1]
                act.wait_ge(h_mm, n + 1)
                if n >= 1:
                    act.wait_ge(prod, n)
                for r in range(2):
                    h = nc.scalar.activation(H[0:fw, r, :], psf[4 * (n % 2) + 2 + r][0:fw, :], ACT.Copy)
                h.then_inc(h_out, 1)

        @block.vector
        def _(dve):
            steps = Count(v_steps)

            def outputs(h):
                c, o, ln = halves[h]
                o += SEQS[c][0]
                at = ROWS["hy_bias"][0]
                for ch in range(4):
                    n = 4 * h + ch
                    dve.wait_ge(inv_mm, n + 1)
                    bank = psf[4 + ch if h < 2 else ch]
                    steps.link(dve, nc.vector.scalar_tensor_tensor(u[:, ch, o:o + ln], u[:, ch, o:o + ln],
                                                                   S["vec"][:, at + ch:at + ch + 1], bank[:, 0:ln], ALU.mult, ALU.add))
                    nc.vector.tensor_tensor(x0[:, ch, o:o + ln], x0[:, ch, o:o + ln], u[:, ch, o:o + ln], ALU.mult).then_inc(out_ready, 1)

            for n, (c, f) in enumerate(ftiles):
                if n == 2:
                    outputs(0)
                fw = CONV[c][1]
                dve.wait_ge(u_mm, n + 1)
                dve.wait_ge(h_out, n + 1)
                if n >= 1:
                    dve.wait_ge(y_ready, n)
                if n == 2:
                    dve.wait_ge(inv_mm, 4)
                ur, ui = (psf[4 * (n % 2) + r][0:fw, :] for r in range(2))
                yf = f
                for j, (a, r) in enumerate(((ur, 0), (ui, 1), (ur, 1), (ui, 0))):
                    last = nc.vector.tensor_tensor(tmp[0:fw, j, :], a, H[0:fw, r, :], ALU.mult)
                steps.give(last)
                steps.wait(dve)
                nc.vector.tensor_tensor(Y[0:fw, yf, 0, :], tmp[0:fw, 0, :], tmp[0:fw, 1, :], ALU.subtract).then_inc(prod, 1)
                nc.vector.tensor_tensor(Y[0:fw, yf, 1, :], tmp[0:fw, 2, :], tmp[0:fw, 3, :], ALU.add).then_inc(y_ready, 1)
            outputs(1)
            outputs(2)


KT = NT + PAST // P


def key_tile(t):
    return t if t < CT else t + PAST // P


def qkv_in(nc, A, S, hnT, qT, kT, v, out_k, out_v):
    QW, KW = NH * HD, NKV * HD
    NHQ = NH + NKV
    with ExitStack() as ctx:
        sb, ps, sem = scope(nc, ctx, "qkv")
        w = sb("w", [P, KD, QW + 2 * KW])
        z = sb("z", [P, 2, QW + KW])
        sq = sb("sq", [P, 2, QW + KW])
        kd = sb("kd", [P, 2, NKV, 2, HD])
        ck = sb("ck", [P, PAST // P, NKV, HD])
        ckd = sb("ckd", [P, PAST // P, NKV, 2, HD])
        ra, rb = sb("ra", [P, NHQ, 2, 2, 16]), sb("rb", [P, NHQ, 2, 2, 16])
        cos, sin = sb("cos", [P, LL // P, 2, 16]), sb("sin", [P, LL // P, 2, 16])
        gain = sb("gain", [P, 2, HD])
        ss = sb("ss", [P, NT, NHQ])
        psq = [ps(f"psq{i}", [P, 512]) for i in range(2)]
        pskv = [ps(f"pskv{i}", [P, 512]) for i in range(2)]
        ptq = [ps(f"ptq{i}", [P, 512]) for i in range(2)]
        ptk = [ps(f"ptk{i}", [P, 512]) for i in range(2)]
        w_in = [sem(f"w_in{k}") for k in range(KD)]
        k_stored = [sem(f"k_stored{t}") for t in range(CT)]
        loaded, v_steps, mm, z_out, z_sq, inv, root, r_ready, tr, tr_used, c_dup, stored, kv_out, gains = (
            sem("loaded"), sem("v"), sem("mm"), sem("z_out"), sem("z_sq"), sem("inv"), sem("root"), sem("r_ready"),
            sem("tr"), sem("tr_used"), sem("c_dup"), sem("stored"), sem("kv_out"), sem("gains"))
        block = ctx.enter_context(nc.Block())

        @block.sync
        def _(sp):
            for k in range(KD):
                sp.dma_start(w[:, k, :], A["e_w_in"][0, k * P:(k + 1) * P, 3 * HW:]).then_inc(w_in[k], 16)
            sp.dma_start(cos[:, :, :, :].rearrange("p t a f -> p t (a f)"), A["k_cos"]).then_inc(loaded, 16)
            sp.dma_start(sin[:, :, :, :].rearrange("p t a f -> p t (a f)"), A["k_sin"]).then_inc(loaded, 16)
            sp.dma_start(gain[:, 0, :], A["q_norm_g"].broadcast_to([P, HD])).then_inc(loaded, 16)
            sp.dma_start(gain[:, 1, :], A["k_norm_g"].broadcast_to([P, HD])).then_inc(loaded, 16)
            sp.dma_start(ck[:, :, :, :], A["cache_k"][0, 0].rearrange("(t p) g d -> p t g d", p=P)).then_inc(loaded, 16)
            sp.dma_start(v[:, CT:CT + PAST // P, :], A["cache_v"][0, 0].rearrange("(t p) g d -> p t (g d)", p=P)).then_inc(loaded, 16)
            for t in range(CT):
                sp.wait_ge(r_ready, t + 1)
                sp.dma_start(out_k[t * P:(t + 1) * P], z[:, t % 2, QW:]).then_inc(k_stored[t], 16)
                sp.wait_ge(kv_out, t + 1)
                sp.dma_start(out_v[t * P:(t + 1) * P], v[:, t, :]).then_inc(stored, 16)
            sp.wait_ge(stored, 16 * CT)
            for t in range(CT):
                sp.wait_ge(k_stored[t], 16)
            sp.wait_ge(loaded, 6 * 16)

        @block.tensor
        def _(pe):
            def transposes(n, src_q, src_k):
                if n >= 2:
                    pe.wait_ge(tr_used, n - 1)
                if src_q is not None:
                    for pr in range(4):
                        nc.tensor.transpose(ptq[n % 2][:, pr * P:(pr + 1) * P], src_q[:, pr * P:(pr + 1) * P], S["ident"][:, :])
                for g in range(NKV):
                    m = nc.tensor.transpose(ptk[n % 2][:, g * P:(g + 1) * P],
                                            src_k[:, g, :, :].rearrange("p a d -> p (a d)"), S["ident"][:, :])
                m.then_inc(tr, 1)

            for t in range(NT + 1):
                if t < NT:
                    if t >= 2:
                        pe.wait_ge(z_out, t - 1)
                        pe.wait_ge(kv_out, t - 1)
                    for k in range(KD):
                        if t == 0:
                            pe.wait_ge(w_in[k], 16)
                        st = dict(start=(k == 0), stop=(k == KD - 1))
                        x = hnT[:, k, t * P:(t + 1) * P]
                        nc.tensor.matmul(psq[t % 2][:, :], x, w[:, k, 0:QW], **st)
                        m = nc.tensor.matmul(pskv[t % 2][:, 0:2 * KW], x, w[:, k, QW:], **st)
                    m.then_inc(mm, 1)
                if t == 1:
                    pe.wait_ge(c_dup, 1)
                    for i in range(PAST // P):
                        transposes(i, None, ckd[:, i])
                if t >= 1:
                    pe.wait_ge(r_ready, t)
                    transposes(t + 1, z[:, (t - 1) % 2, 0:QW], kd[:, (t - 1) % 2])

        @block.scalar
        def _(act):
            def copies(n, t):
                act.wait_ge(tr, n + 1)
                if t >= 0:
                    nc.scalar.activation(qT[:, :, t * P:(t + 1) * P], ptq[n % 2][:, :].rearrange("p (a c) -> p a c", c=P), ACT.Copy)
                kt = key_tile(t) if t >= 0 else CT + n
                nc.scalar.activation(kT[:, :, kt * P:(kt + 1) * P], ptk[n % 2][:, 0:NKV * P].rearrange("p (a c) -> p a c", c=P),
                                     ACT.Copy).then_inc(tr_used, 1)

            for t in range(NT + 1):
                if t < NT:
                    act.wait_ge(mm, t + 1)
                    if t >= 2:
                        act.wait_ge(tr, t + 1)
                        if t - 2 < CT:
                            act.wait_ge(k_stored[t - 2], 16)
                    nc.scalar.activation(z[:, t % 2, 0:QW], psq[t % 2][:, :], ACT.Copy).then_inc(z_out, 1)
                    nc.scalar.activation(z[:, t % 2, QW:], pskv[t % 2][:, 0:KW], ACT.Copy)
                    nc.scalar.activation(v[:, key_tile(t), :], pskv[t % 2][:, KW:2 * KW], ACT.Copy).then_inc(kv_out, 1)
                    act.wait_ge(kv_out, t + 1)
                    if t >= 2:
                        act.wait_ge(inv, t - 1)
                    nc.scalar.activation(sq[:, t % 2, :], z[:, t % 2, :], ACT.Square).then_inc(z_sq, 1)
                    act.wait_ge(inv, t + 1)
                    nc.scalar.activation(ss[:, t, :], ss[:, t, :], ACT.Sqrt).then_inc(root, 1)
                if t == 1:
                    copies(0, -1)
                    copies(1, -1)
                if t >= 1:
                    copies(t + 1, t - 1)

        @block.vector
        def _(dve):
            steps = Count(v_steps)
            dve.wait_ge(loaded, 6 * 16)
            steps.link(dve, nc.vector.tensor_scalar(gain[:, 0, :], gain[:, 0, :], HD ** -0.5, None, ALU.mult))
            for i in range(PAST // P):
                r = nc.vector.tensor_copy(ckd[:, i, :, :, :], ck[:, i, :, :].rearrange("p g (a d) -> p g a d", a=1).broadcast_to([P, NKV, 2, HD]))
            r.then_inc(c_dup, 1)
            for t in range(NT):
                zt = z[:, t % 2, :]
                heads = zt.rearrange("p (h d) -> p h d", d=HD)
                s = ss[:, t, :]
                dve.wait_ge(z_sq, t + 1)
                steps.link(dve, nc.vector.reduce_sum(s, sq[:, t % 2, :].rearrange("p (h d) -> p h d", d=HD), AX_X))
                steps.link(dve, nc.vector.tensor_scalar(s, s, 1.0 / HD, EPS, ALU.mult, ALU.add))
                nc.vector.reciprocal(s, s).then_inc(inv, 1)
                dve.wait_ge(root, t + 1)
                steps.link(dve, nc.vector.tensor_tensor(
                    heads, heads, s.rearrange("p (h a) -> p h a", a=1).broadcast_to([P, NHQ, HD]), ALU.mult))
                for h0, hn, j in ((0, NH, 0), (NH, NKV, 1)):
                    r = nc.vector.tensor_tensor(heads[:, h0:h0 + hn, :], heads[:, h0:h0 + hn, :],
                                                gain[:, j:j + 1, :].broadcast_to([P, hn, HD]), ALU.mult)
                steps.link(dve, r)
                if t >= CT:
                    def half(x, h):
                        return x[:, :, :, h, :]
                    x5 = zt.rearrange("p (h a b f) -> p h a b f", a=2, b=2, f=16)
                    c4 = cos[:, t - CT:t - CT + 1, :, :].broadcast_to([P, NHQ, 2, 16])
                    s4 = sin[:, t - CT:t - CT + 1, :, :].broadcast_to([P, NHQ, 2, 16])
                    for h in range(2):
                        nc.vector.tensor_tensor(half(ra, h), half(x5, h), c4, ALU.mult)
                        r = nc.vector.tensor_tensor(half(rb, h), half(x5, 1 - h), s4, ALU.mult)
                    steps.link(dve, r)
                    nc.vector.tensor_tensor(half(x5, 0), half(ra, 0), half(rb, 0), ALU.subtract)
                    steps.link(dve, nc.vector.tensor_tensor(half(x5, 1), half(ra, 1), half(rb, 1), ALU.add))
                if t >= 2:
                    dve.wait_ge(tr, t + 1)
                nc.vector.tensor_copy(kd[:, t % 2, :, :, :], zt[:, QW:].rearrange("p (g a d) -> p g a d", g=NKV, a=1).broadcast_to([P, NKV, 2, HD])
                                      ).then_inc(r_ready, 1)


def attention(nc, A, S, qT, kT, v, yT):
    items = [(2 * pr + r, t, 0 if t < CT else CT, CT if t < CT else KT - CT)
             for pr in range(4) for t in range(NT) for r in range(2)]
    N = len(items)
    chunks = [[(k, min(4, nk - k)) for k in range(0, nk, 4)] for _, _, _, nk in items]
    first = [sum(len(c) for c in chunks[:i]) for i in range(N + 1)]
    KMAX = KT - CT
    with ExitStack() as ctx:
        sb, ps, sem = scope(nc, ctx, "att")
        p = sb("p", [P, 2, KMAX * P])
        pT = sb("pT", [P, 2, KMAX, P])
        top, part = sb("top", [P, N, 3]), sb("part", [P, N, 3])
        nmax, total = sb("nmax", [P, N]), sb("total", [P, N])
        s_ps = ps("s_ps", [P, 3 * 512])
        t_ps = [ps(f"t_ps{i}", [P, 512]) for i in range(4)]
        o_ps = ps("o_ps", [P, 512])
        qk, maxed, exped, normed, v_steps, tr, tr_out, pv, o_out = (
            sem("qk"), sem("maxed"), sem("exped"), sem("normed"), sem("v"), sem("tr"), sem("tr_out"), sem("pv"), sem("o_out"))
        block = ctx.enter_context(nc.Block())

        @block.tensor
        def _(pe):
            def scores(i):
                h, t, k0, nk = items[i]
                r = h % 2
                for j, (k, n) in enumerate(chunks[i]):
                    if i >= 1:
                        pe.wait_ge(exped, min(first[i - 1] + j + 1, first[i]))
                    nc.tensor.matmul(s_ps[:, k * P:(k + n) * P], qT[64 * r:64 * r + HD, h // 2, t * P:(t + 1) * P],
                                     kT[64 * r:64 * r + HD, h // 4, (k0 + k) * P:(k0 + k + n) * P], start=True, stop=True).then_inc(qk, 1)

            def products(i):
                h, t, k0, nk = items[i]
                r = h % 2
                if i >= 2:
                    pe.wait_ge(o_out, i - 1)
                for j, (k, n) in enumerate(chunks[i]):
                    pe.wait_ge(tr_out, first[i] + j + 1)
                    for a in range(k, k + n):
                        m = nc.tensor.matmul(o_ps[64 * r:64 * r + HD, 0:P], v[:, k0 + a, (h // 4) * HD:(h // 4 + 1) * HD],
                                             pT[:, i % 2, a, :], start=(a == 0), stop=(a == nk - 1))
                m.then_inc(pv, 1)

            scores(0)
            for i in range(N):
                h, t, k0, nk = items[i]
                r = h % 2
                if i + 1 < N:
                    scores(i + 1)
                pe.wait_ge(normed, i + 1)
                for j, (k, n) in enumerate(chunks[i]):
                    c = first[i] + j
                    if c >= 4:
                        pe.wait_ge(tr_out, c - 3)
                    for a in range(n):
                        m = nc.tensor.transpose(t_ps[c % 4][:, a * P:(a + 1) * P], p[:, i % 2, (k + a) * P:(k + a + 1) * P],
                                                S["ident"][:, :])
                    m.then_inc(tr, 1)
                if i >= 1:
                    products(i - 1)
            products(N - 1)

        @block.scalar
        def _(act):
            def exps(i):
                h, t, k0, nk = items[i]
                act.wait_ge(maxed, i + 1)
                if i >= 2:
                    act.wait_ge(tr, first[i - 1])
                for j, (k, n) in enumerate(chunks[i]):
                    nc.scalar.activation(p[:, i % 2, k * P:(k + n) * P], s_ps[:, k * P:(k + n) * P], ACT.Exp, bias=nmax[:, i:i + 1],
                                         accum_out=part[:, i, j:j + 1]).then_inc(exped, 1)

            exps(0)
            for i in range(N):
                if i + 1 < N:
                    exps(i + 1)
                if i >= 2:
                    act.wait_ge(pv, i - 1)
                for j, (k, n) in enumerate(chunks[i]):
                    c = first[i] + j
                    act.wait_ge(tr, c + 1)
                    nc.scalar.activation(pT[:, i % 2, k:k + n, :].rearrange("p a c -> p (a c)"), t_ps[c % 4][:, 0:n * P],
                                         ACT.Copy).then_inc(tr_out, 1)

        @block.vector
        def _(dve):
            steps = Count(v_steps)

            def softmax(i):
                h, t, k0, nk = items[i]
                nch = len(chunks[i])
                for j, (k, n) in enumerate(chunks[i]):
                    dve.wait_ge(qk, first[i] + j + 1)
                    r = nc.vector.tensor_reduce(top[:, i, j:j + 1], s_ps[:, k * P:(k + n) * P], AX_X, ALU.max)
                steps.link(dve, r)
                nc.vector.tensor_reduce(nmax[:, i:i + 1], top[:, i, 0:nch], AX_X, ALU.max, negate=True).then_inc(maxed, 1)
                dve.wait_ge(exped, first[i + 1])
                steps.link(dve, nc.vector.reduce_sum(total[:, i:i + 1], part[:, i, 0:nch], AX_X))
                steps.link(dve, nc.vector.reciprocal(total[:, i:i + 1], total[:, i:i + 1]))
                nc.vector.tensor_scalar(p[:, i % 2, 0:nk * P], p[:, i % 2, 0:nk * P], total[:, i:i + 1], None, ALU.mult).then_inc(normed, 1)

            def output(i):
                h, t, _, _ = items[i]
                r = h % 2
                dve.wait_ge(pv, i + 1)
                nc.vector.tensor_copy(yT[64 * r:64 * r + HD, h // 2, t * P:(t + 1) * P], o_ps[64 * r:64 * r + HD, 0:P]).then_inc(o_out, 1)

            softmax(0)
            for i in range(N):
                if i + 1 < N:
                    softmax(i + 1)
                if i >= 1:
                    output(i - 1)
            output(N - 1)


def out_proj_norm(nc, A, S, tag, w_dram, lhs, x_in, x_out, layer, hnT, xn_dram, lhs_dram=None):
    NB = 3
    with ExitStack() as ctx:
        sb, ps, sem = scope(nc, ctx, tag)
        w = sb("w", [P, KD, D])
        gate = sb("gate", [P, 2, D])
        x = sb("x", [P, NB, D])
        xn = sb("xn", [P, 2, D])
        junk = sb("junk", [P, D])
        ssq, rstd = sb("ssq", [P, NT]), sb("rstd", [P, NT])
        psm = [ps(f"psm{i}", [P, D]) for i in range(NB)]
        pst = ps("pst", [P, D])
        w_in = [sem(f"w_in{k}") for k in range(KD)]
        l_in = [sem(f"l_in{k}") for k in range(KD)]
        g_in, mm, products, gated, squared, v_steps, inverted, rooted, scaled, tr, hn_out = (sem(n) for n in (
            "g_in mm products gated squared v inverted rooted scaled tr hn_out").split())
        x_ins, stored = [sem(f"x_in{i}") for i in range(NB)], [sem(f"stored{i}") for i in range(NB)]
        xn_stored = [sem(f"xn_stored{i}") for i in range(2)]
        block = ctx.enter_context(nc.Block())
        mc = S["modcol"]

        @block.sync
        def _(sp):
            for k in range(KD):
                sp.dma_start(w[:, k, :], w_dram[k * P:(k + 1) * P, :]).then_inc(w_in[k], 16)
                if lhs_dram is not None:
                    sp.dma_start(lhs(k), lhs_dram[k]).then_inc(l_in[k], 16)
            for c in range(2):
                sp.dma_start(gate[:, c, :], S["mod_dram"][layer, c:c + 1, 2 * D:3 * D].broadcast_to([P, D])).then_inc(g_in, 16)
            for t in range(NT):
                if t >= NB:
                    sp.wait_ge(stored[t % NB], 16 * (t // NB))
                    sp.wait_ge(scaled, t - NB + 1)
                sp.dma_start(x[:, t % NB, :], x_in(t)).then_inc(x_ins[t % NB], 16)

        @block.gpsimd
        def _(pool):
            for t in range(NT):
                pool.wait_ge(scaled, t + 1)
                pool.dma_start(xn_dram[t * P:(t + 1) * P, :], xn[:, t % 2, :]).then_inc(xn_stored[t % 2], 16)
            for i in range(2):
                pool.wait_ge(xn_stored[i], 16 * len(range(i, NT, 2)))

        @block.tensor
        def _(pe):
            def transposes(t):
                pe.wait_ge(scaled, t + 1)
                if t:
                    pe.wait_ge(hn_out, t)
                for k in range(KD):
                    m = nc.tensor.transpose(pst[:, k * P:(k + 1) * P], xn[:, t % 2, k * P:(k + 1) * P], S["ident"][:, :])
                m.then_inc(tr, 1)

            for t in range(NT):
                if t >= NB:
                    pe.wait_ge(gated, t - NB + 1)
                for k in range(KD):
                    if t == 0:
                        pe.wait_ge(w_in[k], 16)
                        if lhs_dram is not None:
                            pe.wait_ge(l_in[k], 16)
                    for h in range(2):
                        m = nc.tensor.matmul(psm[t % NB][:, h * 512:(h + 1) * 512], lhs(k)[:, t * P:(t + 1) * P],
                                             w[:, k, h * 512:(h + 1) * 512], start=(k == 0), stop=(k == KD - 1))
                m.then_inc(mm, 1)
                if t:
                    transposes(t - 1)
            transposes(NT - 1)

        @block.vector
        def _(dve):
            steps = Count(v_steps)
            dve.wait_ge(g_in, 32)
            for t in range(NT):
                dve.wait_ge(mm, t + 1)
                nc.vector.tensor_tensor(psm[t % NB][:, :], psm[t % NB][:, :], gate[:, 0 if t < CT else 1, :], ALU.mult).then_inc(products, 1)
                dve.wait_ge(products, t + 1)
                dve.wait_ge(x_ins[t % NB], 16 * (t // NB + 1))
                nc.vector.tensor_tensor(x[:, t % NB, :], psm[t % NB][:, :], x[:, t % NB, :], ALU.add).then_inc(gated, 1)
                dve.wait_ge(squared, t + 1)
                steps.link(dve, nc.vector.tensor_scalar(rstd[:, t:t + 1], ssq[:, t:t + 1], 1.0 / D, EPS, ALU.mult, ALU.add))
                nc.vector.reciprocal(rstd[:, t:t + 1], rstd[:, t:t + 1]).then_inc(inverted, 1)
                dve.wait_ge(rooted, t + 1)
                if t >= 2:
                    dve.wait_ge(tr, t - 1)
                    dve.wait_ge(xn_stored[t % 2], 16 * (t // 2))
                nc.vector.tensor_scalar(xn[:, t % 2, :], x[:, t % NB, :], rstd[:, t:t + 1], None, ALU.mult).then_inc(scaled, 1)

        @block.scalar
        def _(act):
            def to_hnT(t):
                c = 0 if t < CT else 1
                act.wait_ge(tr, t + 1)
                for k in range(KD):
                    r = nc.scalar.activation(hnT[:, k, t * P:(t + 1) * P], pst[:, k * P:(k + 1) * P], ACT.Identity,
                                             bias=mc[:, layer, 3, c, k:k + 1], scale=mc[:, layer, 4, c, k:k + 1])
                r.then_inc(hn_out, 1)

            for t in range(NT):
                act.wait_ge(gated, t + 1)
                act.dma_start(x_out(t), x[:, t % NB, :]).then_inc(stored[t % NB], 16)
                if t:
                    act.wait_ge(squared, t)
                nc.scalar.activation(junk[:, :], x[:, t % NB, :], ACT.Square, accum_out=ssq[:, t:t + 1]).then_inc(squared, 1)
                act.wait_ge(inverted, t + 1)
                nc.scalar.activation(rstd[:, t:t + 1], rstd[:, t:t + 1], ACT.Sqrt).then_inc(rooted, 1)
                if t:
                    to_hnT(t - 1)
            to_hnT(NT - 1)
            for i in range(NB):
                act.wait_ge(stored[i], 16 * len(range(i, NT, NB)))


SW = 256


def load_expert(sp, A, layer, w, w_in, j, e):
    if j < 8:
        jj, part = divmod(j, 2)
        c0 = part * FH + jj * SW
        src = A["moe_w_gu"][layer][bass.ds(e, 1), :, c0:c0 + SW]
    else:
        src = A["moe_w_down"][layer][bass.ds(e, 1), :, (j - 8) * SW:(j - 7) * SW]
    sp.dma_start(w[:, j, :, :], src.rearrange("a (k p) n -> p (a k) n", p=P)).then_inc(w_in[j], 16)


def route(nc, A, S, tag, hnT, layer, idx, gates, expert_w, expert_w_in, next_modulation=False):
    with ExitStack() as ctx:
        sb, ps, sem = scope(nc, ctx, tag)
        w = sb("w", [P, KD, NE])
        lt = sb("lt", [P, 512])
        aff = sb("aff", [P, NT, NE])
        stat = sb("stat", [P, 2, NT])
        work = sb("work", [NE, T])
        top = sb("top", [NE, 2, max(CAP)])
        topi = sb("topi", [NE, 2, max(CAP)], U32)
        topf = sb("topf", [NE, 2, max(CAP)])
        lg = ps("lg", [P, 512])
        tok = ps("tok", [P, NT * NE])
        pa = [ps(f"pa{i}", [P, 512]) for i in range(3)]
        pt = ps("pt", [P, 4 * NE])
        w_in, mm, lt_out, tr, v_steps, subbed, exped, aff_ready, back, copied, picked, tr2 = (
            sem("w_in"), sem("mm"), sem("lt_out"), sem("tr"), sem("v"), sem("subbed"), sem("exped"), sem("aff_ready"),
            sem("back"), sem("copied"), sem("picked"), sem("tr2"))
        mod = None
        if next_modulation:
            ring = expert_w[:, :, :, :].rearrange("p j k n -> p (j k n)").rearrange("p (s j k n) -> p s j k n", s=MOD_RING, j=4, k=KH)
            mod = LayerModulation(nc, A, S, layer + 1, ring, pa, lg, sb, sem)
        block = ctx.enter_context(nc.Block())

        @block.sync
        def _(sp):
            sp.dma_start(w[:, :, :], A["router_w"][layer].rearrange("(k p) e -> p k e", p=P)).then_inc(w_in, 16)
            if mod:
                mod.load_weights(sp)
            for j in range(8):
                if mod and j % 4 == 0:
                    sp.wait_ge(mod.w_used, 4 * (MOD_RING + j // 4 + 1))
                load_expert(sp, A, layer, expert_w, expert_w_in, j, 0)

        @block.tensor
        def _(pe):
            pe.wait_ge(w_in, 16)
            for k in range(KD):
                for g, (t0, n, _) in enumerate(PIECES):
                    m = nc.tensor.matmul(lg[32 * g:32 * g + NE, 0:n * P], w[:, k, :], hnT[:, k, t0 * P:(t0 + n) * P],
                                         start=(k == 0), stop=(k == KD - 1), tile_position=(0, 32 * g))
            m.then_inc(mm, 1)
            pe.wait_ge(lt_out, 1)
            for g, (t0, n, _) in enumerate(PIECES):
                q = slice(32 * g, 32 * g + NE)
                if g:
                    pe.wait_ge(tr, g)
                for t in range(n):
                    m = nc.tensor.transpose(tok[:, (t0 + t) * NE:(t0 + t + 1) * NE], lt[q, t * P:(t + 1) * P], S["ident"][q, q])
                m.then_inc(tr, 1)
            pe.wait_ge(aff_ready, 1)
            for g, (t0, n, _) in enumerate(PIECES):
                for t in range(n):
                    m = nc.tensor.transpose(pa[g][0:NE, t * P:(t + 1) * P], aff[:, t0 + t, :], S["ident"][:, :])
            m.then_inc(back, 1)
            if mod:
                pe.wait_ge(copied, 1)
                for g in range(MOD_G):
                    mod.multiply(pe, g)
            pe.wait_ge(picked, 1)
            for c in range(2):
                cap = CAP[c]
                nc.tensor.transpose(pt[0:cap, (2 * c) * NE:(2 * c + 1) * NE], top[:, c, 0:cap], S["ident"][0:NE, 0:NE])
                m = nc.tensor.transpose(pt[0:cap, (2 * c + 1) * NE:(2 * c + 2) * NE], topf[:, c, 0:cap], S["ident"][0:NE, 0:NE])
            m.then_inc(tr2, 1)
            if mod:
                mod.transpose(pe)

        @block.scalar
        def _(act):
            act.wait_ge(subbed, 1)
            nc.scalar.activation(aff[:, :, :], aff[:, :, :], ACT.Exp).then_inc(exped, 1)
            if mod:
                mod.load_bias(act)
                mod.store(act)

        @block.vector
        def _(dve):
            steps = Count(v_steps)
            if mod:
                mod.zero(dve)
            dve.wait_ge(mm, 1)
            for g, (t0, n, _) in enumerate(PIECES):
                r = nc.vector.tensor_copy(lt[32 * g:32 * g + NE, 0:n * P], lg[32 * g:32 * g + NE, 0:n * P])
            r.then_inc(lt_out, 1)
            dve.wait_ge(tr, len(PIECES))
            logits = tok[:, :].rearrange("p (t e) -> p t e", e=NE)

            def per_token(j):
                return stat[:, j, :].rearrange("p (t a) -> p t a", a=1).broadcast_to([P, NT, NE])
            steps.link(dve, nc.vector.reduce_max(stat[:, 0, :], logits, AX_X))
            nc.vector.tensor_tensor(aff[:, :, :], logits, per_token(0), ALU.subtract).then_inc(subbed, 1)
            dve.wait_ge(exped, 1)
            steps.link(dve, nc.vector.reduce_sum(stat[:, 1, :], aff[:, :, :], AX_X))
            steps.link(dve, nc.vector.reciprocal(stat[:, 1, :], stat[:, 1, :]))
            nc.vector.tensor_tensor(aff[:, :, :], aff[:, :, :], per_token(1), ALU.mult).then_inc(aff_ready, 1)
            dve.wait_ge(back, 1)
            for g, (t0, n, _) in enumerate(PIECES):
                r = nc.vector.tensor_copy(work[:, t0 * P:(t0 + n) * P], pa[g][0:NE, 0:n * P])
            r.then_inc(copied, 1)
            dve.wait_ge(copied, 1)
            for c, (o, ln) in enumerate(SEQS):
                cols = work[:, o:o + ln]
                for r8 in range(0, CAP[c], 8):
                    t8 = top[:, c, r8:r8 + 8]
                    steps.link(dve, nc.vector.max(t8, cols))
                    nc.vector.max_index(topi[:, c, r8:r8 + 8], t8, cols)
                    steps.link(dve, nc.vector.match_replace(cols, t8, cols, -1.0))
            for c, (o, ln) in enumerate(SEQS):
                steps.link(dve, nc.vector.tensor_copy(topf[:, c, 0:CAP[c]], topi[:, c, 0:CAP[c]]))
                if c == 1:
                    steps.link(dve, nc.vector.tensor_scalar(topf[:, c, 0:CAP[c]], topf[:, c, 0:CAP[c]], float(o), None, ALU.add))
            nc.vector.tensor_copy(stat[:, 0, 0:1], stat[:, 1, 0:1]).then_inc(picked, 1)
            dve.wait_ge(tr2, 1)
            for c in range(2):
                cap = CAP[c]
                nc.vector.tensor_copy(gates[c][0:cap, :], pt[0:cap, (2 * c) * NE:(2 * c + 1) * NE])
                nc.vector.tensor_copy(idx[c][0:cap, :], pt[0:cap, (2 * c + 1) * NE:(2 * c + 2) * NE])
            if mod:
                for g in range(MOD_G):
                    mod.add_bias(dve, g)
                mod.columns(dve)


def experts(nc, A, S, tag, layer, xn_dram, x_dram, idx, gates, w, w_in):
    CP, CL = CAP
    CC = CP + CL
    with ExitStack() as ctx:
        sb, ps, sem = scope(nc, ctx, tag)
        xl, xc = sb("xl", [P, D]), sb("xc", [CP, D])
        xT = sb("xT", [P, KD, CC])
        sg = sb("sg", [P, 2, CC])
        hT = sb("hT", [P, KD, CC])
        ol, oc = sb("ol", [P, D]), sb("oc", [CP, D])
        icg, ics = [sb("icg0", [CP, 1], U32), sb("icg1", [P, 1], U32)], [sb("ics0", [CP, 1], U32), sb("ics1", [P, 1], U32)]
        gate_f = sb("gate_f", [P, 2, D])
        pgu = [ps(f"pgu{i}", [P, CC]) for i in range(4)]
        pxt = ps("pxt", [P, 2 * CC])
        pol = [ps("pol0", [P, 512]), ps("pol1", [P, 512])]
        poc = ps("poc", [P, SW])
        xl_in, xc_in, gu_mm, silued, multiplied, tr, xT_out, ol_mm, oc_mm, ol_out, oc_out, l_added, c_added = (
            sem("xl_in"), sem("xc_in"), sem("gu_mm"), sem("silued"), sem("multiplied"), sem("tr"), sem("xT_out"),
            sem("ol_mm"), sem("oc_mm"), sem("ol_out"), sem("oc_out"), sem("l_added"), sem("c_added"))
        gate_in, p_steps, o_free, issued = sem("gate_in"), sem("p_steps"), sem("o_free"), sem("issued")
        block = ctx.enter_context(nc.Block())

        @block.sync
        def _(sp):
            sp.wait_ge(xl_in, 16)
            sp.wait_ge(xc_in, 16)
            for j in range(8, 12):
                load_expert(sp, A, layer, w, w_in, j, 0)
            for c in range(2):
                sp.dma_start(gate_f[:, c, :], S["mod_dram"][layer, c:c + 1, 5 * D:6 * D].broadcast_to([P, D])).then_inc(gate_in, 16)
            with sp.Fori(1, NE) as e:
                for j in range(12):
                    if j < 8 and j % 2 == 0:
                        sp.wait_ge(gu_mm, e * 16 + (4 * (j // 2) + 4 - 16))
                    if j == 8:
                        sp.wait_ge(oc_mm, e)
                    load_expert(sp, A, layer, w, w_in, j, e)

        @block.gpsimd
        def _(pool):
            def gather(e, first=False):
                if not first:
                    pool.wait_ge(tr, e * 4)
                    pool.wait_ge(xl_in, e * 16)
                    pool.wait_ge(xc_in, e * 16)
                nc.gpsimd.tensor_copy(icg[0][:, :], idx[0][0:CP, bass.ds(e, 1)])
                nc.gpsimd.tensor_copy(icg[1][:, :], idx[1][:, bass.ds(e, 1)]).then_inc(p_steps, 1)
                pool.wait_ge(p_steps, 1 if first else e * 2)
                pool.sem_inc(issued, 1)
                pool.indirect_dma_start(xc[:, :], None, xn_dram, bass.IndirectOffsetOnAxis(icg[0][:, 0:1], 0)).then_inc(xc_in, 16)
                pool.indirect_dma_start(xl[:, :], None, xn_dram, bass.IndirectOffsetOnAxis(icg[1][:, 0:1], 0)).then_inc(xl_in, 16)

            def scatter(e):
                nc.gpsimd.tensor_copy(ics[0][:, :], idx[0][0:CP, bass.ds(e, 1)])
                nc.gpsimd.tensor_copy(ics[1][:, :], idx[1][:, bass.ds(e, 1)]).then_inc(p_steps, 1)
                pool.wait_ge(p_steps, e * 2 + 3 if not isinstance(e, int) or e < NE - 1 else 2 * NE)
                pool.wait_ge(ol_out, e * 2 + 4)
                pool.sem_inc(issued, 1)
                pool.indirect_dma_start(x_dram, bass.IndirectOffsetOnAxis(ics[1][:, 0:1], 0), ol[:, :], None,
                                        compute_op=ALU.add).then_inc(l_added, 16)
                pool.wait_ge(oc_out, e + 2)
                pool.sem_inc(issued, 1)
                pool.indirect_dma_start(x_dram, bass.IndirectOffsetOnAxis(ics[0][:, 0:1], 0), oc[:, :], None,
                                        compute_op=ALU.add).then_inc(c_added, 16)
                pool.wait_ge(l_added, e * 16 + 16)
                pool.wait_ge(c_added, e * 16 + 16)
                pool.sem_inc(o_free, 1)

            pool.sem_inc(o_free, 1)
            gather(0, first=True)
            with pool.Fori(0, NE - 1) as e:
                gather(e + 1)
                scatter(e)
            scatter(NE - 1)

        @block.tensor
        def _(pe):
            def transposes(e, g):
                for j in range(2):
                    k = 2 * g + j
                    nc.tensor.transpose(pxt[:, j * CC:j * CC + CL], xl[:, k * P:(k + 1) * P], S["ident"][:, :])
                    m = nc.tensor.transpose(pxt[:, j * CC + CL:(j + 1) * CC], xc[:, k * P:(k + 1) * P], S["ident"][0:CP, 0:CP])
                m.then_inc(tr, 1)

            def expert(e, last):
                for f in range(FH // P):
                    for part in range(2):
                        j = 2 * (f // 2) + part
                        if f % 2 == 0:
                            pe.wait_ge(w_in[j], e * 16 + 16)
                        if f == 0 and part == 0:
                            pe.wait_ge(xT_out, e * 4 + 4)
                        pe.wait_ge(multiplied if part else silued, e * 8 + (f + 1))
                        for k in range(KD):
                            m = nc.tensor.matmul(pgu[2 * (f % 2) + part][:, :], w[:, j, k, (f % 2) * P:(f % 2 + 1) * P], xT[:, k, :],
                                                 start=(k == 0), stop=(k == KD - 1))
                        m.then_inc(gu_mm, 1)
                if not last:
                    pe.wait_ge(xl_in, e * 16 + 32)
                    pe.wait_ge(xc_in, e * 16 + 32)
                    transposes(e + 1, 0)
                pe.wait_ge(multiplied, e * 8 + 10)
                for q in range(4):
                    pe.wait_ge(w_in[8 + q], e * 16 + 16)
                    if q % 2 == 0:
                        pe.wait_ge(ol_out, e * 2 + (q // 2 + 1))
                    for k in range(KD):
                        m = nc.tensor.matmul(pol[q // 2][:, (q % 2) * SW:(q % 2 + 1) * SW], hT[:, k, 0:CL], w[:, 8 + q, k, :],
                                             start=(k == 0), stop=(k == KD - 1))
                    if q % 2:
                        m.then_inc(ol_mm, 1)
                    if not last and q < 3:
                        pe.wait_ge(xT_out, e * 4 + (5 + q))
                        transposes(e + 1, q + 1)
                pe.wait_ge(oc_out, e + 1)
                for k in range(KD):
                    for q in range(4):
                        m = nc.tensor.matmul(poc[32 * q:32 * q + CP, :], hT[:, k, CL:CC], w[:, 8 + q, k, :],
                                             start=(k == 0), stop=(k == KD - 1), tile_position=(0, 32 * q))
                m.then_inc(oc_mm, 1)

            pe.wait_ge(xl_in, 16)
            pe.wait_ge(xc_in, 16)
            for g in range(4):
                if g:
                    pe.wait_ge(xT_out, g)
                transposes(0, g)
            with pe.Fori(0, NE - 1) as e:
                expert(e, False)
            expert(NE - 1, True)

        mc = S["modcol"]

        @block.scalar
        def _(act):
            def to_xT(e, g):
                act.wait_ge(tr, e * 4 + (g + 1))
                for j in range(2):
                    k = 2 * g + j
                    for c, c0, n in ((1, 0, CL), (0, CL, CP)):
                        r = nc.scalar.activation(xT[:, k, c0:c0 + n], pxt[:, j * CC + c0:j * CC + c0 + n], ACT.Identity,
                                                 bias=mc[:, layer, 3, c, k:k + 1], scale=mc[:, layer, 4, c, k:k + 1])
                r.then_inc(xT_out, 1)

            def expert(e, last):
                for f in range(FH // P):
                    act.wait_ge(multiplied, e * 8 + (f + 1))
                    act.wait_ge(gu_mm, e * 16 + (2 * f + 1))
                    nc.scalar.activation(sg[:, f % 2, :], pgu[2 * (f % 2)][:, :], ACT.Silu).then_inc(silued, 1)
                if not last:
                    for g in range(4):
                        to_xT(e + 1, g)

            act.sem_inc(silued, 2)
            for g in range(4):
                to_xT(0, g)
            with act.Fori(0, NE - 1) as e:
                expert(e, False)
            expert(NE - 1, True)

        @block.vector
        def _(dve):
            dve.sem_inc(multiplied, 2)
            dve.sem_inc(ol_out, 2)
            dve.sem_inc(oc_out, 1)
            dve.wait_ge(gate_in, 32)
            with dve.Fori(0, NE) as e:
                for f in range(FH // P):
                    dve.wait_ge(silued, e * 8 + (f + 3))
                    dve.wait_ge(gu_mm, e * 16 + (2 * f + 2))
                    nc.vector.tensor_tensor(hT[:, f, :], sg[:, f % 2, :], pgu[2 * (f % 2) + 1][:, :], ALU.mult).then_inc(multiplied, 1)
                dve.wait_ge(o_free, e + 1)
                for b in range(2):
                    dve.wait_ge(ol_mm, e * 2 + (b + 1))
                    nc.vector.scalar_tensor_tensor(ol[:, b * 512:(b + 1) * 512], pol[b][:, :], gates[1][:, bass.ds(e, 1)],
                                                   gate_f[:, 1, b * 512:(b + 1) * 512], ALU.mult, ALU.mult).then_inc(ol_out, 1)
                dve.wait_ge(oc_mm, e + 1)
                for q in range(4):
                    r = nc.vector.scalar_tensor_tensor(oc[:, q * SW:(q + 1) * SW], poc[32 * q:32 * q + CP, :],
                                                       gates[0][0:CP, bass.ds(e, 1)], gate_f[32 * q:32 * q + CP, 0, q * SW:(q + 1) * SW],
                                                       ALU.mult, ALU.mult)
                r.then_inc(oc_out, 1)


LEVELS = (64, 32, 16, 8)
FLOOR = -20.0
SIG_FLOOR = -40.0
RT = RH * RD
L64, INTER, L32, L16, L8, DQ, DK = range(7)
ITEM_LEVEL = {L64: 64, L32: 32, L16: 16, L8: 8}
ITEM_BUF = {L64: 2, INTER: 3, L32: 4, L16: 0, L8: 1, DQ: 2, DK: 3}
USES = [(d, i) for d in range(2) for i in (L64, L32, INTER, L16, L8, DK)] + ["o", "yT"]
NU = len(USES)
BANKS = [(0, 4), (4, 4), (8, 2)]
PARTS = ("q", "f0", "f1")
NZU = NT // 2
NP_STEPS = 3 * NZU + NT


def rec_order():
    def unit(h, d, ps, tail):
        nh, nd = (h, 1) if d == 0 else (h + 1, 0)
        here = lambda *toks: [(h, t) for t in toks]
        following = lambda *kinds: [(nh, (k, nd)) for k in kinds if nh < RH]
        proj = lambda i: [((h, ("p", n - NP_STEPS)) if n >= NP_STEPS else (h + 1, ("p", n))) for n in ps[i] if n >= NP_STEPS or h + 1 < RH]
        o = here(*([("z_last",)] if h == RH - 1 and d == 0 else [])) + here(("post", d, L64)) + proj(0) + here(("prod", d, L64), ("pre", d, L32), ("post", d, INTER), ("kt", d)) + proj(1)
        o += here(("pre", d, L16), ("post", d, L32), ("fin", d, L64)) + proj(2)
        o += here(("prod", d, L32), ("pre", d, L8), ("post", d, L16)) + following("sig")
        o += here(("fin", d, L32)) + proj(3) + here(("prod", d, INTER), ("pre", d, DQ), ("post", d, L8), ("pre", d, DK))
        o += here(("fin", d, INTER)) + following("fk") + proj(4) + here(("prod", d, L16), ("post", d, DQ), ("post", d, DK))
        o += following("logf") + here(("fin", d, L16)) + proj(5) + here(("prod", d, L8))
        o += here(("fin", d, L8)) + proj(6) + here(("prod", d, DK))
        if d == 0:
            return o + proj(8) + following("scan") + here(("fin", d, DK)) + following("etot") + proj(7) + [(nh, ("pre", nd, L64)), (nh, ("pre", nd, INTER))]
        last = h == RH - 1
        o += ([] if last else [(nh, ("q",))]) + here(("g",)) + ([] if last else [(nh, ("q_ln",))]) + here(("g_ln",), ("fin", d, DK))
        o += [(h + 1, ("p", n)) for n in tail[0] if not last] + here(("prod_o",))
        o += following("scan", "etot") + ([] if last else [(nh, ("q_sig",))]) + here(("g_sig",), ("fin_o",)) + here(("gate",), ("norm",))
        o += [(h + 1, ("p", n)) for n in tail[1] if not last]
        o += ([] if last else [(nh, ("pre", nd, L64)), (nh, ("pre", nd, INTER))])
        return o + here(("y",), ("prod_y",), ("fin_y",)) + [(h + 1, ("p", n)) for n in tail[2] if not last]

    first = lambda *ns: [(0, ("p", n)) for n in ns]
    o = first(*range(11)) + [(0, ("q",)), (0, ("q_ln",)), (0, ("sig", 0)), (0, ("fk", 0))] + first(11) + [(0, ("logf", 0))]
    o += first(12, 13) + [(0, ("scan", 0)), (0, ("q_sig",)), (0, ("etot", 0))] + first(*range(14, 18))
    o += [(0, ("pre", 0, L64)), (0, ("pre", 0, INTER))]
    for h in range(RH):
        ps0 = [[0], [1], [2], [3], [4, 5], [], [], [9, 10], [6, 7, 8]]
        if h == 0:
            ps0[0:2] = [[NP_STEPS + n for n in range(18, 21)], [NP_STEPS + n for n in range(21, NP_STEPS)] + [0, 1]]
        o += unit(h, 0, ps0, None) + unit(h, 1, [[11], [12], [13], [14], [15, 16], [], []], [[17, 18], [19, 20, 21], [22, 23, 24]])
    return o


def recurrence(nc, A, S, hnT, y_dram, out_state):
    with ExitStack() as ctx:
        sb, ps, sem = scope(nc, ctx, "rec")
        U8 = mybir.dt.uint8
        w = sb("w", [P, KD, 5, RD])
        zc = sb("zc", [P, 2, 3, T])
        zv = sb("zv", [P, 2, NT, RD])
        zg = sb("zg", [P, 2, NT, RD])
        kk = sb("kk", [P, T])
        X, X8 = sb("X", [P, T]), sb("X8", [P, T])
        ring = sb("ring", [P, 5, T])
        Qi = sb("Qi", [P, 2, T])
        St = sb("St", [P, 2, NT, RD])
        kT = sb("kT", [P, NT, RD])
        AT = sb("AT", [P, NT, P])
        dtmp = sb("dtmp", [P, 4, P])
        y = sb("y", [P, NT, RD])
        fin = sb("fin", [P, 2, RD])
        s0 = sb("s0", [P, 2, 2, RD])
        tot, etot, tot8 = sb("tot", [P, NT, 2]), sb("etot", [P, NT, 2]), sb("tot8", [P, NT, 2])
        decay = sb("decay", [P, NT])
        ms = sb("ms", [P, NT])
        restart = sb("restart", [P, T], U8)
        maskb = sb("maskb", [P, 8, P], U8)
        maskf = sb("maskf", [P, 2, P])
        lb = sb("lb", [P, 2, RH])
        oml = sb("oml", [P, 2, RH])
        lbt = sb("lbt", [P, 2, RH])
        pz = [ps(f"pz{i}", [P, 512]) for i in range(3)]
        pk = [ps(f"pk{i}", [P, 512]) for i in range(2)]
        pg = [ps(f"pg{i}", [P, 512]) for i in range(3)]
        w_in, s0_in, consts, fin_out, y_out = (
            [sem(f"w_in{j}") for j in range(5)], [sem("s0_in0"), sem("s0_in1")], sem("consts"), sem("fin_out"), sem("y_out"))
        (z_mm, z_out, v_steps, lb_e, lb_d, q_clamped, q_sig, zc_clamped, f_exp, f_ready, log_f, x_ready,
         tot_e, pre, exped, post, k_tr, kT_out, g_full, g_free, g_clamped, g_sig, o_out, o_sq, ms_ready, rstd, y_ready,
         yT_ready, fin_ready) = (sem(n) for n in (
             "z_mm z_out v lb_e lb_d q_clamped q_sig zc_clamped f_exp f_ready log_f x_ready tot_e pre exped "
             "post k_tr kT_out g_full g_free g_clamped g_sig o_out o_sq ms_ready rstd y_ready yT_ready fin_ready").split())
        a_steps = sem("a")
        block = ctx.enter_context(nc.Block())
        ORDER = rec_order()

        def blocks(x, h):
            return x.rearrange("p (b s h) -> p b s h", s=2, h=h)

        def qhalf(d):
            return 1 - d

        def reference(x, d, h):
            b = blocks(x, h)
            return b[:, :, d, h - 1:h] if d == 0 else b[:, :, d, 0:1]

        def totals(x, d):
            b = blocks(x, 64)
            return b[:, :, :, 63] if d == 0 else b[:, :, :, 0]

        def use(h, key):
            return NU * h + USES.index(key)

        def unit_before(h, d):
            return (h, 0) if d else (h - 1, 1)

        @block.sync
        def _(sp):
            sp.dma_start(ring[:, 0, 0:8 * P], A["k_maskb"].rearrange("p m c -> p (m c)")).then_inc(consts, 16)
            sp.dma_start(maskf[:, :, :], A["k_maskf"]).then_inc(consts, 16)
            for h in range(RH):
                for j, part in enumerate((0, 2, 3, 1, 4)):
                    if h:
                        sp.wait_ge(z_mm, NP_STEPS * (h - 1) + (NZU * (j + 1) if j < 3 else NP_STEPS))
                    sp.dma_start(w[:, :, j, :], A["r_w_in"][0, :, part * D + h * RD:part * D + (h + 1) * RD]
                                 .rearrange("(k p) n -> p k n", p=P)).then_inc(w_in[j], 16)
                if h >= 2:
                    sp.wait_ge(g_free, 3 * use(h - 2, (1, INTER)) + 3)
                sp.dma_start(s0[:, h % 2, :, :], A["state_rec"][0, 0, :, h].rearrange("s d e -> d s e")).then_inc(s0_in[h % 2], 16)

        @block.gpsimd
        def _(pool):
            for h in range(RH):
                for d in range(2):
                    pool.wait_ge(fin_ready, 2 * h + d + 1)
                    pool.dma_start(out_state[d, h], fin[:, d, :]).then_inc(fin_out, 16)
                pool.wait_ge(yT_ready, 3 * (h + 1))
                pool.dma_start(y_dram[h], ring[:, 1, :]).then_inc(y_out, 16)
            pool.wait_ge(fin_out, 32 * RH)
            pool.wait_ge(y_out, 16 * RH)

        @block.tensor
        def _(pe):
            def project(h, n):
                i = NP_STEPS * h + n
                if n in (0, NZU, 2 * NZU):
                    pe.wait_ge(w_in[n // NZU], 16 * (h + 1))
                if n == 3 * NZU:
                    pe.wait_ge(w_in[3], 16 * (h + 1))
                    pe.wait_ge(w_in[4], 16 * (h + 1))
                if i >= 3:
                    pe.wait_ge(z_out, i - 2)
                for k in range(KD):
                    if n < 3 * NZU:
                        c0 = n % NZU * 2 * P
                        m = nc.tensor.matmul(pz[i % 3][:, 0:2 * P], w[:, k, n // NZU, :], hnT[:, k, c0:c0 + 2 * P],
                                             start=(k == 0), stop=(k == KD - 1))
                    else:
                        t = n - 3 * NZU
                        m = nc.tensor.matmul(pz[i % 3][:, 0:2 * RD], hnT[:, k, t * P:(t + 1) * P],
                                             w[:, k, 3:5, :].rearrange("p a c -> p (a c)"), start=(k == 0), stop=(k == KD - 1))
                m.then_inc(z_mm, 1)

            def into_banks(h, key, mm):
                u = use(h, key)
                for b, (t0, nt) in enumerate(BANKS):
                    if u:
                        pe.wait_ge(g_free, 3 * (u - 1) + b + 1)
                    for t in range(t0, t0 + nt):
                        m = mm(pg[b][:, (t - t0) * P:(t - t0 + 1) * P], t)
                    m.then_inc(g_full, 1)

            def step(h, tok):
                kind = tok[0]
                if kind == "p":
                    project(h, tok[1])
                elif kind == "prod" and tok[2] == INTER:
                    d = tok[1]
                    pe.wait_ge(z_out, NP_STEPS * (h + 1))
                    pe.wait_ge(kT_out, 3 * (2 * h + d + 1))
                    into_banks(h, (d, INTER), lambda o, t: nc.tensor.matmul(o, kT[:, t, :], zv[:, h % 2, t, :], start=True, stop=True))
                elif kind == "prod":
                    d, i = tok[1:]
                    pe.wait_ge(post, 7 * (2 * h + d) + i + 1)
                    kb, qb = ring[:, ITEM_BUF[i], :], ring[:, ITEM_BUF[DQ if i == DK else i], :]
                    into_banks(h, (d, i), lambda o, t: nc.tensor.matmul(o, kb[:, t * P:(t + 1) * P], qb[:, t * P:(t + 1) * P],
                                                                       start=True, stop=True))
                elif kind == "kt":
                    d = tok[1]
                    n = 3 * (2 * h + d)
                    pe.wait_ge(post, 7 * (2 * h + d) + INTER + 1)
                    for b, (t0, nt) in enumerate(BANKS):
                        if n + b >= 2:
                            pe.wait_ge(kT_out, n + b - 1)
                        for t in range(t0, t0 + nt):
                            m = nc.tensor.transpose(pk[(n + b) % 2][:, (t - t0) * P:(t - t0 + 1) * P],
                                                    ring[:, ITEM_BUF[INTER], t * P:(t + 1) * P], S["ident"][:, :])
                        m.then_inc(k_tr, 1)
                elif kind == "prod_o":
                    pe.wait_ge(g_free, 3 * use(h, (1, DK)) + 3)

                    def mm(o, t):
                        nc.tensor.matmul(o, AT[:, t, :], zv[:, h % 2, t, :], start=True, stop=False)
                        nc.tensor.matmul(o, Qi[:, 0, t * P:(t + 1) * P], St[:, 0, t, :], start=False, stop=False)
                        return nc.tensor.matmul(o, Qi[:, 1, t * P:(t + 1) * P], St[:, 1, t, :], start=False, stop=True)
                    into_banks(h, "o", mm)
                elif kind == "prod_y":
                    pe.wait_ge(y_ready, h + 1)
                    into_banks(h, "yT", lambda o, t: nc.tensor.transpose(o, y[:, t, :], S["ident"][:, :]))

            for h, tok in ORDER:
                step(h, tok)

        @block.scalar
        def _(act):
            chain = Count(a_steps)

            def z_copy(h, n):
                i = NP_STEPS * h + n
                act.wait_ge(z_mm, i + 1)
                if n == 0 and h >= 2:
                    act.wait_ge(post, 14 * (h - 1))
                    act.wait_ge(g_full, 3 * use(h - 2, "o") + 3)
                    act.wait_ge(y_ready, h - 1)
                if n < 3 * NZU:
                    c0 = n % NZU * 2 * P
                    nc.scalar.activation(zc[:, h % 2, n // NZU, c0:c0 + 2 * P], pz[i % 3][:, 0:2 * P], ACT.Copy).then_inc(z_out, 1)
                else:
                    chain.link(act, nc.scalar.activation(zv[:, h % 2, n - 3 * NZU, :], pz[i % 3][:, 0:RD], ACT.Copy))
                    nc.scalar.activation(zg[:, h % 2, n - 3 * NZU, :], pz[i % 3][:, RD:2 * RD], ACT.Copy).then_inc(z_out, 1)

            def exp_neg(x):
                chain.link(act, nc.scalar.activation(x, x, ACT.Exp, scale=-1.0))

            def step(h, tok):
                kind = tok[0]
                d = tok[1] if len(tok) > 1 and kind != "p" else 0
                n2 = 2 * h + d
                z = zc[:, h % 2, 1 + d, :]
                r4 = ring[:, 4, :]
                if kind == "p":
                    i = NP_STEPS * h + tok[1] - 1
                    if i >= 0:
                        z_copy(i // NP_STEPS, i % NP_STEPS)
                elif kind == "z_last":
                    z_copy(h, NP_STEPS - 1)
                elif kind == "q":
                    act.wait_ge(q_clamped, h + 1)
                    exp_neg(ring[:, 1, :])
                elif kind == "q_ln":
                    chain.give(nc.scalar.activation(ring[:, 1, :], ring[:, 1, :], ACT.Ln, bias=1.0))
                elif kind == "q_sig":
                    chain.wait(act)
                    nc.scalar.activation(ring[:, 1, :], ring[:, 1, :], ACT.Exp, scale=-1.0).then_inc(q_sig, 1)
                elif kind == "g":
                    act.wait_ge(g_clamped, h + 1)
                    exp_neg(ring[:, 2, :])
                elif kind == "g_ln":
                    chain.give(nc.scalar.activation(ring[:, 2, :], ring[:, 2, :], ACT.Ln, bias=1.0))
                elif kind == "g_sig":
                    chain.wait(act)
                    nc.scalar.activation(ring[:, 2, :], ring[:, 2, :], ACT.Exp, scale=-1.0).then_inc(g_sig, 1)
                elif kind == "sig":
                    act.wait_ge(zc_clamped, n2 + 1)
                    if n2:
                        uh, ud = unit_before(h, d)
                        act.wait_ge(g_full, 3 * use(uh, (ud, L32)) + 3)
                    chain.link(act, nc.scalar.activation(r4, z, ACT.Exp, scale=-1.0))
                    chain.link(act, nc.scalar.activation(z, r4, ACT.Ln, bias=1.0))
                    nc.scalar.activation(z, z, ACT.Exp, scale=-1.0).then_inc(f_exp, 1)
                elif kind == "logf":
                    act.wait_ge(f_ready, n2 + 1)
                    nc.scalar.activation(z, z, ACT.Ln).then_inc(log_f, 1)
                elif kind == "etot":
                    act.wait_ge(x_ready, n2 + 1)
                    nc.scalar.activation(etot[:, :, :], tot[:, :, :], ACT.Exp).then_inc(tot_e, 1)
                elif kind == "pre":
                    d, i = tok[1:]
                    act.wait_ge(pre, 7 * n2 + i + 1)
                    r = ring[:, ITEM_BUF[i], :]
                    nc.scalar.activation(r, r, ACT.Exp).then_inc(exped, 1)
                elif kind == "kt":
                    for b, (t0, nt) in enumerate(BANKS):
                        n = 3 * n2 + b
                        act.wait_ge(k_tr, n + 1)
                        if n2 and b == 0:
                            act.wait_ge(g_full, 3 * use((n2 - 1) // 2, ((n2 - 1) % 2, INTER)) + 3)
                        nc.scalar.activation(kT[:, t0:t0 + nt, :].rearrange("p t c -> p (t c)"), pk[n % 2][:, 0:nt * P],
                                             ACT.Copy).then_inc(kT_out, 1)
                elif kind == "norm":
                    act.wait_ge(o_out, h + 1)
                    nc.scalar.activation(ring[:, 3, :], y[:, :, :].rearrange("p t e -> p (t e)"), ACT.Square).then_inc(o_sq, 1)
                    act.wait_ge(ms_ready, h + 1)
                    chain.link(act, nc.scalar.activation(ms[:, :], ms[:, :], ACT.Ln))
                    nc.scalar.activation(ms[:, :], ms[:, :], ACT.Exp, scale=-0.5).then_inc(rstd, 1)

            act.wait_ge(lb_d, 1)
            nc.scalar.activation(lbt[:, :, :], lbt[:, :, :], ACT.Exp).then_inc(lb_e, 1)
            for h, tok in ORDER:
                step(h, tok)

        @block.vector
        def _(dve):
            steps = Count(v_steps)
            TT, TS, STT = nc.vector.tensor_tensor, nc.vector.tensor_scalar, nc.vector.scalar_tensor_tensor

            def wide(x, n):
                return x.broadcast_to([P, x.shape[1], n])

            def take(h, key, b):
                dve.wait_ge(g_full, 3 * use(h, key) + b + 1)

            def states(h, d):
                take(h, (d, INTER), 2)
                dve.wait_ge(s0_in[h % 2], 16 * (h // 2 + 1))
                if h and d == 0:
                    dve.wait_ge(g_full, 3 * use(h - 1, "o") + 3)
                for o, ln in SEQS:
                    tiles = list(range(o // P, (o + ln) // P))
                    if d:
                        tiles.reverse()
                    if o == 0:
                        r = nc.vector.memset(St[:, d, tiles[0], :], 0.0)
                    else:
                        r = nc.vector.tensor_copy(St[:, d, tiles[0], :], s0[:, h % 2, d, :])
                    steps.link(dve, r)
                    for j, t in enumerate(tiles):
                        if j + 1 < len(tiles):
                            dst = St[:, d, tiles[j + 1], :]
                        elif o == 0:
                            dst = fin[:, d, :]
                            if h:
                                dve.wait_ge(fin_out, 32 * h)
                        else:
                            break
                        b = t // 4
                        r = STT(dst, St[:, d, t, :], decay[:, t:t + 1], pg[b][:, (t - 4 * b) * P:(t - 4 * b + 1) * P], ALU.mult, ALU.add)
                        if j + 1 < len(tiles):
                            steps.link(dve, r)
                        else:
                            r.then_inc(fin_ready, 1)
                steps.link(dve, TS(tot8[:, 0, :], tot8[:, 0, :], 1.0, None, ALU.mult))
                nc.vector.tensor_copy(tot8[:, 1, :], tot8[:, 0, :]).then_inc(g_free, 3)

            def step(h, tok):
                kind = tok[0]
                if kind == "p":
                    return
                d = tok[1] if len(tok) > 1 and kind != "p" else 0
                n2 = 2 * h + d
                q = zc[:, h % 2, 0, :]
                k = kk[:, :]
                z = zc[:, h % 2, 1 + d, :]
                r0, r1 = ring[:, 0, :], ring[:, 1, :]
                qh, kh = qhalf(d), d
                r4 = ring[:, 4, :]
                if kind == "q":
                    dve.wait_ge(z_out, NP_STEPS * h + NZU)
                    if h:
                        dve.wait_ge(g_full, 3 * use(h - 1, (1, L8)) + 3)
                    TS(r1, q, SIG_FLOOR, None, ALU.max).then_inc(q_clamped, 1)
                elif kind == "q_sig":
                    dve.wait_ge(q_sig, h + 1)
                    steps.link(dve, TT(q, q, r1, ALU.mult))
                elif kind == "sig":
                    dve.wait_ge(z_out, NP_STEPS * h + NZU * (2 + d))
                    TS(z, z, SIG_FLOOR, None, ALU.max).then_inc(zc_clamped, 1)
                elif kind == "fk":
                    dve.wait_ge(f_exp, n2 + 1)
                    steps.link(dve, TT(r4, r4, z, ALU.mult))
                    TS(z, z, oml[:, d, h:h + 1], lb[:, d, h:h + 1], ALU.mult, ALU.add).then_inc(f_ready, 1)
                elif kind == "scan":
                    if n2:
                        dve.wait_ge(post, 7 * n2)
                    steps.link(dve, TS(k, r4, oml[:, d, h:h + 1], None, ALU.mult))
                    dve.wait_ge(log_f, n2 + 1)
                    steps.link(dve, TS(r4, z, FLOOR, None, ALU.max))
                    steps.give(nc.vector.tensor_tensor_scan(X[:, :], restart[:, :], z, 0.0, ALU.mult, ALU.add))
                    steps.link(dve, nc.vector.tensor_tensor_scan(X8[:, :], restart[:, :], r4, 0.0, ALU.mult, ALU.add))
                    if d == 1:
                        for x, g, tt in ((X[:, :], z, tot), (X8[:, :], r4, tot8)):
                            steps.link(dve, nc.vector.tensor_copy(tt[:, :, :], totals(x, 0)))
                            steps.link(dve, STT(x, x, -1.0, g, ALU.mult, ALU.add))
                            xv = x.rearrange("p (b h) -> p b h", h=64)
                            steps.link(dve, TT(xv, xv, wide(tt[:, :, :].rearrange("p t (s a) -> p (t s) a", a=1), 64), ALU.add))
                    nc.vector.tensor_copy(tot[:, :, :], totals(X[:, :], d)).then_inc(x_ready, 1)
                elif kind == "etot":
                    dve.wait_ge(tot_e, n2 + 1)
                    steps.link(dve, TT(decay[:, :], etot[:, :, 0], etot[:, :, 1], ALU.mult))
                elif kind == "pre":
                    i = tok[2]
                    r = ring[:, ITEM_BUF[i], :]
                    if i == L64 and n2:
                        dve.wait_ge(g_full, 3 * use((n2 - 1) // 2, ((n2 - 1) % 2, DK)) + 3)
                    if i == L32 and n2:
                        dve.wait_ge(g_full, 3 * use((n2 - 1) // 2, ((n2 - 1) % 2, L32)) + 3)
                    if i == L8 and h and d == 0:
                        dve.wait_ge(y_out, 16 * h)
                    if i == DQ:
                        dve.wait_ge(g_full, 3 * use(h, (d, L64)) + 3)
                    if i == DK:
                        dve.wait_ge(k_tr, 3 * (n2 + 1))
                    if i in (DQ, DK):
                        b8 = X8[:, :].rearrange("p (b h) -> p b h", h=8)
                        m = 3 + d
                        ref = wide(b8[:, :, m:m + 1], 8)
                        rb = r.rearrange("p (b h) -> p b h", h=8)
                        last = TT(rb, b8, ref, ALU.subtract) if i == DQ else TT(rb, ref, b8, ALU.subtract)
                    else:
                        hh = 64 if i == INTER else ITEM_LEVEL[i]
                        xb, rb = blocks(X[:, :], hh), blocks(r, hh)
                        ref = wide(reference(X[:, :], d, hh), hh)
                        if i == INTER:
                            own = xb[:, :, qh, 63:64] if d == 0 else xb[:, :, qh, 0:1]
                            nc.vector.tensor_copy(rb[:, :, kh, :], xb[:, :, kh, :])
                            last = TT(rb[:, :, qh, :], wide(own, 64), xb[:, :, qh, :], ALU.subtract)
                        else:
                            if i == L64:
                                nc.vector.tensor_copy(rb[:, :, qh, :], xb[:, :, qh, :])
                            else:
                                TT(rb[:, :, qh, :], xb[:, :, qh, :], ref, ALU.subtract)
                            last = TT(rb[:, :, kh, :], ref, xb[:, :, kh, :], ALU.subtract)
                    last.then_inc(pre, 1)
                elif kind == "post":
                    i = tok[2]
                    r = ring[:, ITEM_BUF[i], :]
                    dve.wait_ge(exped, 7 * n2 + i + 1)
                    if i in (DQ, DK):
                        last = TT(r, r, q if i == DQ else k, ALU.mult)
                    elif i == INTER:
                        if h and d == 0:
                            dve.wait_ge(g_full, 3 * use(h - 1, "o") + 3)
                        rb, qb, kb, w64, qi = (blocks(a, 64) for a in (r, q, k, ring[:, ITEM_BUF[L64], :], Qi[:, d, :]))
                        e = etot[:, :, :]
                        dve.wait_ge(post, 7 * n2 + L64 + 1)
                        steps.give(TT(qi[:, :, kh, :], qb[:, :, kh, :], rb[:, :, kh, :], ALU.mult))
                        steps.give(TT(qi[:, :, qh, :], w64[:, :, qh, :], wide(e[:, :, kh:kh + 1], 64), ALU.mult))
                        steps.wait(dve)
                        TT(rb[:, :, qh, :], kb[:, :, qh, :], rb[:, :, qh, :], ALU.mult)
                        last = TT(rb[:, :, kh, :], w64[:, :, kh, :], wide(e[:, :, qh:qh + 1], 64), ALU.mult)
                    else:
                        hh = ITEM_LEVEL[i]
                        rb, qb, kb = (blocks(a, hh) for a in (r, q, k))
                        TT(rb[:, :, qh, :], rb[:, :, qh, :], qb[:, :, qh, :], ALU.mult)
                        last = TT(rb[:, :, kh, :], rb[:, :, kh, :], kb[:, :, kh, :], ALU.mult)
                    last.then_inc(post, 1)
                elif kind == "fin" and tok[2] == INTER:
                    states(h, d)
                elif kind == "fin":
                    i = tok[2]
                    if d == 0 and i == L64 and h:
                        dve.wait_ge(g_full, 3 * use(h - 1, "o") + 3)
                    for b, (t0, nt) in enumerate(BANKS):
                        take(h, (d, i), b)
                        src = pg[b][:, 0:nt * P].rearrange("p (t c) -> p t c", c=P)
                        at = AT[:, t0:t0 + nt, :]
                        if d == 0 and i == L64:
                            last = TT(at, src, maskf[:, 0:1, :].broadcast_to([P, nt, P]), ALU.mult)
                        elif d == 1 and i == DK:
                            if b:
                                dve.wait_ge(g_free, 3 * use(h, (d, i)) + b)
                            steps.link(dve, TT(dtmp[:, 0:nt, :], src, maskf[:, 1:2, :].broadcast_to([P, nt, P]), ALU.mult))
                            last = TT(at, at, dtmp[:, 0:nt, :], ALU.add)
                        else:
                            j = {(0, L32): 0, (0, L16): 1, (0, L8): 2, (0, DK): 3, (1, L64): 4, (1, L32): 5, (1, L16): 6, (1, L8): 7}[(d, i)]
                            last = nc.vector.copy_predicated(at, maskb[:, j:j + 1, :].broadcast_to([P, nt, P]), src)
                        last.then_inc(g_free, 1)
                    dve.wait_ge(g_free, 3 * use(h, (d, i)) + 3)
                elif kind == "g":
                    dve.wait_ge(z_out, NP_STEPS * (h + 1))
                    dve.wait_ge(g_full, 3 * use(h, (1, DK)) + 3)
                    TS(ring[:, 2, :], zg[:, h % 2, :, :].rearrange("p t e -> p (t e)"), SIG_FLOOR, None, ALU.max).then_inc(g_clamped, 1)
                elif kind == "gate":
                    g = zg[:, h % 2, :, :]
                    dve.wait_ge(g_sig, h + 1)
                    steps.link(dve, TT(g, g, ring[:, 2, :].rearrange("p (t e) -> p t e", e=RD), ALU.mult))
                elif kind == "fin_o":
                    if h:
                        dve.wait_ge(g_full, 3 * use(h - 1, "yT") + 3)
                    for b, (t0, nt) in enumerate(BANKS):
                        take(h, "o", b)
                        nc.vector.tensor_copy(y[:, t0:t0 + nt, :].rearrange("p t e -> p (t e)"), pg[b][:, 0:nt * P]).then_inc(g_free, 1)
                    dve.wait_ge(g_free, 3 * use(h, "o") + 3)
                    steps.give(nc.vector.tensor_copy(dtmp[:, 0, 0:1], tot8[:, 0, 0:1]))
                    nc.vector.tensor_copy(dtmp[:, 0, 1:2], tot8[:, 0, 0:1]).then_inc(o_out, 1)
                elif kind == "norm":
                    dve.wait_ge(o_sq, h + 1)
                    steps.link(dve, nc.vector.reduce_sum(ms[:, :], ring[:, 3, :].rearrange("p (t e) -> p t e", e=RD), AX_X))
                    TS(ms[:, :], ms[:, :], 1.0 / RD, EPS, ALU.mult, ALU.add).then_inc(ms_ready, 1)
                    g = zg[:, h % 2, :, :]
                    steps.link(dve, TT(g, g, y[:, :, :], ALU.mult))
                elif kind == "y":
                    dve.wait_ge(rstd, h + 1)
                    TT(y[:, :, :], zg[:, h % 2, :, :], wide(ms[:, :].rearrange("p (t a) -> p t a", a=1), RD), ALU.mult).then_inc(y_ready, 1)
                elif kind == "fin_y":
                    at = ROWS["r_onorm_g"][0] + h
                    for b, (t0, nt) in enumerate(BANKS):
                        take(h, "yT", b)
                        steps.link(dve, TS(r1[:, t0 * P:(t0 + nt) * P], pg[b][:, 0:nt * P], S["vec"][:, at:at + 1], None, ALU.mult))
                        nc.vector.tensor_copy(dtmp[:, 0, 2:3], tot8[:, 0, 0:1]).then_inc(g_free, 1)
                        dve.wait_ge(g_free, 3 * use(h, "yT") + b + 1)
                        nc.vector.tensor_copy(dtmp[:, 0, 3:4], tot8[:, 0, 0:1]).then_inc(yT_ready, 1)
                        dve.wait_ge(yT_ready, 3 * h + b + 1)

            at = ROWS["r_lb_logits"][0]
            logits = S["vec"][:, at:at + 2 * RH].rearrange("p (s h) -> p s h", s=2)
            steps.link(dve, nc.vector.memset(tot8[:, :, :], 0.0))
            TT(lbt[:, :, :], logits, logits, ALU.subtract).then_inc(lb_d, 1)
            dve.wait_ge(lb_e, 1)
            steps.link(dve, nc.vector.reciprocal(lb[:, :, :], lbt[:, :, :]))
            steps.link(dve, TT(lbt[:, :, :], lbt[:, :, :], lb[:, :, :], ALU.mult))
            steps.link(dve, TT(lb[:, :, :], lbt[:, :, :], lbt[:, :, :], ALU.subtract))
            steps.link(dve, TS(lb[:, :, :], lb[:, :, :], 0.0, None, ALU.max))
            steps.link(dve, TS(oml[:, :, :], lb[:, :, :], -1.0, 1.0, ALU.mult, ALU.add))
            dve.wait_ge(consts, 32)
            steps.give(nc.vector.tensor_copy(maskb[:, :, :].rearrange("p m c -> p (m c)"), ring[:, 0, 0:8 * P]))
            steps.link(dve, nc.vector.memset(restart[:, :], 1.0))
            steps.link(dve, nc.vector.memset(restart[:, :].rearrange("p (b h) -> p b h", h=64)[:, :, 0:1], 0.0))
            for h, tok in ORDER:
                step(h, tok)


def rec_constants():
    s, t = np.arange(P)[:, None], np.arange(P)[None, :]
    lev = lambda h: ((s // (2 * h) == t // (2 * h)) & (s // h < t // h))
    fw = [lev(h) for h in LEVELS]
    d8 = (s // 8 == t // 8) & (s <= t)
    maskb = np.stack([fw[1], fw[2], fw[3], d8] + [m.T for m in fw], 1)
    maskf = np.stack([fw[0], d8.T], 1)
    return {"k_maskb": np.ascontiguousarray(maskb.astype(np.float32)), "k_maskf": np.ascontiguousarray(maskf.astype(np.float32))}


def final_norm(nc, A, S, x_dram, out):
    with ExitStack() as ctx:
        sb, ps, sem = scope(nc, ctx, "fn")
        x = sb("x", [P, NT, D])
        gain = sb("gain", [P, D])
        junk = sb("junk", [P, 2, D])
        ssq = sb("ssq", [P, NT])
        x_in = [sem(f"x{t}") for t in range(NT)]
        g_in, squared, v_steps, inverted, rooted, ready, stored = (sem(n) for n in (
            "g_in squared v inverted rooted ready stored").split())
        block = ctx.enter_context(nc.Block())
        pairs = range(0, NT, 2)

        @block.sync
        def _(sp):
            for t in range(NT):
                sp.dma_start(x[:, t, :], x_dram[t * P:(t + 1) * P, :]).then_inc(x_in[t], 16)
                if t == 1:
                    sp.dma_start(gain[:, :], A["final_norm_g"].rearrange("(a d) -> a d", a=1).broadcast_to([P, D])).then_inc(g_in, 16)
            for t in range(NT):
                sp.wait_ge(ready, t + 1)
                sp.dma_start(out(t), x[:, t, :]).then_inc(stored, 16)
            sp.wait_ge(stored, 16 * NT)

        @block.scalar
        def _(act):
            for t0 in pairs:
                for t in (t0, t0 + 1):
                    act.wait_ge(x_in[t], 16)
                    if t >= 2:
                        act.wait_ge(squared, t - 1)
                    nc.scalar.activation(junk[:, t % 2, :], x[:, t, :], ACT.Square, accum_out=ssq[:, t:t + 1]).then_inc(squared, 1)
                act.wait_ge(inverted, t0 // 2 + 1)
                nc.scalar.activation(ssq[:, t0:t0 + 2], ssq[:, t0:t0 + 2], ACT.Sqrt).then_inc(rooted, 1)

        @block.vector
        def _(dve):
            steps = Count(v_steps)
            for t0 in pairs:
                dve.wait_ge(squared, t0 + 2)
                s = ssq[:, t0:t0 + 2]
                steps.link(dve, nc.vector.tensor_scalar(s, s, 1.0 / D, EPS, ALU.mult, ALU.add))
                nc.vector.reciprocal(s, s).then_inc(inverted, 1)
                dve.wait_ge(rooted, t0 // 2 + 1)
                if t0 == 0:
                    dve.wait_ge(g_in, 16)
                for t in (t0, t0 + 1):
                    nc.vector.scalar_tensor_tensor(x[:, t, :], x[:, t, :], ssq[:, t:t + 1], gain[:, :], ALU.mult, ALU.mult).then_inc(ready, 1)


def build_step(nc, A, O, W):
    def rows(t_dram):
        return lambda t: t_dram[t * P:(t + 1) * P, :]

    def x_tile(prompt, sample):
        return lambda t: (prompt[0, t * P:(t + 1) * P, :] if t < CT else sample[0, (t - CT) * P:(t - CT + 1) * P, :])

    with ExitStack() as ctx:
        sb, _, _ = scope(nc, ctx, "step")
        S = {"ident": sb("ident", [P, P]), "vec": sb("vec", [P, NROWS]), "modcol": sb("modcol", [P, DEPTH, 6, 2, KD]),
             "scond": sb("scond", [P, 2, KD]), "mod_dram": W["mod"]}
        hnT = sb("hnT", [P, KD, T])

        with ExitStack() as layer0:
            sb0, _, _ = scope(nc, layer0, "l0")
            filt = sb0("filt", [P, NT, HW])
            modulation(nc, A, S, filt, hnT)
            yh = sb0("yh", [P, 4, T])
            with ExitStack() as proj:
                sb1, _, _ = scope(nc, proj, "l0p")
                norm_transpose(nc, A, S, "n0", x_tile(A["x_prompt"], A["x_sample"]), 0, 0, 1, hnT)
                with ExitStack() as hy:
                    sb2, _, _ = scope(nc, hy, "l0h")
                    u, uT = sb2("u", [P, 4, T]), sb2("uT", [P, NT, HW])
                    hyena_in(nc, A, S, hnT, yh, u, uT)
                    hyena_conv(nc, A, S, yh, u, uT, filt)
                qT, kT, v = sb1("qT", [P, 4, T]), sb1("kT", [P, NKV, KT * P]), sb1("v", [P, KT, NKV * HD])
                qkv_in(nc, A, S, hnT, qT, kT, v, O["new_k"].rearrange("b a t g d -> (b a t) (g d)"),
                       O["new_v"].rearrange("b a t g d -> (b a t) (g d)"))
                ya = filt[:, :, :].rearrange("p t c -> p (t c)").rearrange("p (k t) -> p k t", k=4)
                attention(nc, A, S, qT, kT, v, ya)
                out_proj_norm(nc, A, S, "op0", A["e_w_out"][0], lambda k: (yh if k < 4 else ya)[:, k % 4, :],
                              x_tile(A["x_prompt"], A["x_sample"]), rows(W["xm0"]), 0, hnT, W["xn"])

        idx = [sb("idx0", [CAP[0], NE], U32), sb("idx1", [CAP[1], NE], U32)]
        gates = [sb("gates0", [CAP[0], NE]), sb("gates1", [CAP[1], NE])]

        def mixer(layer):
            with ExitStack() as mix:
                sb1, _, sem1 = scope(nc, mix, f"mw{layer}")
                w, w_in = sb1("w", [P, 12, KD, SW]), [sem1(f"w_in{j}") for j in range(12)]
                route(nc, A, S, f"rt{layer}", hnT, layer, idx, gates, w, w_in, next_modulation=layer + 1 < DEPTH)
                experts(nc, A, S, f"moe{layer}", layer, W["xn"], W[f"xm{layer}"], idx, gates, w, w_in)

        mixer(0)

        norm_transpose(nc, A, S, "n2", rows(W["xm0"]), 1, 0, 1, hnT)
        recurrence(nc, A, S, hnT, W["yr"], O["new_state"].rearrange("b r s h d e -> (b r s) h d e"))
        with ExitStack() as layer1:
            sb1, _, _ = scope(nc, layer1, "l1o")
            yr = sb1("yr", [P, RH, T])
            out_proj_norm(nc, A, S, "op1", A["r_w_out"][0], lambda k: yr[:, k, :], rows(W["xm0"]), rows(W["xm1"]), 1, hnT, W["xn"],
                          W["yr"])

        mixer(1)
        final_norm(nc, A, S, W["xm1"], x_tile(O["y_prompt"], O["y_sample"]))


def constants():
    f32 = np.float32
    out = {"k_ident": np.eye(P, dtype=f32)}
    feats, offs = [], []
    for _, ln in SEQS:
        t = np.arange(ln, dtype=np.float64)
        tn = t / ln
        ang = 2 * math.pi * tn[:, None] * np.arange(1, 17)[None, :]
        feats.append(np.concatenate([tn[:, None], np.sin(ang), np.cos(ang)], axis=-1))
        offs.append(-np.abs(t - ln // 2) / (ln // 2))
    out["k_feats"] = np.ascontiguousarray(np.concatenate(feats).T.astype(f32))
    out["k_offsets"] = np.ascontiguousarray(np.concatenate(offs).reshape(NT, P).T.astype(f32))
    for tag, (o, ln), (n, fw, nf) in (("c", SEQS[0], CONV[0]), ("l", SEQS[1], CONV[1])):
        w = 2 * math.pi * (np.arange(n // 2) + 0.5) / n
        t = np.arange(ln)
        fw_m = np.stack([np.cos(np.outer(t, w)), -np.sin(np.outer(t, w))], 1)
        fw_m = fw_m.reshape(ln // P, P, 2, nf, fw).transpose(3, 1, 0, 2, 4)
        out["k_fwd_" + tag] = np.ascontiguousarray(fw_m.reshape(nf, P, -1).astype(f32))
        tau = np.arange(ln) + ln // 2
        inv = np.stack([2 / n * np.cos(np.outer(w, tau)), -2 / n * np.sin(np.outer(w, tau))], 1)
        inv = inv.reshape(nf, fw, 2, ln).transpose(1, 0, 2, 3).reshape(fw, 2 * nf, ln)
        if tag == "c":
            out["k_inv_c"] = np.ascontiguousarray(inv.astype(f32))
        else:
            out["k_inv_l"] = np.ascontiguousarray(inv.reshape(fw, 2 * nf, 2, 512).transpose(2, 0, 1, 3).astype(f32))
    pos = np.arange(LL)
    inv_f = 10000.0 ** (-np.arange(0, 32, 2, dtype=np.float64) / 32)
    ang = np.stack([(pos // 64)[:, None] * inv_f, (pos % 64)[:, None] * inv_f], 1)
    for name, f in (("k_cos", np.cos), ("k_sin", np.sin)):
        out[name] = np.ascontiguousarray(f(ang).reshape(LL // P, P, 32).transpose(1, 0, 2).astype(f32))
    return out


_INS = ["x_prompt", "x_sample", "cache_k", "cache_v", "state_rec", "c", "c_ctx", "mod_w", "mod_b", "norm_mix_g", "norm_ffn_g",
        "e_w_in", "e_conv_w", "e_conv_b", "f_w1", "f_b1", "f_freq", "f_w2", "f_b2", "f_w3", "f_decay", "hy_bias", "q_norm_g",
        "k_norm_g", "e_w_out", "r_w_in", "r_lb_logits", "r_onorm_g", "r_w_out", "router_w", "moe_w_gu", "moe_w_down",
        "final_norm_g"]
_OUTS = [("y_prompt", (1, LC, D)), ("y_sample", (1, LL, D)), ("new_k", (1, 1, LC, NKV, HD)), ("new_v", (1, 1, LC, NKV, HD)),
         ("new_state", (1, 1, 2, RH, RD, RD))]
_SCRATCH = [("mod", (DEPTH, 2, 6 * D)), ("xm0", (T, D)), ("xm1", (T, D)), ("xn", (T, D)),
            ("yr", (RH, P, T))]


def kernel(**inputs):
    import concourse.bacc as _bacc
    from concourse.bass_utils import run_bass_kernel_spmd as _run

    nc = _bacc.Bacc("TRN2", target_bir_lowering=False, num_devices=1)
    arrays, A = {}, {}
    data = {name: np.ascontiguousarray(inputs[name]) for name in _INS}
    data.update(constants())
    data.update(rec_constants())
    for name, a in data.items():
        arrays[f"in_{name}"] = a
        A[name] = nc.dram_tensor(f"in_{name}", a.shape, mybir.dt.from_np(a.dtype), kind="ExternalInput").ap()
    O = {name: nc.dram_tensor(f"out_{name}", shape, F32, kind="ExternalOutput").ap() for name, shape in _OUTS}
    W = {name: nc.dram_tensor(f"scratch_{name}", shape, F32, kind="Internal").ap() for name, shape in _SCRATCH}
    build_step(nc, A, O, W)
    r = _run(nc, [arrays], core_ids=[0])
    return tuple(r.results[0][f"out_{name}"] for name, _ in _OUTS)
```
